# Optimizing a Trainium2 kernel written in Bass

```python
import math
import jax, jax.numpy as jnp
from jax import lax
import numpy as np

D_MODEL = 2048
BATCH = 1
SEQ = 256
DEPTH = 1

N_Q_HEADS = 16
N_KV_HEADS = 4
Q_GROUP = N_Q_HEADS // N_KV_HEADS
HEAD_DIM = 128
WINDOW = 128
BLOCK = 128
ATTN_WIDTH = N_Q_HEADS * HEAD_DIM
KV_WIDTH = N_KV_HEADS * HEAD_DIM

SSM_WIDTH = D_MODEL // 2
SSM_GROUP = 16
SSM_GROUPS = SSM_WIDTH // SSM_GROUP
SSM_STATE = 64
DT_MIN = 1e-3
DT_MAX = 1e-1

PEER_HEADS = 8
N_KEYS = 128
N_EXPERTS = N_KEYS * N_KEYS
PEER_QDIM = 256
PEER_HALF = PEER_QDIM // 2
PEER_TOPK = 16
PEER_TOKEN_BLOCK = 128

RMS_EPS = 1e-6
IN_WIDTH = ATTN_WIDTH + 2 * KV_WIDTH + SSM_WIDTH + 2 * D_MODEL
IN_SPLITS = (ATTN_WIDTH, ATTN_WIDTH + KV_WIDTH, ATTN_WIDTH + 2 * KV_WIDTH,
             ATTN_WIDTH + 2 * KV_WIDTH + SSM_WIDTH,
             ATTN_WIDTH + 2 * KV_WIDTH + SSM_WIDTH + D_MODEL)


def rms_norm(x, g):
    xf = x.astype(jnp.float32)
    y = xf * lax.rsqrt(jnp.mean(xf * xf, axis=-1, keepdims=True) + RMS_EPS)
    return (y * g.astype(jnp.float32)).astype(x.dtype)

def alibi_slopes(n_heads):
    return jnp.exp2(-8.0 * (jnp.arange(n_heads, dtype=jnp.float32) + 1.0) / n_heads)

def windowed_gqa(q, k, v, sink):
    b_, s_ = q.shape[0], q.shape[1]
    nb = s_ // BLOCK
    qb = q.reshape(b_, nb, BLOCK, N_KV_HEADS, Q_GROUP, HEAD_DIM).transpose(1, 0, 2, 3, 4, 5)
    pad = ((0, 0), (BLOCK, BLOCK), (0, 0), (0, 0))

    def band(t):
        tp = jnp.pad(t, pad).reshape(b_, nb + 2, BLOCK, N_KV_HEADS, HEAD_DIM)
        tw = jnp.concatenate([tp[:, :-2], tp[:, 1:-1], tp[:, 2:]], axis=2)
        return tw.transpose(1, 0, 2, 3, 4)

    kw, vw = band(k), band(v)
    slopes = alibi_slopes(N_Q_HEADS).reshape(N_KV_HEADS, Q_GROUP)[:, :, None, None]
    sink_f = sink.astype(jnp.float32).reshape(N_KV_HEADS, Q_GROUP)[:, :, None, None]
    scale = HEAD_DIM ** -0.5

    def block_attn(args):
        blk, qi, ki, vi = args
        qpos = blk * BLOCK + jnp.arange(BLOCK)
        kpos = (blk - 1) * BLOCK + jnp.arange(3 * BLOCK)
        dist = jnp.abs(qpos[:, None] - kpos[None, :])
        valid = (dist <= WINDOW) & (kpos >= 0) & (kpos < s_)
        s = jnp.einsum('bqkgd,bskd->bkgqs', qi.astype(jnp.float32), ki.astype(jnp.float32)) * scale
        s = s - slopes * dist.astype(jnp.float32)
        s = jnp.where(valid, s, -jnp.inf)
        m = jnp.maximum(jnp.max(s, axis=-1, keepdims=True), sink_f)
        p = jnp.exp(s - m)
        denom = jnp.sum(p, axis=-1, keepdims=True) + jnp.exp(sink_f - m)
        o = jnp.einsum('bkgqs,bskd->bqkgd', p / denom, vi.astype(jnp.float32))
        return o.astype(q.dtype)

    out = lax.map(block_attn, (jnp.arange(nb), qb, kw, vw))
    return out.transpose(1, 0, 2, 3, 4, 5).reshape(b_, s_, ATTN_WIDTH)

def _ssm_combine(left, right):
    a_l, b_l = left
    a_r, b_r = right
    return a_r * a_l, a_r * b_l + b_r

def s5_direction(u, a_re, a_im, log_step, b_re, b_im, c_re, c_im, reverse):
    s_ = u.shape[1]
    lam = lax.complex(a_re.astype(jnp.float32), a_im.astype(jnp.float32))
    step = jnp.exp(log_step.astype(jnp.float32))[:, None]
    lam_bar = jnp.exp(lam * step)
    b_mat = lax.complex(b_re.astype(jnp.float32), b_im.astype(jnp.float32))
    b_bar = ((lam_bar - 1.0) / lam)[:, :, None] * b_mat
    bu = jnp.einsum('bsgc,gnc->bsgn', u.astype(jnp.complex64), b_bar)
    a = jnp.broadcast_to(lam_bar[None, None], (1, s_, SSM_GROUPS, SSM_STATE))
    _, states = lax.associative_scan(_ssm_combine, (a, bu), reverse=reverse, axis=1)
    c_mat = lax.complex(c_re.astype(jnp.float32), c_im.astype(jnp.float32))
    return jnp.real(jnp.einsum('bsgn,gcn->bsgc', states, c_mat))

def peer(h, w_query, sub_keys_1, sub_keys_2, expert_down, expert_up):
    b_, s_, d_ = h.shape
    t_ = b_ * s_
    ht = h.reshape(t_, d_)
    q = (ht @ w_query).astype(jnp.float32).reshape(t_, PEER_HEADS, 2, PEER_HALF)
    s1 = jnp.einsum('thd,hkd->thk', q[:, :, 0], sub_keys_1.astype(jnp.float32))
    s2 = jnp.einsum('thd,hkd->thk', q[:, :, 1], sub_keys_2.astype(jnp.float32))
    v1, i1 = lax.top_k(s1, PEER_TOPK)
    v2, i2 = lax.top_k(s2, PEER_TOPK)
    cand = (v1[..., :, None] + v2[..., None, :]).reshape(t_, PEER_HEADS, PEER_TOPK * PEER_TOPK)
    cand_idx = (i1[..., :, None] * N_KEYS + i2[..., None, :]).reshape(t_, PEER_HEADS, PEER_TOPK * PEER_TOPK)
    top_s, pos = lax.top_k(cand, PEER_TOPK)
    idx = jnp.take_along_axis(cand_idx, pos, axis=-1)
    gate = jax.nn.softmax(top_s, axis=-1)
    nblk = t_ // PEER_TOKEN_BLOCK
    k_sel = PEER_HEADS * PEER_TOPK
    xs = (ht.reshape(nblk, PEER_TOKEN_BLOCK, d_),
          idx.reshape(nblk, PEER_TOKEN_BLOCK, k_sel),
          gate.reshape(nblk, PEER_TOKEN_BLOCK, k_sel))

    def token_block(args):
        hb, ib, gb = args
        u_sel = jnp.take(expert_down, ib, axis=0)
        act = jnp.einsum('tkd,td->tk', u_sel.astype(jnp.float32), hb.astype(jnp.float32))
        w = gb * jax.nn.gelu(act, approximate=False)
        v_sel = jnp.take(expert_up, ib, axis=0)
        return jnp.einsum('tk,tkd->td', w, v_sel.astype(jnp.float32))

    return lax.map(token_block, xs).reshape(b_, s_, d_)

def first_inputs(seed: int = 0) -> dict:
    key = jax.random.key(seed)
    ks = jax.random.split(key, 24)
    L, D, f32 = DEPTH, D_MODEL, jnp.float32
    G, N, C = SSM_GROUPS, SSM_STATE, SSM_GROUP
    nrm = lambda k, shape, sc: jax.random.normal(k, shape, f32) * sc
    a_im_base = jnp.pi * jnp.arange(N, dtype=f32)
    return {
        "x": nrm(ks[0], (BATCH, SEQ, D), 1.0),
        "mix_norm_g": 1.0 + nrm(ks[1], (L, D), 0.02),
        "w_in": nrm(ks[2], (L, D, IN_WIDTH), D ** -0.5),
        "q_norm_g": 1.0 + nrm(ks[3], (L, HEAD_DIM), 0.02),
        "k_norm_g": 1.0 + nrm(ks[4], (L, HEAD_DIM), 0.02),
        "attn_sink": nrm(ks[5], (L, N_Q_HEADS), 0.5),
        "w_attn_o": nrm(ks[6], (L, ATTN_WIDTH, D), ATTN_WIDTH ** -0.5),
        "ssm_a_re": -0.5 + nrm(ks[7], (L, 2, G, N), 0.01),
        "ssm_a_im": a_im_base + nrm(ks[8], (L, 2, G, N), 0.01),
        "ssm_log_step": jax.random.uniform(ks[9], (L, 2, G), f32, math.log(DT_MIN), math.log(DT_MAX)),
        "ssm_b_re": nrm(ks[10], (L, 2, G, N, C), (2.0 * C) ** -0.5),
        "ssm_b_im": nrm(ks[11], (L, 2, G, N, C), (2.0 * C) ** -0.5),
        "ssm_c_re": nrm(ks[12], (L, 2, G, C, N), (2.0 * N) ** -0.5),
        "ssm_c_im": nrm(ks[13], (L, 2, G, C, N), (2.0 * N) ** -0.5),
        "ssm_d": nrm(ks[14], (L, SSM_WIDTH), 1.0),
        "glu_w_a": nrm(ks[15], (L, SSM_WIDTH, D), SSM_WIDTH ** -0.5),
        "glu_w_b": nrm(ks[16], (L, SSM_WIDTH, D), SSM_WIDTH ** -0.5),
        "w_out": nrm(ks[17], (L, D, D), D ** -0.5),
        "ffn_norm_g": 1.0 + nrm(ks[18], (L, D), 0.02),
        "peer_w_query": nrm(ks[19], (L, D, PEER_HEADS * PEER_QDIM), D ** -0.5),
        "peer_sub_keys_1": nrm(ks[20], (L, PEER_HEADS, N_KEYS, PEER_HALF), PEER_HALF ** -0.5),
        "peer_sub_keys_2": nrm(ks[21], (L, PEER_HEADS, N_KEYS, PEER_HALF), PEER_HALF ** -0.5),
        "peer_down": nrm(ks[22], (L, N_EXPERTS, D), D ** -0.5),
        "peer_up": nrm(ks[23], (L, N_EXPERTS, D), 0.25),
    }

def first_block(x, mix_norm_g, w_in, q_norm_g, k_norm_g, attn_sink, w_attn_o,
              ssm_a_re, ssm_a_im, ssm_log_step, ssm_b_re, ssm_b_im, ssm_c_re, ssm_c_im, ssm_d,
              glu_w_a, glu_w_b, w_out, ffn_norm_g, peer_w_query, peer_sub_keys_1,
              peer_sub_keys_2, peer_down, peer_up):
    b_, s_ = x.shape[0], x.shape[1]
    for l in range(DEPTH):
        h = rms_norm(x, mix_norm_g[l])
        proj = h @ w_in[l]
        q, k, v, u, gate_a, gate_b = jnp.split(proj, IN_SPLITS, axis=-1)
        q = rms_norm(q.reshape(b_, s_, N_Q_HEADS, HEAD_DIM), q_norm_g[l])
        k = rms_norm(k.reshape(b_, s_, N_KV_HEADS, HEAD_DIM), k_norm_g[l])
        v = v.reshape(b_, s_, N_KV_HEADS, HEAD_DIM)
        y_a = windowed_gqa(q, k, v, attn_sink[l]) @ w_attn_o[l]

        ug = u.astype(jnp.float32).reshape(b_, s_, SSM_GROUPS, SSM_GROUP)
        y_fwd = s5_direction(ug, ssm_a_re[l, 0], ssm_a_im[l, 0], ssm_log_step[l, 0],
                             ssm_b_re[l, 0], ssm_b_im[l, 0], ssm_c_re[l, 0], ssm_c_im[l, 0], False)
        y_bwd = s5_direction(ug, ssm_a_re[l, 1], ssm_a_im[l, 1], ssm_log_step[l, 1],
                             ssm_b_re[l, 1], ssm_b_im[l, 1], ssm_c_re[l, 1], ssm_c_im[l, 1], True)
        y_ssm = (y_fwd + y_bwd).reshape(b_, s_, SSM_WIDTH) + ssm_d[l] * ug.reshape(b_, s_, SSM_WIDTH)
        y_act = jax.nn.gelu(y_ssm, approximate=False)
        y_b = (y_act @ glu_w_a[l]) * jax.nn.sigmoid(y_act @ glu_w_b[l])

        merged = jax.nn.sigmoid(gate_a) * y_a + jax.nn.sigmoid(gate_b) * y_b
        x = x + merged @ w_out[l]

        h2 = rms_norm(x, ffn_norm_g[l])
        x = x + peer(h2, peer_w_query[l], peer_sub_keys_1[l], peer_sub_keys_2[l],
                     peer_down[l], peer_up[l])
    return x


MIX_WIDTH = D_MODEL
ATTN_WIDTH_2 = MIX_WIDTH // 2
REC_WIDTH = MIX_WIDTH - ATTN_WIDTH_2
N_ATTN_HEADS = 8
V_HEAD_DIM = ATTN_WIDTH_2 // N_ATTN_HEADS
QK_NOPE_DIM = 128
QK_ROPE_DIM = 64
QK_HEAD_DIM = QK_NOPE_DIM + QK_ROPE_DIM
Q_LORA_RANK = 512
KV_LORA_RANK = 256
ROPE_THETA = 10000.0
Q_BLOCK = 128
N_REC_HEADS = 8
REC_HEAD_DIM = REC_WIDTH // N_REC_HEADS
CONV_WIDTH = 4
LRU_C = 8.0
N_PEER_HEADS = 8
N_EXPERTS_2 = N_KEYS * N_KEYS
PEER_QUERY_DIM = 256
PEER_HALF_2 = PEER_QUERY_DIM // 2
TOKEN_CHUNK = 128
EPS = 1e-6
OFF_CQ = 0
OFF_CKV = OFF_CQ + Q_LORA_RANK
OFF_KR = OFF_CKV + KV_LORA_RANK
OFF_XR = OFF_KR + QK_ROPE_DIM
OFF_YG = OFF_XR + REC_WIDTH
IN_COLS = OFF_YG + REC_WIDTH


def rms_norm_2(t, g):
    tf = t.astype(jnp.float32)
    y = tf * lax.rsqrt(jnp.mean(tf * tf, axis=-1, keepdims=True) + EPS)
    return (y * g.astype(jnp.float32)).astype(t.dtype)

def rope_tables(positions):
    half = QK_ROPE_DIM // 2
    inv_freq = ROPE_THETA ** (-jnp.arange(half, dtype=jnp.float32) / half)
    ang = positions.astype(jnp.float32)[..., None] * inv_freq
    return jnp.cos(ang), jnp.sin(ang)

def apply_rope(t, cos, sin):
    tf = t.astype(jnp.float32)
    t1, t2 = jnp.split(tf, 2, axis=-1)
    out = jnp.concatenate([t1 * cos - t2 * sin, t1 * sin + t2 * cos], axis=-1)
    return out.astype(t.dtype)

def causal_block_attention(q, k, v):
    S = q.shape[2]
    scale = QK_HEAD_DIM ** -0.5
    diag = jnp.tril(jnp.ones((Q_BLOCK, Q_BLOCK), dtype=bool))
    outs = []
    for blk in range(S // Q_BLOCK):
        start = blk * Q_BLOCK
        end = start + Q_BLOCK
        s = jnp.einsum('bhqd,bhkd->bhqk', q[:, :, start:end], k[:, :, :end],
                       preferred_element_type=jnp.float32) * scale
        mask = jnp.concatenate([jnp.ones((Q_BLOCK, start), dtype=bool), diag], axis=1)
        p = jax.nn.softmax(jnp.where(mask, s, -jnp.inf), axis=-1).astype(v.dtype)
        outs.append(jnp.einsum('bhqk,bhkd->bhqd', p, v[:, :, :end]))
    return jnp.concatenate(outs, axis=2)

def mla_group(c_q, c_kv, k_rope, cos, sin, q_norm_g, w_uq, kv_norm_g, w_ukv, q_head_g, k_head_g):
    B, S, _ = c_q.shape
    q = (rms_norm_2(c_q, q_norm_g) @ w_uq).reshape(B, S, N_ATTN_HEADS, QK_HEAD_DIM)
    kv = (rms_norm_2(c_kv, kv_norm_g) @ w_ukv).reshape(B, S, N_ATTN_HEADS, QK_NOPE_DIM + V_HEAD_DIM)
    k_nope, v = kv[..., :QK_NOPE_DIM], kv[..., QK_NOPE_DIM:]
    k_r = jnp.broadcast_to(k_rope[:, :, None, :], (B, S, N_ATTN_HEADS, QK_ROPE_DIM))
    k = jnp.concatenate([k_nope, k_r], axis=-1)
    q = rms_norm_2(q, q_head_g)
    k = rms_norm_2(k, k_head_g)
    c, s = cos[:, :, None, :], sin[:, :, None, :]
    q = jnp.concatenate([q[..., :QK_NOPE_DIM], apply_rope(q[..., QK_NOPE_DIM:], c, s)], axis=-1)
    k = jnp.concatenate([k[..., :QK_NOPE_DIM], apply_rope(k[..., QK_NOPE_DIM:], c, s)], axis=-1)
    o = causal_block_attention(q.transpose(0, 2, 1, 3), k.transpose(0, 2, 1, 3), v.transpose(0, 2, 1, 3))
    return o.transpose(0, 2, 1, 3).reshape(B, S, ATTN_WIDTH_2)

def _lin_combine(e1, e2):
    a1, b1 = e1
    a2, b2 = e2
    return a1 * a2, a2 * b1 + b2

def rglru_group(x_rec, y_gate, conv_w, conv_b, w_rg, b_rg, w_ig, b_ig, lam):
    B, S, W = x_rec.shape
    xp = jnp.pad(x_rec, ((0, 0), (CONV_WIDTH - 1, 0), (0, 0)))
    xc = conv_b + sum(xp[:, j:j + S] * conv_w[j] for j in range(CONV_WIDTH))
    xh = xc.reshape(B, S, N_REC_HEADS, REC_HEAD_DIM)
    r = jax.nn.sigmoid((jnp.einsum('bshi,hij->bshj', xh, w_rg).reshape(B, S, W) + b_rg).astype(jnp.float32))
    i = jax.nn.sigmoid((jnp.einsum('bshi,hij->bshj', xh, w_ig).reshape(B, S, W) + b_ig).astype(jnp.float32))
    log_a = -LRU_C * r * jax.nn.softplus(-lam.astype(jnp.float32))
    a = jnp.exp(log_a)
    mult = jnp.sqrt(-jnp.expm1(2.0 * log_a))
    b = mult * i * xc.astype(jnp.float32)
    _, h = lax.associative_scan(_lin_combine, (a, b), axis=1)
    out = jax.nn.gelu(y_gate.astype(jnp.float32), approximate=False) * h
    return out.astype(x_rec.dtype)

def peer_ffn(xn, w_q, keys1, keys2, u_tab, v_tab):
    B, S, D = xn.shape
    xt = xn.reshape((B * S) // TOKEN_CHUNK, TOKEN_CHUNK, D)

    def chunk(xc):
        q = (xc @ w_q).reshape(TOKEN_CHUNK, N_PEER_HEADS, 2, PEER_HALF_2).astype(jnp.float32)
        s1 = jnp.einsum('chd,hnd->chn', q[:, :, 0], keys1.astype(jnp.float32))
        s2 = jnp.einsum('chd,hnd->chn', q[:, :, 1], keys2.astype(jnp.float32))
        v1, i1 = lax.top_k(s1, PEER_TOPK)
        v2, i2 = lax.top_k(s2, PEER_TOPK)
        cand = (v1[..., :, None] + v2[..., None, :]).reshape(TOKEN_CHUNK, N_PEER_HEADS, PEER_TOPK * PEER_TOPK)
        top, pos = lax.top_k(cand, PEER_TOPK)
        e = (jnp.take_along_axis(i1, pos // PEER_TOPK, axis=-1) * N_KEYS
             + jnp.take_along_axis(i2, pos % PEER_TOPK, axis=-1))
        g = jax.nn.softmax(top, axis=-1)
        ug = jnp.take(u_tab, e, axis=0)
        act = jax.nn.gelu(jnp.einsum('chkd,cd->chk', ug, xc).astype(jnp.float32), approximate=False)
        vg = jnp.take(v_tab, e, axis=0)
        return jnp.einsum('chk,chkd->cd', (g * act).astype(xc.dtype), vg)

    return lax.map(chunk, xt).reshape(B, S, D)

def second_inputs(seed: int = 0) -> dict:
    key = jax.random.key(seed)
    ks = jax.random.split(key, 32)
    L, D = DEPTH, D_MODEL
    f32 = jnp.float32

    def nrm(k, shape, scale):
        return jax.random.normal(k, shape, f32) * scale

    def gain(k, n):
        return 1.0 + 0.05 * jax.random.normal(k, (L, n), f32)

    x = jax.random.normal(ks[0], (BATCH, SEQ, D), f32)
    start = jax.random.randint(ks[1], (BATCH, 1), 0, 4096, dtype=jnp.int32)
    positions = start + jnp.arange(SEQ, dtype=jnp.int32)[None, :]
    ac = jax.random.uniform(ks[2], (L, REC_WIDTH), f32, 0.9, 0.999)
    a0 = ac ** (1.0 / LRU_C)
    lru_lambda = jnp.log(a0) - jnp.log1p(-a0)
    return {
        "x": x,
        "positions": positions,
        "mix_norm_g": gain(ks[3], D),
        "w_in": nrm(ks[4], (L, D, IN_COLS), D ** -0.5),
        "q_norm_g": gain(ks[5], Q_LORA_RANK),
        "w_uq": nrm(ks[6], (L, Q_LORA_RANK, N_ATTN_HEADS * QK_HEAD_DIM), Q_LORA_RANK ** -0.5),
        "kv_norm_g": gain(ks[7], KV_LORA_RANK),
        "w_ukv": nrm(ks[8], (L, KV_LORA_RANK, N_ATTN_HEADS * (QK_NOPE_DIM + V_HEAD_DIM)), KV_LORA_RANK ** -0.5),
        "q_head_norm_g": gain(ks[9], QK_HEAD_DIM),
        "k_head_norm_g": gain(ks[10], QK_HEAD_DIM),
        "conv_w": nrm(ks[11], (L, CONV_WIDTH, REC_WIDTH), CONV_WIDTH ** -0.5),
        "conv_b": nrm(ks[12], (L, REC_WIDTH), 0.01),
        "w_rgate": nrm(ks[13], (L, N_REC_HEADS, REC_HEAD_DIM, REC_HEAD_DIM), REC_HEAD_DIM ** -0.5),
        "b_rgate": nrm(ks[14], (L, REC_WIDTH), 0.1),
        "w_igate": nrm(ks[15], (L, N_REC_HEADS, REC_HEAD_DIM, REC_HEAD_DIM), REC_HEAD_DIM ** -0.5),
        "b_igate": nrm(ks[16], (L, REC_WIDTH), 0.1),
        "lru_lambda": lru_lambda,
        "attn_out_norm_g": gain(ks[17], ATTN_WIDTH_2),
        "rec_out_norm_g": gain(ks[18], REC_WIDTH),
        "w_out": nrm(ks[19], (L, MIX_WIDTH, D), MIX_WIDTH ** -0.5),
        "ffn_norm_g": gain(ks[20], D),
        "peer_w_q": nrm(ks[21], (L, D, N_PEER_HEADS * PEER_QUERY_DIM), D ** -0.5),
        "peer_keys_1": nrm(ks[22], (L, N_PEER_HEADS, N_KEYS, PEER_HALF_2), PEER_HALF_2 ** -0.5),
        "peer_keys_2": nrm(ks[23], (L, N_PEER_HEADS, N_KEYS, PEER_HALF_2), PEER_HALF_2 ** -0.5),
        "peer_u": nrm(ks[24], (L, N_EXPERTS_2, D), D ** -0.5),
        "peer_v": nrm(ks[25], (L, N_EXPERTS_2, D), (N_PEER_HEADS * PEER_TOPK) ** -0.5),
    }

def second_block(x, positions, mix_norm_g, w_in, q_norm_g, w_uq, kv_norm_g, w_ukv, q_head_norm_g,
              k_head_norm_g, conv_w, conv_b, w_rgate, b_rgate, w_igate, b_igate, lru_lambda,
              attn_out_norm_g, rec_out_norm_g, w_out, ffn_norm_g, peer_w_q, peer_keys_1,
              peer_keys_2, peer_u, peer_v):
    cos, sin = rope_tables(positions)
    for l in range(DEPTH):
        h = rms_norm_2(x, mix_norm_g[l])
        proj = h @ w_in[l]
        c_q = proj[..., OFF_CQ:OFF_CKV]
        c_kv = proj[..., OFF_CKV:OFF_KR]
        k_rope = proj[..., OFF_KR:OFF_XR]
        x_rec = proj[..., OFF_XR:OFF_YG]
        y_gate = proj[..., OFF_YG:IN_COLS]
        attn = mla_group(c_q, c_kv, k_rope, cos, sin, q_norm_g[l], w_uq[l], kv_norm_g[l], w_ukv[l],
                         q_head_norm_g[l], k_head_norm_g[l])
        rec = rglru_group(x_rec, y_gate, conv_w[l], conv_b[l], w_rgate[l], b_rgate[l], w_igate[l],
                          b_igate[l], lru_lambda[l])
        mixed = jnp.concatenate([rms_norm_2(attn, attn_out_norm_g[l]), rms_norm_2(rec, rec_out_norm_g[l])], axis=-1)
        x = x + mixed @ w_out[l]
        x = x + peer_ffn(rms_norm_2(x, ffn_norm_g[l]), peer_w_q[l], peer_keys_1[l], peer_keys_2[l],
                         peer_u[l], peer_v[l])
    return x


def setup_inputs(seed=0):
    out = dict(first_inputs(seed))
    for name, value in second_inputs(seed + 1).items():
        if name != "x":
            out[name + "_2"] = value
    return out


def reference(
    x, mix_norm_g, w_in, q_norm_g, k_norm_g, attn_sink, w_attn_o, ssm_a_re, ssm_a_im,
    ssm_log_step, ssm_b_re, ssm_b_im, ssm_c_re, ssm_c_im, ssm_d, glu_w_a, glu_w_b, w_out,
    ffn_norm_g, peer_w_query, peer_sub_keys_1, peer_sub_keys_2, peer_down, peer_up, positions_2,
    mix_norm_g_2, w_in_2, q_norm_g_2, w_uq_2, kv_norm_g_2, w_ukv_2, q_head_norm_g_2,
    k_head_norm_g_2, conv_w_2, conv_b_2, w_rgate_2, b_rgate_2, w_igate_2, b_igate_2,
    lru_lambda_2, attn_out_norm_g_2, rec_out_norm_g_2, w_out_2, ffn_norm_g_2, peer_w_q_2,
    peer_keys_1_2, peer_keys_2_2, peer_u_2, peer_v_2,
):
    x = first_block(
        x, mix_norm_g, w_in, q_norm_g, k_norm_g, attn_sink, w_attn_o, ssm_a_re, ssm_a_im,
        ssm_log_step, ssm_b_re, ssm_b_im, ssm_c_re, ssm_c_im, ssm_d, glu_w_a, glu_w_b, w_out,
        ffn_norm_g, peer_w_query, peer_sub_keys_1, peer_sub_keys_2, peer_down, peer_up,
    )
    return second_block(
        x, positions_2, mix_norm_g_2, w_in_2, q_norm_g_2, w_uq_2, kv_norm_g_2, w_ukv_2,
        q_head_norm_g_2, k_head_norm_g_2, conv_w_2, conv_b_2, w_rgate_2, b_rgate_2, w_igate_2,
        b_igate_2, lru_lambda_2, attn_out_norm_g_2, rec_out_norm_g_2, w_out_2, ffn_norm_g_2,
        peer_w_q_2, peer_keys_1_2, peer_keys_2_2, peer_u_2, peer_v_2,
    )


_drawn_inputs = setup_inputs


def setup_inputs(seed=0):
    import zlib

    import numpy as np

    out = dict(_drawn_inputs(seed))
    spreads = {}
    factors = {'mix_norm_g': 3.569,
     'q_norm_g': 6.414,
     'k_norm_g': 6.442,
     'attn_sink': 3.943,
     'ssm_a_re': 64.0,
     'q_norm_g_2': 2.703,
     'k_head_norm_g_2': 2.68,
     'b_rgate_2': 6.192,
     'b_igate_2': 2.901,
     'ffn_norm_g_2': 7.547,
     'ssm_b_re': 2.902,
     'ssm_b_im': 2.893,
     'ssm_c_re': 2.805,
     'ssm_c_im': 2.923,
     'ffn_norm_g': 4.398,
     'conv_b_2': 3.257,
     'attn_out_norm_g_2': 2.903,
     'rec_out_norm_g_2': 2.909}
    for name, (base, spread) in spreads.items():
        noise = np.random.default_rng([zlib.crc32(name.encode()), seed]).standard_normal(out[name].shape)
        drawn = base * np.exp(spread * noise) if base else spread * noise
        out[name] = __import__('jax').numpy.asarray(drawn.astype(out[name].dtype))
    for name, factor in factors.items():
        out[name] = (out[name] * factor).astype(out[name].dtype)
    return out
```

```python
from contextlib import ExitStack

import numpy as np

import concourse.bass as bass
from concourse import mybir

F32 = mybir.dt.float32
I32 = mybir.dt.int32
U32 = mybir.dt.uint32
ALU = mybir.AluOpType
ACT = mybir.ActivationFunctionType
AX = mybir.AxisListType.X
ds = bass.ds

P = 128
T = 256
NT = T // P
D = 2048
KD = D // P
SLOTS = 8
SLOT = 2048
KS = 4
EPS = 1e-6
ROUND = 12582912.0
TWO_PI_BELOW = float(np.nextafter(np.float32(2 * np.pi), np.float32(0)))
HUGE = 1e30

NQ, NKV, HD, WINDOW = 16, 4, 128, 128
GQ = NQ // NKV
SSM_W = 1024
SSM_K = SSM_W // P
PAIRS = 4
NKEY, TOPK, PH = 128, 16, 8
UNITS = NT * PH
GROUNDS = 2 * TOPK // SLOTS

Q_LORA, KV_LORA, ROPE, NH2 = 512, 256, 64, 8
NOPE = 128
QKD = NOPE + ROPE
W_C = Q_LORA + KV_LORA + ROPE
REC = 1024
CONV = 4
LRU_C = 8.0
ROPE_THETA = 10000.0
PI_A, PI_B = 6.28125, 0.0019340515136718750
PI_C = float(2 * np.pi - PI_A - PI_B)

R_U, R_QKV, R_GATE, R_AO, R_GLU, R_WO, R_PQ = 0, 1, 4, 8, 10, 12, 14
R_IN2, R_MID, R_WO2, R_PQ2 = 16, 19, 20, 22
B_U, B_QKV, B_AO, B_GLU, B_WO, B_PQ = 0, 1, 8, 10, 14, 16
B_IN2, B_UQ, B_WO2, B_PQ2 = 18, 21, 25, 29
BC = 128


class Steps:

    def __init__(self, eng, sem):
        self.eng, self.sem, self.n = eng, sem, 0

    def add(self, ins):
        ins.then_inc(self.sem, 1)
        self.n += 1
        return self.n

    def wait(self, upto=None):
        upto = self.n if upto is None else upto
        if upto:
            self.eng.wait_ge(self.sem, upto)

    def link(self, ins):
        self.add(ins)
        self.wait()

    def clear(self):
        self.wait()
        self.eng.sem_clear(self.sem)
        self.n = 0


def two_blocks(nc, a, out):
    ctx = ExitStack()
    with ctx:
        def sb(name, cols, dt=F32):
            return ctx.enter_context(nc.sbuf_tensor(name, [P, cols], dt))

        def sem(name):
            return ctx.enter_context(nc.semaphore(name))

        wring = sb("wring", SLOTS * SLOT)
        big = sb("big", SLOTS * SLOT)
        xs = sb("xs", NT * D)
        hs = sb("hs", NT * D)
        ht = sb("ht", KD * T)
        sc = sb("sc", 7168)
        cn = sb("cn", 860)

        wslot = wring[:, :].rearrange("p (s c) -> p s c", s=SLOTS)
        gslot = big[:, :].rearrange("p (s c) -> p s c", s=SLOTS)
        x = xs[:, :].rearrange("p (t c) -> p t c", t=NT)
        h = hs[:, :].rearrange("p (t c) -> p t c", t=NT)
        hT = ht[:, :].rearrange("p (k n) -> p k n", k=KD)
        uT = hs[:, 0:2048].rearrange("p (k n) -> p k n", k=SSM_K)
        yT = hs[:, 2048:4096].rearrange("p (k n) -> p k n", k=SSM_K)
        proj = big[:, 0:14336].rearrange("p (t c) -> p t c", t=NT)
        C_K, C_V, C_GA, C_GB = 2048, 2560, 3072, 5120

        ident = cn[:, 0:128]
        iota_t = cn[:, 128:384]
        mask_b = cn[:, 384:416].rearrange("p (q b) -> p q b", q=PAIRS)
        mask_c = cn[:, 416:544]
        quarter = cn[:, 544:546]
        nslope = cn[:, 546:562]
        sink = cn[:, 562:578]
        nsink = cn[:, 578:594]
        ssm_d = cn[:, 594:602]
        stat = cn[:, 602:634]
        iota16 = cn[:, 128:144]
        ones_c = cn[:, 636:637]
        par = cn[:, 640:752]

        psum = [ctx.enter_context(nc.psum_tensor(f"bank{i}", [P, 512], F32)) for i in range(8)]
        dense_bank = psum[0:4]
        tb = psum[4:6]
        mb = psum[6:8]

        x_loaded = sem("x_loaded")
        small_loaded = sem("small_loaded")
        wfull = [sem(f"wfull{b}") for b in range(SLOTS)]
        wused = [sem(f"wused{b}") for b in range(SLOTS)]
        pair_evac = [sem(f"pair_evac{g}") for g in range(2)]
        consts_ready = sem("consts_ready")
        gain_loaded = sem("gain_loaded")
        msq_ready = sem("msq_ready")
        rms_ready = sem("rms_ready")
        h_ready = sem("h_ready")
        tb_filled = sem("tb_filled")
        tb_evac = sem("tb_evac")
        dve = sem("dve_steps")
        acs = sem("act_steps")
        pls = sem("pool_steps")
        ssm_loaded = sem("ssm_loaded")
        sp_in = sem("ssm_param_dve")
        sp_act = sem("ssm_param_act")
        sp_t = sem("ssm_param_transposed")
        sp_done = sem("ssm_param_done")
        bc_loaded = sem("bc_loaded")
        ct_done = sem("ct_transposed")
        ct_evac = sem("ct_evacuated")
        bpad_ready = sem("bpad_ready")
        bt_done = sem("bt_transposed")
        bt_evac = sem("bt_evacuated")
        bu_done = sem("bu_done")
        bu_used = sem("bu_used")
        f_ready = sem("phase_ready")
        e_ready = sem("rotation_ready")
        de_ready = sem("states_ready")
        y_done = sem("y_done")
        y_evac = sem("y_evacuated")
        y_act = sem("y_activated")
        dist_ready = sem("dist_ready")
        qk_copied = sem("qk_copied")
        qk_msq = sem("qk_msq")
        qk_rms = sem("qk_rms")
        qk_ready = sem("qk_ready")
        qk_t = sem("qk_transposed")
        qk_tevac = sem("qk_t_evacuated")
        s_done = sem("scores_done")
        nmax_ready = sem("nmax_ready")
        p_exp = sem("p_exp")
        p_ready = sem("p_ready")
        pt_done = sem("p_transposed")
        pt_evac = sem("pt_evacuated")
        o_done = sem("o_done")
        o_evac = sem("o_evacuated")
        gate_sig = sem("gates_sigmoid")
        merged_ready = sem("merged_ready")
        glu_used = sem("glu_used")
        x_ready = sem("x_ready")
        keys_loaded = sem("keys_loaded")
        keys_t = sem("keys_transposed")
        keys_evac = sem("keys_evacuated")
        sk_done = sem("key_scores_done")
        sk_evac = sem("key_scores_evacuated")
        topk_v = sem("topk_values")
        topk_e = sem("topk_exp")
        stage_ready = sem("indices_ready")
        gfull = [sem(f"gfull{b}") for b in range(SLOTS)]
        gused = [sem(f"gused{b}") for b in range(SLOTS)]
        gathers_issued = sem("gathers_issued")
        gelu_ready = sem("gelu_ready")
        out_done = sem("out_done")
        par_loaded = sem("par_loaded")
        par_t = sem("par_transposed")
        par_ready = sem("par_ready")
        rope_loaded = sem("rope_loaded")
        inv_ready = sem("inv_freq_ready")
        ang_ready = sem("angles_ready")
        trig_ready = sem("trig_ready")
        c_msq = sem("latent_msq")
        c_rms = sem("latent_rms")
        c_ready = sem("latents_normed")
        gates_loaded = sem("gates_loaded")
        xc_ready = sem("conv_ready")
        gate_mm = sem("gate_products")
        gate_act = sem("gates_activated")
        lru_act = sem("lru_activated")
        lru_dve = sem("lru_elementwise")
        lam_act = sem("lambda_exp")
        lam_dve = sem("lambda_decay")
        qk2_msq = sem("qk2_msq")
        qk2_rms = sem("qk2_rms")
        qk2_ready = sem("qk2_ready")
        causal_ready = sem("causal_ready")
        hd_copied = sem("head_copied")
        hd_t = sem("head_transposed")
        hd_tevac = sem("head_t_evacuated")
        s2_done = sem("scores2_done")
        nm2_ready = sem("nmax2_ready")
        p2_exp = sem("p2_exp")
        p2_ready = sem("p2_ready")
        pt2_done = sem("p2_transposed")
        pt2_evac = sem("p2t_evacuated")
        o2_done = sem("o2_done")
        o2_evac = sem("o2_evacuated")
        osq_ready = sem("osq_ready")
        oss_done = sem("o_sums_done")
        oss_rms = sem("o_sums_rms")
        mixed_ready = sem("mixed_ready")
        turn_over = sem("turn_over")

        gain = sc[:, 0:D]

        def cut(base, sizes):
            at, res = base, []
            for n in sizes:
                res.append((at, at + n))
                at += n
            return res

        (rA, rB, rZI, rZ, rD, rE, rF, rR, rBP, rBT, rCT, rCP, rPR) = cut(
            0, [512] * 8 + [512, 512, 512, 768, 256])
        two = lambda r: sc[:, r[0]:r[1]].rearrange("p (c n) -> p c n", c=2)
        bre_e, bim_e, z_in, z_out, zr_e, zi_e, phase, whole = map(two, (rA, rB, rZI, rZ, rD, rE, rF, rR))
        b_pad = sc[:, rBP[0]:rBP[1]].rearrange("p (i a b c) -> p i a b c", i=2, a=2, b=8)
        b_t = sc[:, rBT[0]:rBT[1]].rearrange("p (i a n) -> p i a n", i=2, a=2)
        c_t = sc[:, rCT[0]:rCT[1]].rearrange("p (d a n) -> p d a n", d=2, a=2)
        c_p = sc[:, rCP[0]:rCP[1]].rearrange("p (j d q c) -> p j d q c", j=3, d=2, q=PAIRS)
        prm = sc[:, rPR[0]:rPR[1]].rearrange("p (j n) -> p j n", j=4)
        b_st = big[:, 14336:14592].rearrange("p (a d q c) -> p a d q c", a=2, d=2, q=PAIRS)
        c_st = big[:, 14592:15104].rearrange("p (d a u n) -> p d a u n", d=2, a=2, u=2)
        rot = big[:, 15104:16128].rearrange("p (i c n) -> p i c n", i=2, c=2)
        pw = [sc[0:64, i * 128:(i + 1) * 128] for i in range(14)]
        step2 = sc[0:64, 1800:1802]

        (rQK, rSQ, rGQ, rQT, rVN, rDI, rS, rPT, rSM) = cut(0, [1280, 1280, 640, 1280, 256, 512, 512, 512, 64])
        qk = sc[:, rQK[0]:rQK[1]].rearrange("p (t j c) -> p t j c", t=NT, j=GQ + 1)
        qk_sq = sc[:, rSQ[0]:rSQ[1]]
        g_qk = sc[:, rGQ[0]:rGQ[1]].rearrange("p (j c) -> p j c", j=GQ + 1)
        qkT = sc[:, rQT[0]:rQT[1]].rearrange("p (j n) -> p j n", j=GQ + 1)
        v_sb = sc[:, rVN[0]:rVN[1]].rearrange("p (t c) -> p t c", t=NT)
        dist = sc[:, rDI[0]:rDI[1]].rearrange("p (t n) -> p t n", t=NT)
        prob = sc[:, rS[0]:rS[1]].rearrange("p (i n) -> p i n", i=2)
        probT = sc[:, rPT[0]:rPT[1]].rearrange("p (i k n) -> p i k n", i=2, k=NT)
        sm = sc[:, rSM[0]:rSM[1]]
        glu_sg = sc[:, 0:1024].rearrange("p (t c) -> p t c", t=NT)
        glu_t = sc[:, 1024:2048].rearrange("p (t c) -> p t c", t=NT)
        q_bank, pt_bank, o_bank = dense_bank[2:4], (tb[0], dense_bank[0]), (tb[1], dense_bank[1])
        UA = NT * GQ

        pqT = big[:, 0:4096].rearrange("p (k n) -> p k n", k=KD)
        key_n = big[:, 4096:6144].rearrange("p (h s c) -> p h s c", h=PH, s=2)
        keyT = big[:, 6144:8192].rearrange("p (j c) -> p j c", j=KD)
        kscore = ht[:, :]
        (rW1, rW2, rCA, rCB, rO1, rO2, rV, rIF, rTP, rPF, rIS, rAC, rGE, rWT, rGT, rSS) = cut(
            0, [256, 256, 256, 256, 256, 256, 32, 32, 32, 32, 32, 32, 32, 32, 32, 8])
        sub = lambda r: sc[:, r[0]:r[1]]
        usub = lambda r: sc[:, r[0]:r[1]].bitcast(U32)
        rIU, rPU, rP2, rST = cut(3000, [32, 16, 32, 32])

        c2 = big[:, 0:2 * W_C].rearrange("p (t c) -> p t c", t=NT)
        xrT = big[:, 1664:3712].rearrange("p (k n) -> p k n", k=8)
        ygT = big[:, 3712:5760].rearrange("p (k n) -> p k n", k=8)
        q2 = big[:, 5760:8832].rearrange("p (t h c) -> p t h c", t=NT, h=NH2)
        kv2 = big[:, 8832:12928].rearrange("p (t h c) -> p t h c", t=NT, h=NH2)
        cT = big[:, 12928:14464].rearrange("p (k n) -> p k n", k=6)
        g_cq, g_ckv = big[:, 14464:14976], big[:, 14976:15232]
        g_qh, g_kh = big[:, 15232:15424], big[:, 15424:15616]
        pos_f, inv_freq = big[:, 15616:15618], big[:, 15618:15650]
        ang = big[:, 15650:15778].rearrange("p (j t c) -> p j t c", j=2, t=NT)
        rnd = big[:, 15778:15906].rearrange("p (j t c) -> p j t c", j=2, t=NT)
        trig = big[:, 15906:16034].rearrange("p (j t c) -> p j t c", j=2, t=NT)
        krr = big[:, 16034:16162].rearrange("p (t c) -> p t c", t=NT)
        krg = big[:, 16162:16290].rearrange("p (t c) -> p t c", t=NT)
        pos_i = big[:, 16290:16292].bitcast(I32)
        w_gates = hs[:, 0:2048].rearrange("p (g h j) -> p g h j", g=2, h=NH2)
        xcT = hs[:, 2048:4096].rearrange("p (k n) -> p k n", k=8)
        th_g, rr_g, ii_g = (sc[:, 2048 * i:2048 * (i + 1)] for i in range(3))
        k3 = lambda t: t.rearrange("p (k n) -> p k n", k=8)
        sq_g = ht[:, 0:2048]
        par_rows = sc[0:80, 6144:6272]
        conv_w, conv_b, b_rg, b_ig, lam, g_mix = (par[:, lo:hi] for lo, hi in (
            (0, 32), (32, 40), (40, 48), (48, 56), (56, 64), (64, 80)))
        neg_c, lp = par[:, 80:88], par[:, 88:112]
        kn2 = sc[:, 0:2048].rearrange("p (t h c) -> p t h c", t=NT, h=NH2)
        krh = sc[:, 2048:3072].rearrange("p (t h c) -> p t h c", t=NT, h=NH2)
        qr2 = sc[:, 3072:4096].rearrange("p (t h c) -> p t h c", t=NT, h=NH2)
        qk2_sq = big[:, 1664:1664 + 3072]
        rope_t = big[:, 1664:1664 + 1024].rearrange("p (i t h c) -> p i t h c", i=2, t=NT, h=NH2)
        head_n = sc[:, 4096:4608].rearrange("p (j t c) -> p j t c", j=2, t=NT)
        head_r = sc[:, 4608:4864].rearrange("p (j t c) -> p j t c", j=2, t=NT)
        head_v = sc[:, 4864:5120].rearrange("p (t c) -> p t c", t=NT)
        headT_n = sc[:, 5120:5632].rearrange("p (j n) -> p j n", j=2)
        headT_r = sc[0:64, 5632:6144].rearrange("p (j n) -> p j n", j=2)
        prob2 = sc[:, 6144:6656].rearrange("p (i n) -> p i n", i=2)
        prob2T = sc[:, 6656:7168].rearrange("p (i n) -> p i n", i=2)
        causal = big[:, 0:256]
        sm2 = big[:, 256:384]
        msq2, rms2, rs2 = sm2[:, 0:34], sm2[:, 34:66], sm2[:, 66:98]
        att = sm2[:, 98:114]
        osq = big[:, 5760:5760 + 4096].rearrange("p (k n) -> p k n", k=KD)

        w_in2 = a["w_in_2"][0].rearrange("(k p) n -> p k n", p=P)
        w_uq = a["w_uq_2"][0].rearrange("(k p) n -> p k n", p=P)
        w_ukv = a["w_ukv_2"][0].rearrange("(k p) n -> p k n", p=P)
        w_out2 = a["w_out_2"][0].rearrange("(k p) n -> p k n", p=P)
        w_pq2 = a["peer_w_q_2"][0].rearrange("(k p) n -> p k n", p=P)
        w_in = a["w_in"][0].rearrange("(k p) n -> p k n", p=P)
        w_ao = a["w_attn_o"][0].rearrange("(k p) n -> p k n", p=P)
        w_ga = a["glu_w_a"][0].rearrange("(k p) n -> p k n", p=P)
        w_gb = a["glu_w_b"][0].rearrange("(k p) n -> p k n", p=P)
        w_out = a["w_out"][0].rearrange("(k p) n -> p k n", p=P)
        w_pq = a["peer_w_query"][0].rearrange("(k p) n -> p k n", p=P)

        block = ctx.enter_context(nc.Block())

        @block.sync
        def _(sp):
            def fill(b, src, r):
                if not (isinstance(r, int) and r == 0):
                    sp.wait_ge(wused[b], r)
                n = src.shape[1] * src.shape[2]
                dst = wslot[:, b, 0:n].rearrange("p (k n) -> p k n", k=src.shape[1])
                sp.dma_start(dst, src).then_inc(wfull[b], 16)

            def fill_round(w, r, col):
                for b in range(SLOTS):
                    k = (b % 4) * KS
                    fill(b, w[:, k:k + KS, ds(col + (b // 4) * 512, 512)], r)

            for t in range(NT):
                sp.dma_start(x[:, t, :], a["x"][0, t * P:(t + 1) * P, :]).then_inc(x_loaded, 16)
            fill_round(w_in, R_U, 3072)
            with sp.Fori(0, 3) as i:
                fill_round(w_in, i + R_QKV, i * 1024)
            with sp.Fori(0, 4) as i:
                fill_round(w_in, i + R_GATE, i * 1024 + 4096)
            with sp.Fori(0, 2) as i:
                fill_round(w_ao, i + R_AO, i * 1024)
            with sp.Fori(0, 2) as i:
                for b in range(SLOTS):
                    w = w_ga if b % 4 < 2 else w_gb
                    k = (b % 2) * KS
                    fill(b, w[:, k:k + KS, ds(i * 1024 + (b // 4) * 512, 512)], i + R_GLU)
            with sp.Fori(0, 2) as i:
                fill_round(w_out, i + R_WO, i * 1024)
            with sp.Fori(0, 2) as i:
                fill_round(w_pq, i + R_PQ, i * 1024)

            for r in range(3):
                for b in range(SLOTS):
                    k, g = (b % 4) * KS, b // 4
                    lo, hi = ((0, 512), (512, W_C))[g] if r == 0 else (W_C + (2 * r - 2 + g) * 512,
                                                                     W_C + (2 * r - 1 + g) * 512)
                    fill(b, w_in2[:, k:k + KS, lo:hi], R_IN2 + r)
            for b in range(3):
                fill(b, w_uq[:, :, b * 512:(b + 1) * 512], R_MID)
            for b in range(4):
                fill(3 + b, w_ukv[:, :, b * 512:(b + 1) * 512], R_MID)
            sp.wait_ge(wused[7], R_MID)
            sp.sem_inc(wfull[7], 16)
            with sp.Fori(0, 2) as i:
                fill_round(w_out2, i + R_WO2, i * 1024)
            with sp.Fori(0, 2) as i:
                fill_round(w_pq2, i + R_PQ2, i * 1024)
            sp.wait_ge(gused[7], 2 * GROUNDS * UNITS + 1)
            for t in range(NT):
                sp.dma_start(out[0, t * P:(t + 1) * P, :], x[:, t, :]).then_inc(out_done, 16)
            sp.wait_ge(out_done, 16 * NT)

        @block.gpsimd
        def _(pool):
            st = Steps(pool, pls)
            st.add(pool.memset(ident, 0.0))
            st.add(pool.memset(cn[:, 384:546], 0.0))
            st.add(pool.memset(ones_c, 1.0))
            st.wait()
            st.add(pool.affine_select(out=ident, in_=ident, compare_op=ALU.not_equal, fill=1.0, base=0,
                                      pattern=[[-1, P]], channel_multiplier=1))
            st.link(pool.iota(iota_t, pattern=[[1, T]], base=0, channel_multiplier=0,
                             allow_small_or_imprecise_dtypes=True))
            for half in range(2):
                rows = slice(64 * half, 64 * half + 64)
                for q in range(PAIRS):
                    st.link(pool.memset(mask_b[rows, q, 2 * q + half:2 * q + half + 1], 1.0))
                st.link(pool.memset(mask_c[rows, :].rearrange("p (q f c) -> p q f c", q=PAIRS, f=2)[:, :, half, :], 1.0))
            st.add(pool.memset(quarter[:, 1:2], 0.25))
            for i in range(NQ):
                st.add(pool.memset(nslope[:, i:i + 1], -float(2.0 ** (-8.0 * (i + 1) / NQ))))
            st.wait()
            pool.sem_inc(consts_ready, 1)

            with pool.Fori(0, SSM_K) as k:
                pool.wait_ge(bc_loaded, k * BC + BC)
                for s in range(8):
                    q, d = s // 2, s % 2
                    pool.wait_ge(bt_done, k * 8 + s + 1)
                    pool.tensor_tensor(
                        b_pad[:, s % 2], b_st[:, :, d, q, :].unsqueeze(2).broadcast_to([P, 2, 8, 16]),
                        mask_b[:, q, :].unsqueeze(1).unsqueeze(3).broadcast_to([P, 2, 8, 16]),
                        ALU.mult).then_inc(bpad_ready, 1)

            pool.wait_ge(y_evac, SSM_K + 1)
            st.link(pool.iota(dist, pattern=[[P, NT], [-1, T]], base=0, channel_multiplier=1,
                              allow_small_or_imprecise_dtypes=True))
            pool.sem_inc(dist_ready, 1)
            pool.wait_ge(dist_ready, 2)
            for sign in (1, -1):
                st.link(pool.affine_select(out=dist, in_=dist, compare_op=ALU.is_ge, fill=HUGE, base=WINDOW,
                                           pattern=[[-sign * P, NT], [sign, T]], channel_multiplier=-sign))
            pool.sem_inc(dist_ready, 1)

            def gathers(unit0, down, up):
                for b in range(2):
                    pool.wait_ge(stage_ready, unit0 + b + 1)
                    for kk in range(2 * TOPK):
                        slot, j = kk % SLOTS, kk % TOPK
                        pool.wait_ge(gused[slot], (unit0 + b) * GROUNDS + kk // SLOTS + 1)
                        pool.sem_inc(gathers_issued, 1)
                        table = down if kk < TOPK else up
                        pool.indirect_dma_start(
                            out=gslot[:, slot, :], out_offset=None, in_=table[0],
                            in_offset=bass.IndirectOffsetOnAxis(
                                ap=usub(rST)[:, b * TOPK + j:b * TOPK + j + 1], axis=0),
                        ).then_inc(gfull[slot], 16)

            pool.wait_ge(sk_evac, 8)
            with pool.Fori(0, UNITS // 2) as i:
                gathers(i * 2, a["peer_down"], a["peer_up"])
            pool.wait_ge(x_ready, 16)
            for i in range(ROPE // 2):
                st.add(pool.memset(inv_freq[:, i:i + 1], float(
                    np.float32(ROPE_THETA) ** np.float32(-i / np.float32(ROPE // 2)))))
            st.wait()
            pool.sem_inc(inv_ready, 1)
            pool.wait_ge(qk2_msq, 1)
            st.link(pool.memset(causal[:, 0:P], 0.0))
            st.link(pool.affine_select(out=causal[:, 0:P], in_=causal[:, 0:P], compare_op=ALU.is_ge, fill=-HUGE,
                                       base=0, pattern=[[-1, P]], channel_multiplier=1))
            pool.sem_inc(causal_ready, 1)
            pool.wait_ge(sk_evac, 16)
            with pool.Fori(0, UNITS // 2) as i:
                gathers(i * 2 + UNITS, a["peer_u_2"], a["peer_v_2"])

        @block.tensor
        def _(pe):
            def dense_slot(b, r, lhs, used, kt=KD, w_cols=512):
                g, per = b // 4, kt // KS
                if b % per == 0 and used is not None:
                    pe.wait_ge(pair_evac[g if per == 4 else (b // 2) % 2], used)
                pair = g if per == 4 else (b // 2) % 2
                pe.wait_ge(wfull[b], r * 16 + 16)
                for kk in range(KS):
                    k = (b % per) * KS + kk
                    for t in range(NT):
                        mm = pe.matmul(dense_bank[2 * pair + t][:, 0:w_cols], lhs[:, k, t * P:(t + 1) * P],
                                       wslot[:, b, kk * w_cols:(kk + 1) * w_cols], start=(k == 0),
                                       stop=(k == kt - 1))
                mm.then_inc(wused[b], 1)

            def dense_slot_T(b, r, rhs, used):
                g = b // 4
                if b % 4 == 0 and used is not None:
                    pe.wait_ge(pair_evac[g], used)
                pe.wait_ge(wfull[b], r * 16 + 16)
                for kk in range(KS):
                    k = (b % 4) * KS + kk
                    for c in range(4):
                        mm = pe.matmul(dense_bank[2 * g + c // 2][:, (c % 2) * T:(c % 2 + 1) * T],
                                       wslot[:, b, kk * 512 + c * P:kk * 512 + (c + 1) * P], rhs[:, k, :],
                                       start=(k == 0 and c % 2 == 0), stop=(k == KD - 1), skip_group_check=True)
                mm.then_inc(wused[b], 1)

            batches = [0]

            def transpose_tiles(src, ready, level):
                for t in range(NT):
                    pe.wait_ge(ready, level + t + 1)
                    for kk in range(4):
                        n = batches[0]
                        if n >= 2:
                            pe.wait_ge(tb_evac, n - 1)
                        for j in range(4):
                            c = (kk * 4 + j) * P
                            tr = pe.transpose(tb[n % 2][:, j * P:(j + 1) * P], src[:, t, c:c + P], ident)
                        tr.then_inc(tb_filled, 1)
                        batches[0] += 1

            pe.wait_ge(consts_ready, 1)
            pe.sem_inc(bt_done, 2)
            pe.sem_inc(bu_done, 2)
            pe.sem_inc(y_done, 1)
            pe.sem_inc(o_done, 2)
            transpose_tiles(h, h_ready, 0)
            pe.wait_ge(tb_evac, 8)
            for b in range(SLOTS):
                dense_slot_T(b, R_U, hT, None)
            pe.wait_ge(sp_done, 1)
            for j, w in enumerate((6, 7, 8, 9)):
                tr = pe.transpose(tb[0][:, j * 64:(j + 1) * 64], pw[w], ident[0:64, 0:64])
            tr.then_inc(sp_t, 1)

            def b_transposes(k, s):
                pe.wait_ge(bpad_ready, k * 8 + s + 1)
                pe.wait_ge(bt_evac, k * 8 + s + 2)
                for part in range(2):
                    tr = pe.transpose(tb[0][:, part * P:(part + 1) * P],
                                      b_pad[:, s % 2, part].rearrange("p b c -> p (b c)"), ident)
                tr.then_inc(bt_done, 1)

            def b_times_u(k, s):
                pe.wait_ge(bt_evac, k * 8 + s + 3)
                if s == 0:
                    pe.wait_ge(ct_evac, k + 1)
                pe.wait_ge(bu_used, k * 8 + s + 1)
                for part in range(2):
                    mm = pe.matmul(mb[s % 2][:, part * T:(part + 1) * T], b_t[:, s % 2, part, :],
                                   uT[:, ds(k, 1), :].rearrange("p a n -> p (a n)"), start=(part == 0), stop=True,
                                   skip_group_check=True)
                mm.then_inc(bu_done, 1)

            def c_times_states(k, s):
                q, d = s // 2, s % 2
                if s == 0:
                    pe.wait_ge(y_evac, k + 1)
                pe.wait_ge(de_ready, k * 8 + s + 3)
                for n, (j, rhs) in enumerate(((0, zr_e[:, 1, :]), (1, zi_e[:, 0, :]),
                                              (2, zr_e[:, 0, :]), (2, zi_e[:, 1, :]))):
                    mm = pe.matmul(tb[1][32 * q:32 * q + 32, 0:T], c_p[:, j, d, q, :], rhs,
                                   start=(d == 0 and n == 0), stop=(d == 1 and n == 3), skip_group_check=True)
                mm.then_inc(y_done, 1)

            def ssm_tile(k, dense):
                pe.wait_ge(bc_loaded, k * BC + BC)
                pe.wait_ge(bu_used, k * 8 + 1)
                for j in range(4):
                    tr = pe.transpose(mb[0][:, j * P:(j + 1) * P],
                                      c_st[:, j // 2, j % 2].rearrange("p u n -> p (u n)"), ident)
                tr.then_inc(ct_done, 1)
                b_transposes(k, 0)
                b_times_u(k, 0)
                b_transposes(k, 1)
                for s in range(8):
                    if s < 7:
                        b_times_u(k, s + 1)
                    if s < 6:
                        b_transposes(k, s + 2)
                    if dense is not None:
                        dense_slot(s, dense, hT, dense * 2)
                    c_times_states(k, s)

            pe.wait_ge(sp_done, 2)
            with pe.Fori(0, SSM_K - 1) as k:
                ssm_tile(k, k + R_QKV)
            ssm_tile(SSM_K - 1, None)

            with pe.Fori(0, NKV) as j:
                for t in range(NT):
                    pe.wait_ge(qk_ready, j + 1)
                    for i in range(GQ):
                        tr = pe.transpose(q_bank[t][:, i * P:(i + 1) * P], qk[:, t, i, :], ident)
                    tr.then_inc(qk_t, 1)
                for t in range(NT):
                    tr = pe.transpose(pt_bank[0][:, t * P:(t + 1) * P], qk[:, t, GQ, :], ident)
                tr.then_inc(qk_t, 1)

                def scores(u):
                    t, i = u // GQ, u % GQ
                    pe.wait_ge(nmax_ready, j * UA + u + 1)
                    pe.matmul(mb[u % 2][:, 0:T], qkT[:, i, t * P:(t + 1) * P], qkT[:, GQ, :],
                              start=True, stop=True).then_inc(s_done, 1)

                def p_times_v(u):
                    pe.wait_ge(pt_evac, j * UA + u + 1)
                    pe.wait_ge(o_evac, j * UA + u + 1)
                    for n in range(NT):
                        mm = pe.matmul(o_bank[u % 2][:, 0:P], v_sb[:, n, :],
                                       probT[:, u % 2, n, :], start=(n == 0), stop=(n == NT - 1))
                    mm.then_inc(o_done, 1)

                pe.wait_ge(qk_tevac, j * 3 + 3)
                scores(0)
                for u in range(UA):
                    if u + 1 < UA:
                        scores(u + 1)
                    pe.wait_ge(p_ready, j * UA + u + 1)
                    for n in range(NT):
                        tr = pe.transpose(pt_bank[u % 2][:, n * P:(n + 1) * P],
                                          prob[:, u % 2, n * P:(n + 1) * P], ident)
                    tr.then_inc(pt_done, 1)
                    if u >= 1:
                        p_times_v(u - 1)
                p_times_v(UA - 1)

            pe.wait_ge(o_evac, NKV * UA + 2)
            with pe.Fori(0, 2) as i:
                for b in range(SLOTS):
                    dense_slot(b, i + R_AO, hT, i * 2 + 2 * B_AO)
            pe.wait_ge(y_act, 1)
            with pe.Fori(0, 2) as i:
                for b in range(SLOTS):
                    dense_slot(b, i + R_GLU, yT, i * 4 + (b // 4) * 2 + 2 * B_GLU, kt=SSM_W // P)
            transpose_tiles(proj[:, :, C_GA:C_GA + D], merged_ready, 0)
            pe.wait_ge(tb_evac, 16)
            with pe.Fori(0, 2) as i:
                for b in range(SLOTS):
                    dense_slot(b, i + R_WO, hT, i * 2 + 2 * B_WO)

            def peer_scores(layer, r_pq, b_pq):
                transpose_tiles(h, h_ready, 2 + 4 * layer)
                pe.wait_ge(tb_evac, batches[0])
                with pe.Fori(0, 2) as i:
                    for b in range(SLOTS):
                        dense_slot_T(b, i + r_pq, hT, i * 2 + 2 * b_pq)
                pe.wait_ge(keys_loaded, 32 * (layer + 1))
                for n in range(4):
                    if n >= 2:
                        pe.wait_ge(keys_evac, 4 * layer + n - 1)
                    for j in range(4):
                        i = n * 4 + j
                        tr = pe.transpose(tb[n % 2][:, j * P:(j + 1) * P], key_n[:, i // 2, i % 2, :], ident)
                    tr.then_inc(keys_t, 1)
                pe.wait_ge(keys_evac, 4 * layer + 4)
                for g in range(2):
                    pe.wait_ge(pair_evac[g], 2 * b_pq + 4)
                for n in range(8):
                    if n >= 2:
                        pe.wait_ge(sk_evac, 8 * layer + n - 1)
                    for j in range(4):
                        t, i = n // 4, (n % 4) * 4 + j
                        mm = pe.matmul(mb[n % 2][:, j * P:(j + 1) * P], pqT[:, i, t * P:(t + 1) * P],
                                       keyT[:, i, :], start=True, stop=True)
                    mm.then_inc(sk_done, 1)

            peer_scores(0, R_PQ, B_PQ)

            pe.wait_ge(par_loaded, 16 * 7)
            pe.transpose(mb[0][:, 0:80], par_rows, ident[0:80, 0:80]).then_inc(par_t, 1)
            transpose_tiles(h, h_ready, 4)
            pe.wait_ge(tb_evac, batches[0])
            for b in range(SLOTS):
                dense_slot(b, R_IN2, hT, 2 * B_IN2, w_cols=512 if b < 4 else W_C - 512)
            for r in (1, 2):
                for b in range(SLOTS):
                    dense_slot_T(b, R_IN2 + r, hT, 2 * (B_IN2 + r))
            pe.wait_ge(c_ready, 1)
            for t in range(NT):
                for n_tr, lo in ((4, 0), (2, 4)):
                    n = batches[0]
                    pe.wait_ge(tb_evac, n - 1)
                    for j in range(n_tr):
                        tr = pe.transpose(tb[n % 2][:, j * P:(j + 1) * P], c2[:, t, (lo + j) * P:(lo + j + 1) * P], ident)
                    tr.then_inc(tb_filled, 1)
                    batches[0] += 1
            pe.wait_ge(tb_evac, batches[0])
            for b in range(7):
                pair = b % 2
                pe.wait_ge(pair_evac[pair], 2 * (B_UQ + b // 2))
                pe.wait_ge(wfull[b], 16 * (R_MID + 1))
                lo, kt = (0, 4) if b < 3 else (4, 2)
                for k in range(kt):
                    for t in range(NT):
                        mm = pe.matmul(dense_bank[2 * pair + t][:, :], cT[:, lo + k, t * P:(t + 1) * P],
                                       wslot[:, b, k * 512:(k + 1) * 512], start=(k == 0), stop=(k == kt - 1))
                mm.then_inc(wused[b], 1)
            pe.sem_inc(wused[7], 1)
            pe.wait_ge(gates_loaded, 32)
            pe.wait_ge(xc_ready, 1)
            for hh in range(NH2):
                if hh >= 2:
                    pe.wait_ge(gate_act, 2 * (hh - 1))
                for g in range(2):
                    mm = pe.matmul(mb[hh % 2][:, g * T:(g + 1) * T], w_gates[:, g, hh, :], xcT[:, hh, :],
                                   start=(g == 0), stop=True, skip_group_check=True)
                mm.then_inc(gate_mm, 1)
            pe.wait_ge(gate_act, 16)
            pe.sem_inc(o2_done, 2)
            pe.wait_ge(pair_evac[0], 2 * B_WO2)
            pe.wait_ge(pair_evac[1], 2 * B_WO2)
            with pe.Fori(0, NH2) as j:
                pe.wait_ge(hd_copied, j * 5 + 5)
                for i in range(2):
                    for t in range(NT):
                        pe.transpose(dense_bank[2][:, (i * 2 + t) * P:(i * 2 + t + 1) * P], head_n[:, i, t, :], ident)
                for i in range(2):
                    for t in range(NT):
                        tr = pe.transpose(dense_bank[3][0:64, (i * 2 + t) * P:(i * 2 + t + 1) * P],
                                          head_r[:, i, t, :], ident)
                tr.then_inc(hd_t, 1)
                pe.wait_ge(hd_tevac, j * 2 + 2)
                for t in range(NT):
                    n = (t + 1) * P
                    pe.wait_ge(nm2_ready, j * 2 + t + 1)
                    pe.matmul(mb[t][:, 0:n], headT_n[:, 0, t * P:(t + 1) * P], headT_n[:, 1, 0:n],
                              start=True, stop=False)
                    pe.matmul(mb[t][:, 0:n], headT_r[:, 0, t * P:(t + 1) * P], headT_r[:, 1, 0:n],
                              start=False, stop=True).then_inc(s2_done, 1)
                for t in range(NT):
                    pe.wait_ge(p2_ready, j * 2 + t + 1)
                    for n in range(t + 1):
                        tr = pe.transpose(tb[t][:, n * P:(n + 1) * P], prob2[:, t, n * P:(n + 1) * P], ident)
                    tr.then_inc(pt2_done, 1)
                for t in range(NT):
                    pe.wait_ge(pt2_evac, j * 2 + t + 1)
                    pe.wait_ge(o2_evac, j * 2 + t + 1)
                    for n in range(t + 1):
                        mm = pe.matmul(dense_bank[t][:, 0:P], head_v[:, n, :], prob2T[:, t, n * P:(n + 1) * P],
                                       start=(n == 0), stop=(n == t))
                    mm.then_inc(o2_done, 1)
            pe.wait_ge(osq_ready, 1)
            for t in range(NT):
                for g in range(2):
                    for k in range(8):
                        mm = pe.matmul(mb[0][:, 2 * t + g:2 * t + g + 1], osq[:, 8 * g + k, t * P:(t + 1) * P],
                                       ones_c, start=(k == 0), stop=(k == 7), skip_group_check=True)
            mm.then_inc(oss_done, 1)
            pe.wait_ge(mixed_ready, 1)
            with pe.Fori(0, 2) as i:
                for b in range(SLOTS):
                    lhs = hT if b % 4 < 2 else hT[:, 8:16, :]
                    dense_slot(b, i + R_WO2, lhs, i * 4 + (b // 4) * 2 + 2 * B_WO2, kt=8)
            peer_scores(1, R_PQ2, B_PQ2)

        @block.scalar
        def _(act):
            st = Steps(act, acs)

            def norm_rms(m):
                for t in range(NT):
                    act.wait_ge(msq_ready, 2 * m + t + 1)
                    act.activation(stat[:, 4 + t:5 + t], stat[:, 2 + t:3 + t], ACT.Sqrt).then_inc(rms_ready, 1)

            batches = [0]

            def evac_tiles():
                for t in range(NT):
                    for kk in range(4):
                        n = batches[0]
                        act.wait_ge(tb_filled, n + 1)
                        act.activation(hT[:, kk * 4:(kk + 1) * 4, t * P:(t + 1) * P],
                                       tb[n % 2][:, :].rearrange("p (k n) -> p k n", k=4),
                                       ACT.Copy).then_inc(tb_evac, 1)
                        batches[0] += 1

            act.dma_start(gain, a["mix_norm_g"][0].partition_broadcast(P)).then_inc(gain_loaded, 16)
            act.dma_start(ssm_d, a["ssm_d"][0].rearrange("(k p) -> p k", p=P),
                          allow_slow_non_contiguous=True).then_inc(small_loaded, 16)
            act.dma_start(sink, a["attn_sink"][0].partition_broadcast(P)).then_inc(small_loaded, 16)
            act.sem_inc(bt_evac, 2)
            norm_rms(0)
            evac_tiles()

            act.dma_start(pw[0], a["ssm_a_re"].rearrange("l d (g two) n -> (l d g) (two n)", two=2)).then_inc(ssm_loaded, 16)
            act.dma_start(pw[1], a["ssm_a_im"].rearrange("l d (g two) n -> (l d g) (two n)", two=2)).then_inc(ssm_loaded, 16)
            act.dma_start(step2, a["ssm_log_step"].rearrange("l d (g two) -> (l d g) two", two=2)).then_inc(ssm_loaded, 16)

            b_dram = [a[n].rearrange("l d (k q two) n c -> k (two n) (l d) q c", q=PAIRS, two=2)
                      for n in ("ssm_b_re", "ssm_b_im")]
            c_dram = [a[n].rearrange("l d (k g) c n -> k (g c) (l d) n", g=8) for n in ("ssm_c_re", "ssm_c_im")]

            def load_bc(k):
                for part in range(2):
                    for d in range(2):
                        src = b_dram[part][ds(k, 1), :, d].rearrange("k p q c -> (k p) q c")
                        act.dma_start(b_st[:, part, d], src).then_inc(bc_loaded, 16)
                    src = c_dram[part][ds(k, 1)].rearrange("k p d n -> (k p) d n")
                    for u in range(2):
                        act.dma_start(c_st[:, :, part, u, :], src).then_inc(bc_loaded, 16)

            load_bc(0)
            for g in range(2):
                act.wait_ge(wused[4 * g + 3], R_U + 1)
                for c in range(2):
                    act.activation(uT[:, 4 * g + 2 * c:4 * g + 2 * c + 2, :],
                                   dense_bank[2 * g + c][:, :].rearrange("p (k n) -> p k n", k=2),
                                   ACT.Copy).then_inc(pair_evac[g], 1)
            act.wait_ge(ssm_loaded, 48)
            act.activation(step2, step2, ACT.Exp).then_inc(sp_act, 1)
            act.wait_ge(sp_in, 1)
            act.activation(pw[6], pw[2], ACT.Exp).then_inc(sp_act, 1)
            act.wait_ge(sp_in, 2)
            act.activation(pw[4], pw[10], ACT.Sin, scale=TWO_PI_BELOW).then_inc(sp_act, 1)
            act.activation(pw[5], pw[11], ACT.Sin, scale=TWO_PI_BELOW).then_inc(sp_act, 1)

            def dense_evac(r, g, dest, col, n=512):
                act.wait_ge(wused[4 * g + 3], r + 1)
                for t in range(NT):
                    act.activation(dest[:, t, ds(col, n)], dense_bank[2 * g + t][:, 0:n],
                                   ACT.Copy).then_inc(pair_evac[g], 1)

            def ssm_tile(k, dense):
                for s in range(8):
                    act.wait_ge(bt_done, k * 8 + s + 3)
                    act.wait_ge(bu_done, k * 8 + s + 1)
                    act.activation(b_t[:, s % 2].rearrange("p a n -> p (a n)"),
                                   tb[0][:, 0:2 * P], ACT.Copy).then_inc(bt_evac, 1)
                    act.wait_ge(f_ready, k * 8 + s + 1)
                    act.wait_ge(de_ready, k * 8 + s + 1)
                    act.activation(rot[:, s % 2], phase, ACT.Sin, scale=TWO_PI_BELOW).then_inc(e_ready, 1)
                    if dense is not None and s in (4, 7):
                        dense_evac(dense, s // 5, proj, (k * 2 + s // 5) * 512)

            with act.Fori(0, SSM_K - 1) as k:
                ssm_tile(k, k + R_QKV)
                act.wait_ge(bpad_ready, k * 8 + 8)
                act.wait_ge(ct_done, k + 1)
                load_bc(k + 1)
            ssm_tile(SSM_K - 1, None)

            act.wait_ge(y_evac, SSM_K + 1)
            act.dma_start(g_qk[:, 0, :], a["q_norm_g"][0].partition_broadcast(P)).then_inc(small_loaded, 16)
            act.dma_start(g_qk[:, GQ, :], a["k_norm_g"][0].partition_broadcast(P)).then_inc(small_loaded, 16)
            for t in range(NT):
                act.activation(proj[:, t, C_GA:C_GA + 2 * D], proj[:, t, C_GA:C_GA + 2 * D],
                               ACT.Sigmoid).then_inc(gate_sig, 1)
            with act.Fori(0, NKV) as j:
                act.wait_ge(o_evac, j * UA + 2)
                act.activation(qk[:, :, 0:GQ, :].rearrange("p t j c -> p t (j c)"), proj[:, :, ds(j * 512, 512)],
                               ACT.Copy).then_inc(qk_copied, 1)
                act.activation(qk[:, :, GQ, :], proj[:, :, ds(j * HD + C_K, HD)], ACT.Copy).then_inc(qk_copied, 1)
                act.activation(v_sb, proj[:, :, ds(j * HD + C_V, HD)], ACT.Copy).then_inc(qk_copied, 1)
                act.wait_ge(qk_msq, j + 1)
                act.activation(sm[:, 10:20], sm[:, 0:10], ACT.Sqrt).then_inc(qk_rms, 1)
                for t in range(NT):
                    act.wait_ge(qk_t, j * 3 + t + 1)
                    act.activation(qkT[:, 0:GQ, t * P:(t + 1) * P], q_bank[t][:, :].rearrange("p (j n) -> p j n", j=GQ),
                                   ACT.Copy).then_inc(qk_tevac, 1)
                act.wait_ge(qk_t, j * 3 + 3)
                act.activation(qkT[:, GQ, :], pt_bank[0][:, 0:T], ACT.Copy).then_inc(qk_tevac, 1)
                for u in range(UA):
                    i = u % GQ
                    act.wait_ge(nmax_ready, j * UA + u + 3)
                    act.activation(prob[:, u % 2, :], prob[:, u % 2, :], ACT.Exp, bias=sm[:, 20 + u % 2:21 + u % 2],
                                   accum_out=sm[:, 22 + u % 2:23 + u % 2]).then_inc(p_exp, 1)
                    act.activation(sm[:, 24 + u % 2:25 + u % 2], sink[:, ds(j * GQ + i, 1)], ACT.Exp,
                                   bias=sm[:, 20 + u % 2:21 + u % 2]).then_inc(p_exp, 1)
                    act.wait_ge(pt_done, j * UA + u + 1)
                    act.wait_ge(o_done, j * UA + u + 1)
                    act.activation(probT[:, u % 2].rearrange("p k n -> p (k n)"),
                                   pt_bank[u % 2][:, 0:T], ACT.Copy).then_inc(pt_evac, 1)

            act.wait_ge(y_evac, SSM_K + 1)
            act.activation(hs[:, 2048:4096], hs[:, 2048:4096], ACT.Gelu).then_inc(y_act, 1)
            with act.Fori(0, 2) as i:
                for g in range(2):
                    act.wait_ge(wused[4 * g + 3], i + R_GLU + 1)
                    act.wait_ge(glu_used, i * 4 + g * 2 + 2)
                    for t in range(NT):
                        act.activation(glu_sg[:, t, :], dense_bank[2 + t][:, :], ACT.Sigmoid).then_inc(pair_evac[1], 1)
            evac_tiles()

            def peer_head(layer, g, keys, r_pq, gain_after):
                act.wait_ge(x_ready, gain_after)
                act.dma_start(gain, g.partition_broadcast(P)).then_inc(gain_loaded, 16)
                for s in range(2):
                    act.dma_start(key_n[:, :, s, :], keys[s].rearrange("h k d -> k h d")).then_inc(keys_loaded, 16)
                norm_rms(1 + 2 * layer)
                evac_tiles()
                with act.Fori(0, 2) as i:
                    for g in range(2):
                        act.wait_ge(wused[4 * g + 3], i + r_pq + 1)
                        for c in range(2):
                            act.activation(pqT[:, ds(i * 8 + 4 * g + 2 * c, 2), :],
                                           dense_bank[2 * g + c][:, :].rearrange("p (k n) -> p k n", k=2),
                                           ACT.Copy).then_inc(pair_evac[g], 1)
                for n in range(4):
                    act.wait_ge(keys_t, 4 * layer + n + 1)
                    act.activation(keyT[:, n * 4:(n + 1) * 4, :].rearrange("p j c -> p (j c)"), tb[n % 2][:, :],
                                   ACT.Copy).then_inc(keys_evac, 1)
                for n in range(8):
                    act.wait_ge(sk_done, 8 * layer + n + 1)
                    act.activation(kscore[:, n * 512:(n + 1) * 512], mb[n % 2][:, :], ACT.Copy).then_inc(sk_evac, 1)

            def peer_soft(u, b):
                act.wait_ge(topk_v, u + 1)
                act.activation(sub(rGT)[:, b * TOPK:(b + 1) * TOPK], sub(rTP)[:, b * TOPK:(b + 1) * TOPK], ACT.Exp,
                               bias=sub(rSS)[:, b:b + 1], accum_out=sub(rSS)[:, 2 + b:3 + b]).then_inc(topk_e, 1)

            def peer_gelu(u, b):
                act.wait_ge(gused[7], u * GROUNDS + 3)
                act.activation(sub(rGE)[:, b * TOPK:(b + 1) * TOPK], sub(rAC)[:, b * TOPK:(b + 1) * TOPK],
                               ACT.Gelu).then_inc(gelu_ready, 1)

            def peer_units(layer):
                base = layer * UNITS
                peer_soft(base, 0)
                with act.Fori(0, UNITS // 2 - 1) as i:
                    peer_gelu(i * 2 + base, 0)
                    peer_soft(i * 2 + base + 1, 1)
                    peer_gelu(i * 2 + base + 1, 1)
                    peer_soft(i * 2 + base + 2, 0)
                last = base + UNITS - 2
                peer_gelu(last, 0)
                peer_soft(last + 1, 1)
                peer_gelu(last + 1, 1)

            peer_head(0, a["ffn_norm_g"][0], (a["peer_sub_keys_1"][0], a["peer_sub_keys_2"][0]), R_PQ, 8)
            peer_units(0)

            act.wait_ge(x_ready, 16)
            act.dma_start(gain, a["mix_norm_g_2"][0].partition_broadcast(P)).then_inc(gain_loaded, 16)
            rows = 0
            for name in ("conv_w_2", "conv_b_2", "b_rgate_2", "b_igate_2", "lru_lambda_2", "attn_out_norm_g_2",
                         "rec_out_norm_g_2"):
                src = (a[name][0].rearrange("j (k p) -> (j k) p", p=P) if name == "conv_w_2"
                       else a[name][0].rearrange("(k p) -> k p", p=P))
                n = src.shape[0]
                act.dma_start(par_rows[rows:rows + n, :], src).then_inc(par_loaded, 16)
                rows += n
            for dst, name in ((g_cq, "q_norm_g_2"), (g_ckv, "kv_norm_g_2"), (g_qh, "q_head_norm_g_2"),
                              (g_kh, "k_head_norm_g_2")):
                act.dma_start(dst, a[name][0].partition_broadcast(P)).then_inc(rope_loaded, 16)
            act.dma_start(pos_i, a["positions_2"][0].rearrange("(t p) -> p t", p=P),
                          allow_slow_non_contiguous=True).then_inc(rope_loaded, 16)
            norm_rms(2)
            evac_tiles()
            for g, name in enumerate(("w_rgate_2", "w_igate_2")):
                act.dma_start(w_gates[:, g], a[name][0].rearrange("h i j -> i h j")).then_inc(gates_loaded, 16)
            act.wait_ge(ang_ready, 1)
            act.activation(trig, ang, ACT.Sin, scale=TWO_PI_BELOW).then_inc(trig_ready, 1)
            act.wait_ge(par_ready, 1)
            act.activation(lp[:, 0:8], lam, ACT.Abs).then_inc(lam_act, 1)
            act.wait_ge(lam_act, 1)
            act.activation(lp[:, 8:16], lp[:, 0:8], ACT.Exp, scale=-1.0).then_inc(lam_act, 1)
            for g in range(2):
                n = 512 if g == 0 else W_C - 512
                dense_evac(R_IN2, g, c2, g * 512, n)
            act.wait_ge(c_msq, 1)
            act.activation(stat[:, 20:24], stat[:, 16:20], ACT.Sqrt).then_inc(c_rms, 1)
            for r, dst in ((1, xrT), (2, ygT)):
                for g in range(2):
                    act.wait_ge(wused[4 * g + 3], R_IN2 + r + 1)
                    for c in range(2):
                        act.activation(dst[:, 4 * g + 2 * c:4 * g + 2 * c + 2, :],
                                       dense_bank[2 * g + c][:, :].rearrange("p (k n) -> p k n", k=2),
                                       ACT.Copy).then_inc(pair_evac[g], 1)
            for t in range(NT):
                for n_tr, lo in ((4, 0), (2, 4)):
                    n = batches[0]
                    act.wait_ge(tb_filled, n + 1)
                    act.activation(cT[:, lo:lo + n_tr, t * P:(t + 1) * P],
                                   tb[n % 2][:, 0:n_tr * P].rearrange("p (k n) -> p k n", k=n_tr),
                                   ACT.Copy).then_inc(tb_evac, 1)
                    batches[0] += 1
            q2f = q2.rearrange("p t h c -> p t (h c)")
            kv2f = kv2.rearrange("p t h c -> p t (h c)")
            for b in range(7):
                act.wait_ge(wused[b], R_MID + 1)
                dst, col = (q2f, b * 512) if b < 3 else (kv2f, (b - 3) * 512)
                for t in range(NT):
                    act.activation(dst[:, t, col:col + 512], dense_bank[2 * (b % 2) + t][:, :],
                                   ACT.Copy).then_inc(pair_evac[b % 2], 1)
            act.wait_ge(pair_evac[1], 2 * B_WO2 - 2)
            act.sem_inc(pair_evac[1], 2)
            for hh in range(NH2):
                act.wait_ge(gate_mm, hh + 1)
                for g, (dst, bias) in enumerate(((rr_g, b_rg), (ii_g, b_ig))):
                    act.activation(k3(dst)[:, hh, :], mb[hh % 2][:, g * T:(g + 1) * T], ACT.Sigmoid,
                                   bias=bias[:, hh:hh + 1]).then_inc(gate_act, 1)
            act.wait_ge(lam_dve, 1)
            act.wait_ge(gate_act, 16)
            for hh in range(NH2):
                act.activation(k3(th_g)[:, hh, :], k3(rr_g)[:, hh, :], ACT.Tanh,
                               scale=neg_c[:, hh:hh + 1]).then_inc(lru_act, 1)
            act.wait_ge(lru_act, 8)
            for hh in range(NH2):
                act.activation(k3(rr_g)[:, hh, :], k3(rr_g)[:, hh, :], ACT.Exp,
                               scale=neg_c[:, hh:hh + 1]).then_inc(lru_act, 1)
            act.wait_ge(lru_dve, 1)
            act.activation(th_g, th_g, ACT.Sqrt, scale=-1.0).then_inc(lru_act, 1)
            act.activation(ygT, ygT, ACT.Gelu).then_inc(lru_act, 1)
            act.wait_ge(qk2_msq, 1)
            act.activation(rms2, msq2[:, 0:32], ACT.Sqrt).then_inc(qk2_rms, 1)
            act.wait_ge(qk2_ready, 1)
            with act.Fori(0, NH2) as j:
                act.wait_ge(o2_done, j * 2 + 2)
                hj = ds(j, 1)
                for dst, src in ((head_n[:, 0], q2[:, :, hj, 0:NOPE]), (head_n[:, 1], kn2[:, :, hj, :]),
                                 (head_r[:, 0], qr2[:, :, hj, :]), (head_r[:, 1], krh[:, :, hj, :]),
                                 (head_v, kv2[:, :, hj, NOPE:2 * NOPE])):
                    act.activation(dst, src.rearrange("p t h c -> p t (h c)"), ACT.Copy).then_inc(hd_copied, 1)
                act.wait_ge(hd_t, j + 1)
                act.activation(headT_n.rearrange("p j n -> p (j n)"), dense_bank[2][:, :], ACT.Copy).then_inc(hd_tevac, 1)
                act.activation(headT_r.rearrange("p j n -> p (j n)"), dense_bank[3][0:64, :],
                               ACT.Copy).then_inc(hd_tevac, 1)
                for t in range(NT):
                    n = (t + 1) * P
                    act.wait_ge(nm2_ready, j * 2 + t + 3)
                    act.activation(prob2[:, t, 0:n], prob2[:, t, 0:n], ACT.Exp, bias=att[:, t:t + 1],
                                   accum_out=att[:, 2 + t:3 + t]).then_inc(p2_exp, 1)
                for t in range(NT):
                    n = (t + 1) * P
                    act.wait_ge(pt2_done, j * 2 + t + 1)
                    act.activation(prob2T[:, t, 0:n], tb[t][:, 0:n], ACT.Copy).then_inc(pt2_evac, 1)
            act.wait_ge(oss_done, 2)
            act.activation(stat[:, 28:32], stat[:, 24:28], ACT.Sqrt).then_inc(oss_rms, 1)
            peer_head(1, a["ffn_norm_g_2"][0], (a["peer_keys_1_2"][0], a["peer_keys_2_2"][0]), R_PQ2, 24)
            peer_units(1)

        @block.vector
        def _(v):
            st = Steps(v, dve)
            v.sem_inc(bu_used, 2)
            v.sem_inc(de_ready, 2)
            v.sem_inc(y_evac, 1)
            v.sem_inc(nmax_ready, 2)
            v.sem_inc(o_evac, 2)
            v.sem_inc(glu_used, 2)
            for b in range(SLOTS):
                v.sem_inc(gused[b], 1)

            def norm(m):
                for t in range(NT):
                    st.link(v.tensor_tensor_reduce(h[:, t, :], x[:, t, :], x[:, t, :], 1.0, 0.0, ALU.mult, ALU.add,
                                                   stat[:, t:t + 1]))
                    v.tensor_scalar(stat[:, 2 + t:3 + t], stat[:, t:t + 1], 1.0 / D, EPS, ALU.mult,
                                    ALU.add).then_inc(msq_ready, 1)
                v.wait_ge(gain_loaded, 16 * (m + 1))
                for t in range(NT):
                    v.wait_ge(rms_ready, 2 * m + t + 1)
                    st.link(v.reciprocal(stat[:, 6 + t:7 + t], stat[:, 4 + t:5 + t]))
                    v.scalar_tensor_tensor(h[:, t, :], x[:, t, :], stat[:, 6 + t:7 + t], gain, ALU.mult,
                                           ALU.mult).then_inc(h_ready, 1)

            v.wait_ge(x_loaded, 32)
            norm(0)

            a_re, a_im = pw[0], pw[1]
            bcast = lambda i: step2.unsqueeze(2).broadcast_to([64, 2, 64])
            v.wait_ge(sp_act, 1)
            v.wait_ge(ssm_loaded, 48)
            halves = lambda w: w.rearrange("p (f n) -> p f n", f=2)
            v.tensor_tensor(halves(pw[2]), halves(a_re), bcast(0), ALU.mult).then_inc(sp_in, 1)
            st.link(v.tensor_tensor(halves(pw[3]), halves(a_im), bcast(0), ALU.mult))
            st.link(v.tensor_scalar(pw[3], pw[3], float(1 / (2 * np.pi)), None, ALU.mult))
            st.link(v.tensor_scalar(pw[12], pw[3], ROUND, -ROUND, ALU.add, ALU.add))
            st.link(v.tensor_tensor(pw[7], pw[3], pw[12], ALU.subtract))
            st.link(v.tensor_scalar(pw[3], pw[7], 0.25, None, ALU.add))
            st.link(v.tensor_scalar(pw[12], pw[3], ROUND, -ROUND, ALU.add, ALU.add))
            st.link(v.tensor_copy(pw[10], pw[7]))
            v.tensor_tensor(pw[11], pw[3], pw[12], ALU.subtract).then_inc(sp_in, 1)
            v.wait_ge(sp_act, 4)
            st.link(v.tensor_tensor(pw[5], pw[5], pw[6], ALU.mult))
            st.link(v.tensor_scalar(pw[5], pw[5], -1.0, None, ALU.add))
            st.link(v.tensor_tensor(pw[4], pw[4], pw[6], ALU.mult))
            st.add(v.tensor_tensor(pw[12], a_re, a_re, ALU.mult))
            st.link(v.tensor_tensor(pw[13], a_im, a_im, ALU.mult))
            st.link(v.tensor_tensor(pw[12], pw[12], pw[13], ALU.add))
            st.link(v.reciprocal(pw[12], pw[12]))
            st.add(v.tensor_tensor(pw[8], pw[5], a_re, ALU.mult))
            st.add(v.tensor_tensor(pw[13], pw[4], a_im, ALU.mult))
            st.add(v.tensor_tensor(pw[9], pw[4], a_re, ALU.mult))
            st.link(v.tensor_tensor(pw[3], pw[5], a_im, ALU.mult))
            st.add(v.tensor_tensor(pw[8], pw[8], pw[13], ALU.add))
            st.link(v.tensor_tensor(pw[9], pw[9], pw[3], ALU.subtract))
            st.link(v.tensor_tensor(pw[8], pw[8], pw[12], ALU.mult))
            v.tensor_tensor(pw[9], pw[9], pw[12], ALU.mult).then_inc(sp_done, 1)
            v.wait_ge(sp_t, 1)
            v.tensor_copy(prm.rearrange("p j n -> p (j n)"), tb[0][:, 0:256]).then_inc(sp_done, 1)
            v.wait_ge(sp_done, 2)
            for g in range(2):
                v.wait_ge(pair_evac[g], 2)
            v.wait_ge(small_loaded, 32)

            def direction(t, d):
                return t if d == 0 else t[:, :, ::-1]

            def phase_1(k, s):
                q, d = s // 2, s % 2
                return v.scalar_tensor_tensor(
                    phase, iota_t.unsqueeze(1).broadcast_to([P, 2, T]), prm[:, 1, ds(k * 4 + (d * 32 + q), 1)],
                    quarter.unsqueeze(2).broadcast_to([P, 2, T]), ALU.mult, ALU.add)

            def phase_2():
                return v.tensor_scalar(whole, phase, ROUND, -ROUND, ALU.add, ALU.add)

            def phase_3():
                return v.tensor_tensor(phase, phase, whole, ALU.subtract)

            def ssm_tile(k):
                st.link(phase_1(k, 0))
                st.link(phase_2())
                phase_3().then_inc(f_ready, 1)
                v.wait_ge(ct_done, k + 1)
                v.tensor_tensor(c_t.rearrange("p d a n -> p (d a) n"),
                                mb[0][:, :].rearrange("p (j n) -> p j n", j=4),
                                mask_c.unsqueeze(1).broadcast_to([P, 4, P]), ALU.mult).then_inc(ct_evac, 1)
                v.wait_ge(ct_evac, k + 1)
                f = [prm[:, 2 + j, :].rearrange("p (d n) -> p d n", d=2)[:, :, ds(k * 4, 4)]
                     .unsqueeze(3).broadcast_to([P, 2, PAIRS, 32]) for j in range(2)]
                c = [c_t[:, :, j, :].rearrange("p d (q c) -> p d q c", q=PAIRS) for j in range(2)]
                t4 = [sc[:, r[0] + 256 * j:r[0] + 256 * (j + 1)] for r in (rA, rB) for j in range(2)]
                w4 = [w.rearrange("p (d q c) -> p d q c", d=2, q=PAIRS) for w in t4]
                st.add(v.tensor_tensor(w4[0], c[0], f[0], ALU.mult))
                st.add(v.tensor_tensor(w4[1], c[1], f[1], ALU.mult))
                st.add(v.tensor_tensor(w4[2], c[0], f[1], ALU.mult))
                st.add(v.tensor_tensor(w4[3], c[1], f[0], ALU.mult))
                v.wait_ge(y_done, k * 8 + 1)
                st.wait()
                flat = [c_p[:, j].rearrange("p d q c -> p (d q c)") for j in range(3)]
                st.add(v.tensor_tensor(flat[0], t4[0], t4[1], ALU.subtract))
                st.add(v.tensor_tensor(flat[1], t4[1], t4[0], ALU.subtract))
                st.link(v.scalar_tensor_tensor(flat[2], t4[2], -1.0, t4[3], ALU.mult, ALU.subtract))
                for s in range(8):
                    q, d = s // 2, s % 2
                    both = lambda t: t.unsqueeze(1).broadcast_to([P, 2, T])
                    e = direction(rot[:, s % 2], d)
                    radius = prm[:, 0, ds(k * 4 + (d * 32 + q), 1)].broadcast_to([P, T])
                    v.wait_ge(bu_done, k * 8 + s + 3)
                    v.wait_ge(e_ready, k * 8 + s + 1)
                    st.add(v.tensor_tensor(bre_e, both(mb[s % 2][:, 0:T]), e, ALU.mult))
                    v.tensor_tensor(bim_e, both(mb[s % 2][:, T:2 * T]), e, ALU.mult).then_inc(bu_used, 1)
                    p1 = st.add(phase_1(k, s + 1)) if s < 7 else None
                    v.wait_ge(bu_used, k * 8 + s + 3)
                    st.add(v.tensor_tensor(z_in[:, 0, :], bre_e[:, 1, :], bim_e[:, 0, :], ALU.add))
                    z2 = st.add(v.tensor_tensor(z_in[:, 1, :], bim_e[:, 1, :], bre_e[:, 0, :], ALU.subtract))
                    if s < 7:
                        st.wait(p1)
                        p2 = st.add(phase_2())
                    st.wait(z2)
                    for c_ in range(2):
                        zi, zo = z_in[:, c_, :], z_out[:, c_, :]
                        if d:
                            zi, zo = zi[:, ::-1], zo[:, ::-1]
                        z3 = st.add(v.tensor_tensor_scan(zo, radius, zi, 0.0, ALU.mult, ALU.add))
                    if s < 7:
                        st.wait(p2)
                        phase_3().then_inc(f_ready, 1)
                    v.wait_ge(y_done, k * 8 + s + 1)
                    st.wait(z3)
                    st.add(v.tensor_tensor(zr_e, both(z_out[:, 0, :]), e, ALU.mult))
                    v.tensor_tensor(zi_e, both(z_out[:, 1, :]), e, ALU.mult).then_inc(de_ready, 1)
                v.wait_ge(y_done, k * 8 + 9)
                kk = ds(k, 1)
                v.scalar_tensor_tensor(yT[:, kk, :].rearrange("p a n -> p (a n)"),
                                       uT[:, kk, :].rearrange("p a n -> p (a n)"), ssm_d[:, kk],
                                       tb[1][:, 0:T], ALU.mult, ALU.add).then_inc(y_evac, 1)
                v.wait_ge(y_evac, k + 2)
                v.sem_inc(turn_over, 1)
                st.clear()

            st.clear()
            v.wait_ge(consts_ready, 1)
            with v.Fori(0, SSM_K) as k:
                ssm_tile(k)

            v.wait_ge(dist_ready, 1)
            v.scalar_tensor_tensor(dist, dist, -1.0, dist, ALU.mult, ALU.max).then_inc(dist_ready, 1)
            st.add(v.tensor_scalar(nsink, sink, -1.0, None, ALU.mult))
            v.wait_ge(small_loaded, 64)
            for i in range(1, GQ):
                st.add(v.tensor_scalar(g_qk[:, i, :], g_qk[:, 0, :], float(HD ** -0.5), None, ALU.mult))
            st.wait()
            st.link(v.tensor_scalar(g_qk[:, 0, :], g_qk[:, 0, :], float(HD ** -0.5), None, ALU.mult))
            v.wait_ge(dist_ready, 3)
            st.clear()
            with v.Fori(0, NKV) as j:
                v.wait_ge(qk_copied, j * 3 + 3)
                rows = qk.rearrange("p t j c -> p (t j) c")
                flat = qk.rearrange("p t j c -> p (t j c)")
                st.link(v.tensor_tensor(qk_sq, flat, flat, ALU.mult))
                st.link(v.tensor_reduce(sm[:, 0:10], qk_sq.rearrange("p (r c) -> p r c", c=HD), AX, ALU.add))
                v.tensor_scalar(sm[:, 0:10], sm[:, 0:10], 1.0 / HD, EPS, ALU.mult, ALU.add).then_inc(qk_msq, 1)
                v.wait_ge(qk_rms, j + 1)
                st.link(v.reciprocal(sm[:, 30:40], sm[:, 10:20]))
                st.link(v.tensor_tensor(rows, rows, sm[:, 30:40].unsqueeze(2).broadcast_to([P, 10, HD]), ALU.mult))
                v.tensor_tensor(qk, qk, g_qk.unsqueeze(1).broadcast_to([P, NT, GQ + 1, HD]),
                                ALU.mult).then_inc(qk_ready, 1)

                def logits(u):
                    t, i = u // GQ, u % GQ
                    v.wait_ge(s_done, j * UA + u + 1)
                    if u >= 2:
                        v.wait_ge(pt_done, j * UA + u - 1)
                    st.link(v.scalar_tensor_tensor(prob[:, u % 2, :], dist[:, t, :], nslope[:, ds(j * GQ + i, 1)],
                                                   mb[u % 2][:, 0:T], ALU.mult, ALU.add))
                    st.link(v.tensor_reduce(sm[:, 26:27], prob[:, u % 2, :], AX, ALU.max, negate=True))
                    v.tensor_tensor(sm[:, 20 + u % 2:21 + u % 2], sm[:, 26:27], nsink[:, ds(j * GQ + i, 1)],
                                    ALU.min).then_inc(nmax_ready, 1)

                def take_o(u):
                    t, i = u // GQ, u % GQ
                    v.wait_ge(o_done, j * UA + u + 3)
                    v.tensor_copy(hT[:, ds(j * GQ + i, 1), t * P:(t + 1) * P].rearrange("p a n -> p (a n)"),
                                  o_bank[u % 2][:, 0:P]).then_inc(o_evac, 1)

                logits(0)
                for u in range(UA):
                    if u + 1 < UA:
                        logits(u + 1)
                    v.wait_ge(p_exp, (j * UA + u) * 2 + 2)
                    st.link(v.tensor_tensor(sm[:, 27:28], sm[:, 22 + u % 2:23 + u % 2],
                                            sm[:, 24 + u % 2:25 + u % 2], ALU.add))
                    st.link(v.reciprocal(sm[:, 28:29], sm[:, 27:28]))
                    v.tensor_scalar(prob[:, u % 2, :], prob[:, u % 2, :], sm[:, 28:29], None,
                                    ALU.mult).then_inc(p_ready, 1)
                    if u >= 2:
                        take_o(u - 2)
                take_o(UA - 2)
                take_o(UA - 1)
                st.clear()

            v.wait_ge(gate_sig, 2)
            with v.Fori(0, 2) as i:
                for g in range(2):
                    v.wait_ge(wused[4 * g + 3], i + R_AO + 1)
                    for t in range(NT):
                        m = proj[:, t, ds(i * 1024 + (C_GA + g * 512), 512)]
                        v.tensor_tensor(m, dense_bank[2 * g + t][:, :], m, ALU.mult).then_inc(pair_evac[g], 1)
            for g in range(2):
                v.wait_ge(pair_evac[g], 2 * B_GLU)
            with v.Fori(0, 2) as i:
                for g in range(2):
                    for t in range(NT):
                        v.wait_ge(pair_evac[1], (i * 2 + g) * 2 + (2 * B_GLU + t + 1))
                        v.tensor_tensor(glu_t[:, t, :], dense_bank[t][:, :], glu_sg[:, t, :],
                                        ALU.mult).then_inc(pair_evac[0], 1)
                    v.wait_ge(pair_evac[0], (i * 2 + g) * 2 + (2 * B_GLU + 2))
                    for t in range(NT):
                        gb = proj[:, t, ds(i * 1024 + (C_GB + g * 512), 512)]
                        v.tensor_tensor(glu_t[:, t, :], glu_t[:, t, :], gb, ALU.mult).then_inc(glu_used, 1)
                    v.wait_ge(glu_used, (i * 2 + g) * 2 + 4)
                    for t in range(NT):
                        m = proj[:, t, ds(i * 1024 + (C_GA + g * 512), 512)]
                        st.add(v.tensor_tensor(m, m, glu_t[:, t, :], ALU.add))
                    st.wait()
                st.clear()
            v.sem_inc(merged_ready, 2)

            def add_to_x(r):
                with v.Fori(0, 2) as i:
                    for g in range(2):
                        v.wait_ge(wused[4 * g + 3], i + r + 1)
                        for t in range(NT):
                            xc = x[:, t, ds(i * 1024 + g * 512, 512)]
                            v.tensor_tensor(xc, dense_bank[2 * g + t][:, :], xc, ALU.add).then_inc(pair_evac[g], 1)

            add_to_x(R_WO)
            for g in range(2):
                v.wait_ge(pair_evac[g], 2 * B_PQ)
            v.sem_inc(x_ready, 8)

            def choose(unit, b, base):
                w1, w2 = sub(rW1), sub(rW2)
                val, cand = sub(rV), sub(rCA)
                iu = usub(rIU)
                st.link(v.tensor_copy(w1, kscore[:, ds((unit - base) * 256, 256)]))
                for s in range(2):
                    src, alt = w1[:, s * P:(s + 1) * P], w2[:, s * P:(s + 1) * P]
                    c = 16 * s
                    st.link(v.max(val[:, c:c + 8], src))
                    st.add(v.max_index(iu[:, c:c + 8], val[:, c:c + 8], src))
                    st.link(v.match_replace(alt, val[:, c:c + 8], src, -HUGE))
                    st.link(v.max(val[:, c + 8:c + 16], alt))
                    st.add(v.max_index(iu[:, c + 8:c + 16], val[:, c + 8:c + 16], alt))
                c3 = cand.rearrange("p (a b) -> p a b", a=TOPK)
                st.wait()
                st.link(v.tensor_tensor(c3, val[:, 0:16].unsqueeze(2).broadcast_to([P, 16, 16]),
                                        val[:, 16:32].unsqueeze(1).broadcast_to([P, 16, 16]), ALU.add))
                top = sub(rTP)[:, b * TOPK:(b + 1) * TOPK]
                pos = usub(rPU)
                st.link(v.max(top[:, 0:8], cand))
                st.add(v.max_index(pos[:, 0:8], top[:, 0:8], cand))
                st.link(v.match_replace(sub(rCB), top[:, 0:8], cand, -HUGE))
                st.link(v.max(top[:, 8:16], sub(rCB)))
                v.tensor_scalar(sub(rSS)[:, b:b + 1], top[:, 0:1], -1.0, None, ALU.mult).then_inc(topk_v, 1)
                st.link(v.max_index(pos[:, 8:16], top[:, 8:16], sub(rCB)))
                p2 = usub(rP2)
                st.add(v.tensor_scalar(p2[:, 0:16], pos, 4, None, ALU.logical_shift_right))
                st.add(v.tensor_scalar(p2[:, 16:32], pos, 15, None, ALU.bitwise_and))
                st.link(v.tensor_copy(sub(rIF), iu))
                st.link(v.tensor_copy(sub(rPF), p2))
                for s in range(2):
                    hot = sub((rO1, rO2)[s]).rearrange("p (a b) -> p a b", a=TOPK)
                    st.link(v.tensor_tensor(
                        hot, sub(rPF)[:, 16 * s:16 * s + 16].unsqueeze(2).broadcast_to([P, 16, 16]),
                        iota16.unsqueeze(1).broadcast_to([P, 16, 16]), ALU.is_equal))
                    st.link(v.tensor_tensor(
                        hot, hot, sub(rIF)[:, 16 * s:16 * s + 16].unsqueeze(1).broadcast_to([P, 16, 16]), ALU.mult))
                    st.link(v.tensor_reduce(sub(rIS)[:, 16 * s:16 * s + 16], hot, AX, ALU.add))
                v.scalar_tensor_tensor(usub(rST)[:, b * TOPK:(b + 1) * TOPK], sub(rIS)[:, 0:16], float(NKEY),
                                       sub(rIS)[:, 16:32], ALU.mult, ALU.add).then_inc(stage_ready, 1)
                v.wait_ge(topk_e, unit + 1)
                st.link(v.reciprocal(sub(rSS)[:, 4 + b:5 + b], sub(rSS)[:, 2 + b:3 + b]))
                gt = sub(rGT)[:, b * TOPK:(b + 1) * TOPK]
                st.link(v.tensor_scalar(gt, gt, sub(rSS)[:, 4 + b:5 + b], None, ALU.mult))

            def unit_down(unit, b, t):
                for kk in range(TOPK):
                    slot = kk % SLOTS
                    v.wait_ge(gfull[slot], (unit * GROUNDS + kk // SLOTS) * 16 + 16)
                    v.tensor_tensor_reduce(gslot[:, slot, :], gslot[:, slot, :], h[:, t, :], 1.0, 0.0, ALU.mult,
                                           ALU.add, sub(rAC)[:, b * TOPK + kk:b * TOPK + kk + 1]
                                           ).then_inc(gused[slot], 1)

            def unit_up(unit, b, t):
                v.wait_ge(gelu_ready, unit + 1)
                wt = sub(rWT)[:, b * TOPK:(b + 1) * TOPK]
                st.link(v.tensor_tensor(wt, sub(rGT)[:, b * TOPK:(b + 1) * TOPK],
                                        sub(rGE)[:, b * TOPK:(b + 1) * TOPK], ALU.mult))
                for kk in range(TOPK):
                    slot = kk % SLOTS
                    rnd = unit * GROUNDS + 2 + kk // SLOTS
                    v.wait_ge(gfull[slot], rnd * 16 + 16)
                    if kk:
                        prev = (kk - 1) % SLOTS
                        v.wait_ge(gused[prev], unit * GROUNDS + 2 + (kk - 1) // SLOTS + 2)
                    v.scalar_tensor_tensor(x[:, t, :], gslot[:, slot, :], wt[:, kk:kk + 1], x[:, t, :], ALU.mult,
                                           ALU.add).then_inc(gused[slot], 1)
                v.wait_ge(gused[SLOTS - 1], unit * GROUNDS + 5)
                v.sem_inc(turn_over, 1)

            def peer_units(layer):
                base = layer * UNITS
                v.wait_ge(sk_evac, 8 * (layer + 1))
                choose(base, 0, base)
                st.clear()
                for t in range(NT):
                    pairs = PH // 2 - (t == NT - 1)
                    first = base + t * PH
                    with v.Fori(0, pairs) as i:
                        for b in range(2):
                            unit = i * 2 + (first + b)
                            unit_down(unit, b, t)
                            choose(unit + 1, 1 - b, base)
                            unit_up(unit, b, t)
                        st.clear()
                last = base + UNITS - 2
                unit_down(last, 0, NT - 1)
                choose(last + 1, 1, base)
                unit_up(last, 0, NT - 1)
                unit_down(last + 1, 1, NT - 1)
                unit_up(last + 1, 1, NT - 1)

            norm(1)
            peer_units(0)
            v.sem_inc(x_ready, 8)

            norm(2)
            v.wait_ge(rope_loaded, 16 * 5)
            v.wait_ge(inv_ready, 1)
            st.link(v.tensor_copy(pos_f, pos_i))
            a0, a1, n0 = ang[:, 0], ang[:, 1], rnd[:, 0]
            for t in range(NT):
                st.add(v.tensor_scalar(a0[:, t, :], inv_freq, pos_f[:, t:t + 1], None, ALU.mult))
            st.wait()
            st.link(v.tensor_scalar(n0, a0, float(1 / (2 * np.pi)), None, ALU.mult))
            st.link(v.tensor_scalar(n0, n0, ROUND, -ROUND, ALU.add, ALU.add))
            for part in (PI_A, PI_B, PI_C):
                st.link(v.scalar_tensor_tensor(a0, n0, -part, a0, ALU.mult, ALU.add))
            st.link(v.tensor_scalar(a0, a0, float(1 / (2 * np.pi)), None, ALU.mult))
            st.link(v.tensor_scalar(a1, a0, 0.25, None, ALU.add))
            st.link(v.tensor_scalar(rnd, ang, ROUND, -ROUND, ALU.add, ALU.add))
            v.tensor_tensor(ang, ang, rnd, ALU.subtract).then_inc(ang_ready, 1)
            v.wait_ge(par_t, 1)
            v.tensor_copy(par[:, 0:80], mb[0][:, 0:80]).then_inc(par_ready, 1)
            v.wait_ge(lam_act, 2)
            e_, z_ = lp[:, 8:16], lp[:, 16:24]
            st.link(v.tensor_scalar(z_, e_, 2.0, None, ALU.add))
            st.link(v.reciprocal(z_, z_))
            st.link(v.tensor_tensor(z_, z_, e_, ALU.mult))
            st.link(v.tensor_tensor(lp[:, 0:8], z_, z_, ALU.mult))
            st.link(v.tensor_scalar(neg_c, lp[:, 0:8], 1 / 17, 1 / 15, ALU.mult, ALU.add))
            for odd in (13, 11, 9, 7, 5, 3, 1):
                st.link(v.tensor_tensor(neg_c, neg_c, lp[:, 0:8], ALU.mult))
                st.link(v.tensor_scalar(neg_c, neg_c, 1 / odd, None, ALU.add))
            st.link(v.scalar_tensor_tensor(neg_c, neg_c, 2.0, z_, ALU.mult, ALU.mult))
            st.link(v.tensor_scalar(e_, lam, -1.0, 0.0, ALU.mult, ALU.max))
            st.link(v.tensor_tensor(neg_c, neg_c, e_, ALU.add))
            v.tensor_scalar(neg_c, neg_c, -LRU_C, None, ALU.mult).then_inc(lam_dve, 1)
            for g in range(2):
                v.wait_ge(pair_evac[g], 2 * B_IN2 + 2)
            junk = big[:, 12928:13440]
            for t in range(NT):
                for g, (lo, hi) in enumerate(((0, Q_LORA), (Q_LORA, Q_LORA + KV_LORA))):
                    n = hi - lo
                    st.link(v.tensor_tensor_reduce(junk[:, 0:n], c2[:, t, lo:hi], c2[:, t, lo:hi], 1.0, 0.0,
                                                   ALU.mult, ALU.add, stat[:, 12 + 2 * t + g:13 + 2 * t + g]))
                    ins = v.tensor_scalar(stat[:, 16 + 2 * t + g:17 + 2 * t + g],
                                          stat[:, 12 + 2 * t + g:13 + 2 * t + g], 1.0 / n, EPS, ALU.mult, ALU.add)
                    if t == 1 and g == 1:
                        ins.then_inc(c_msq, 1)
                    else:
                        st.link(ins)
            v.wait_ge(c_rms, 1)
            st.link(v.reciprocal(stat[:, 12:16], stat[:, 20:24]))
            for t in range(NT):
                for g, (lo, hi) in enumerate(((0, Q_LORA), (Q_LORA, Q_LORA + KV_LORA))):
                    st.add(v.scalar_tensor_tensor(c2[:, t, lo:hi], c2[:, t, lo:hi],
                                                  stat[:, 12 + 2 * t + g:13 + 2 * t + g], (g_cq, g_ckv)[g],
                                                  ALU.mult, ALU.mult))
            st.wait()
            v.sem_inc(c_ready, 1)
            for g in range(2):
                v.wait_ge(pair_evac[g], 2 * B_IN2 + 4)
            for k in range(8):
                st.add(v.tensor_scalar(xcT[:, k, :], xrT[:, k, :], conv_w[:, 24 + k:25 + k], conv_b[:, k:k + 1],
                                       ALU.mult, ALU.add))
            for j in (2, 1, 0):
                back = CONV - 1 - j
                for k in range(8):
                    st.wait(st.n - 7)
                    st.add(v.scalar_tensor_tensor(xcT[:, k, back:T], xrT[:, k, 0:T - back],
                                                  conv_w[:, 8 * j + k:8 * j + k + 1], xcT[:, k, back:T],
                                                  ALU.mult, ALU.add))
            st.wait()
            v.sem_inc(xc_ready, 1)
            v.wait_ge(lru_act, 16)
            st.link(v.tensor_tensor(sq_g, rr_g, rr_g, ALU.mult))
            v.scalar_tensor_tensor(th_g, sq_g, 1.0, th_g, ALU.add, ALU.mult).then_inc(lru_dve, 1)
            st.link(v.tensor_tensor(ii_g, ii_g, hs[:, 2048:4096], ALU.mult))
            v.wait_ge(lru_act, 18)
            st.link(v.tensor_tensor(ii_g, ii_g, th_g, ALU.mult))
            for k in range(8):
                st.add(v.tensor_tensor_scan(k3(th_g)[:, k, :], k3(rr_g)[:, k, :], k3(ii_g)[:, k, :], 0.0,
                                            ALU.mult, ALU.add))
            st.wait()
            st.link(v.tensor_tensor(ht[:, 2048:4096], th_g, big[:, 3712:5760], ALU.mult))

            v.wait_ge(pair_evac[0], 2 * B_WO2)
            v.wait_ge(pair_evac[1], 2 * B_WO2)
            q2f = big[:, 5760:8832]
            rope_k = c2[:, :, Q_LORA + KV_LORA:W_C]
            st.add(v.tensor_tensor(krr, rope_k, rope_k, ALU.mult))
            st.link(v.tensor_tensor(krg, rope_k, g_kh[:, NOPE:QKD].unsqueeze(1).broadcast_to([P, NT, ROPE]), ALU.mult))
            st.link(v.tensor_tensor(qk2_sq, q2f, q2f, ALU.mult))
            st.link(v.tensor_reduce(msq2[:, 0:16], qk2_sq.rearrange("p (r c) -> p r c", c=QKD), AX, ALU.add))
            kn_raw = kv2[:, :, :, 0:NOPE]
            sq4 = qk2_sq[:, 0:2048].rearrange("p (t h c) -> p t h c", t=NT, h=NH2)
            st.link(v.tensor_tensor(sq4, kn_raw, kn_raw, ALU.mult))
            st.add(v.tensor_reduce(msq2[:, 16:32], qk2_sq[:, 0:2048].rearrange("p (r c) -> p r c", c=NOPE), AX, ALU.add))
            st.link(v.tensor_reduce(msq2[:, 32:34], krr, AX, ALU.add))
            mk = msq2[:, 16:32].rearrange("p (t h) -> p t h", t=NT)
            st.link(v.tensor_tensor(mk, mk, msq2[:, 32:34].unsqueeze(2).broadcast_to([P, NT, NH2]), ALU.add))
            v.tensor_scalar(msq2[:, 0:32], msq2[:, 0:32], 1.0 / QKD, EPS, ALU.mult, ALU.add).then_inc(qk2_msq, 1)
            v.wait_ge(qk2_rms, 1)
            st.add(v.tensor_scalar(g_qh, g_qh, float(QKD ** -0.5), None, ALU.mult))
            st.link(v.reciprocal(rs2, rms2))
            q_rows = q2.rearrange("p t h c -> p (t h) c")
            st.link(v.tensor_tensor(q_rows, q_rows, rs2[:, 0:16].unsqueeze(2).broadcast_to([P, 16, QKD]), ALU.mult))
            kn_rows = kn2.rearrange("p t h c -> p (t h) c")
            kn_src = kn_raw.rearrange("p t h c -> p (t h) c")
            st.link(v.tensor_tensor(kn_rows, kn_src, rs2[:, 16:32].unsqueeze(2).broadcast_to([P, 16, NOPE]), ALU.mult))
            st.add(v.tensor_tensor(q_rows, q_rows, g_qh.unsqueeze(1).broadcast_to([P, 16, QKD]), ALU.mult))
            st.link(v.tensor_tensor(kn_rows, kn_rows, g_kh[:, 0:NOPE].unsqueeze(1).broadcast_to([P, 16, NOPE]), ALU.mult))
            v.wait_ge(trig_ready, 1)
            half = ROPE // 2
            sin4, cos4 = (trig[:, i].unsqueeze(2).broadcast_to([P, NT, NH2, half]) for i in range(2))
            t1, t2 = q2[:, :, :, NOPE:NOPE + half], q2[:, :, :, NOPE + half:QKD]
            for (p, q_, op, lo) in ((t1, t2, ALU.subtract, 0), (t2, t1, ALU.add, half)):
                st.add(v.tensor_tensor(rope_t[:, 0], p, cos4, ALU.mult))
                st.link(v.tensor_tensor(rope_t[:, 1], q_, sin4, ALU.mult))
                st.link(v.tensor_tensor(qr2[:, :, :, lo:lo + half], rope_t[:, 0], rope_t[:, 1], op))
            k1, k2 = krg[:, :, 0:half], krg[:, :, half:ROPE]
            u0, u1 = (big[:, 4736 + 64 * i:4736 + 64 * (i + 1)].rearrange("p (t c) -> p t c", t=NT) for i in range(2))
            for (p, q_, op, lo) in ((k1, k2, ALU.subtract, 0), (k2, k1, ALU.add, half)):
                st.add(v.tensor_tensor(u0, p, trig[:, 1], ALU.mult))
                st.link(v.tensor_tensor(u1, q_, trig[:, 0], ALU.mult))
                st.link(v.tensor_tensor(krr[:, :, lo:lo + half], u0, u1, op))
            v.tensor_tensor(krh, krr.unsqueeze(2).broadcast_to([P, NT, NH2, ROPE]),
                            rs2[:, 16:32].rearrange("p (t h) -> p t h", t=NT).unsqueeze(3)
                            .broadcast_to([P, NT, NH2, ROPE]), ALU.mult).then_inc(qk2_ready, 1)
            v.wait_ge(causal_ready, 1)
            v.sem_inc(nm2_ready, 2)
            v.sem_inc(o2_evac, 2)
            st.clear()
            with v.Fori(0, NH2) as j:
                for t in range(NT):
                    n = (t + 1) * P
                    v.wait_ge(s2_done, j * 2 + t + 1)
                    if t == 1:
                        st.add(v.tensor_copy(prob2[:, 1, 0:P], mb[1][:, 0:P]))
                    st.link(v.tensor_tensor(prob2[:, t, t * P:n], mb[t][:, t * P:n], causal[:, 0:P], ALU.add))
                    v.tensor_reduce(att[:, t:t + 1], prob2[:, t, 0:n], AX, ALU.max, negate=True).then_inc(nm2_ready, 1)
                for t in range(NT):
                    n = (t + 1) * P
                    v.wait_ge(p2_exp, j * 2 + t + 1)
                    st.link(v.reciprocal(att[:, 4 + t:5 + t], att[:, 2 + t:3 + t]))
                    v.tensor_scalar(prob2[:, t, 0:n], prob2[:, t, 0:n], att[:, 4 + t:5 + t], None,
                                    ALU.mult).then_inc(p2_ready, 1)
                for t in range(NT):
                    v.wait_ge(o2_done, j * 2 + t + 3)
                    v.tensor_copy(hT[:, ds(j, 1), t * P:(t + 1) * P].rearrange("p a n -> p (a n)"),
                                  dense_bank[t][:, 0:P]).then_inc(o2_evac, 1)
                st.clear()
            v.wait_ge(o2_evac, 2 * NH2 + 2)
            v.tensor_tensor(osq, hT, hT, ALU.mult).then_inc(osq_ready, 1)
            v.wait_ge(osq_ready, 1)
            v.tensor_tensor(hT, hT, g_mix.unsqueeze(2).broadcast_to([P, KD, T]), ALU.mult).then_inc(mixed_ready, 1)
            v.wait_ge(oss_done, 1)
            v.tensor_scalar(stat[:, 24:28], mb[0][:, 0:4], 1.0 / REC, EPS, ALU.mult, ALU.add).then_inc(oss_done, 1)
            v.wait_ge(oss_rms, 1)
            st.link(v.reciprocal(stat[:, 24:28], stat[:, 28:32]))
            with v.Fori(0, 2) as i:
                for g in range(2):
                    for br in range(2):
                        v.wait_ge(wused[4 * g + 2 * br + 1], i + R_WO2 + 1)
                        for t in range(NT):
                            xc = x[:, t, ds(i * 1024 + g * 512, 512)]
                            if br:
                                v.wait_ge(pair_evac[0], (i * 2 + g) * 2 + (2 * B_WO2 + t + 1))
                            v.scalar_tensor_tensor(xc, dense_bank[2 * br + t][:, :],
                                                   stat[:, 24 + 2 * t + br:25 + 2 * t + br], xc, ALU.mult,
                                                   ALU.add).then_inc(pair_evac[br], 1)
            for g in range(2):
                v.wait_ge(pair_evac[g], 2 * B_PQ2)
            v.sem_inc(x_ready, 8)
            norm(3)
            peer_units(1)


def kernel(**inputs):
    import concourse.bacc as _bacc
    from concourse.bass_utils import run_bass_kernel_spmd

    nc = _bacc.Bacc("TRN2", target_bir_lowering=False, num_devices=1)
    arrays = {"in_" + name: np.asarray(value) for name, value in inputs.items()}
    ins = {name: nc.dram_tensor("in_" + name, arrays["in_" + name].shape,
                                mybir.dt.from_np(arrays["in_" + name].dtype), kind="ExternalInput").ap()
           for name in inputs}
    y = nc.dram_tensor("out0", (1, T, D), F32, kind="ExternalOutput").ap()
    two_blocks(nc, ins, y)
    nc.compile()
    got = run_bass_kernel_spmd(nc, [arrays], core_ids=[0]).results
    return np.asarray(got[0]["out0"])
```

```python
from contextlib import ExitStack

import numpy as np

import concourse.bass as bass
from concourse import mybir

F32 = mybir.dt.float32
I32 = mybir.dt.int32
U32 = mybir.dt.uint32
ALU = mybir.AluOpType
ACT = mybir.ActivationFunctionType
AX = mybir.AxisListType.X
ds = bass.ds

P = 128
T = 256
NT = T // P
D = 2048
KD = D // P
SLOTS = 8
SLOT = 2048
KS = 4
EPS = 1e-6
ROUND = 12582912.0
TWO_PI_BELOW = float(np.nextafter(np.float32(2 * np.pi), np.float32(0)))
HUGE = 1e30

NQ, NKV, HD, WINDOW = 16, 4, 128, 128
GQ = NQ // NKV
SSM_W = 1024
SSM_K = SSM_W // P
PAIRS = 4
NKEY, TOPK, PH = 128, 16, 8
UNITS = NT * PH
GROUNDS = 2 * TOPK // SLOTS

Q_LORA, KV_LORA, ROPE, NH2 = 512, 256, 64, 8
NOPE = 128
QKD = NOPE + ROPE
W_C = Q_LORA + KV_LORA + ROPE
REC = 1024
CONV = 4
LRU_C = 8.0
ROPE_THETA = 10000.0
PI_A, PI_B = 6.28125, 0.0019340515136718750
PI_C = float(2 * np.pi - PI_A - PI_B)

R_U, R_QKV, R_GATE, R_GLU, R_AO, R_WO, R_PQ = 0, 1, 4, 8, 10, 12, 14
R_IN2, R_MID, R_WO2, R_PQ2 = 16, 19, 20, 22
B_U, B_QKV, B_GLU, B_AO, B_WO, B_PQ = 0, 1, 8, 12, 14, 16
B_IN2, B_UQ, B_WO2, B_PQ2 = 18, 21, 25, 29
BC = 128


class Steps:

    def __init__(self, eng, sem):
        self.eng, self.sem, self.n = eng, sem, 0

    def add(self, ins):
        ins.then_inc(self.sem, 1)
        self.n += 1
        return self.n

    def wait(self, upto=None):
        upto = self.n if upto is None else upto
        if upto:
            self.eng.wait_ge(self.sem, upto)

    def link(self, ins):
        self.add(ins)
        self.wait()

    def clear(self):
        self.wait()
        self.eng.sem_clear(self.sem)
        self.n = 0


def two_blocks(nc, a, out):
    ctx = ExitStack()
    with ctx:
        def sb(name, cols, dt=F32):
            return ctx.enter_context(nc.sbuf_tensor(name, [P, cols], dt))

        def sem(name):
            return ctx.enter_context(nc.semaphore(name))

        wring = sb("wring", SLOTS * SLOT)
        big = sb("big", SLOTS * SLOT)
        xs = sb("xs", NT * D)
        hs = sb("hs", NT * D)
        ht = sb("ht", KD * T)
        sc = sb("sc", 7168)
        cn = sb("cn", 860)

        wslot = wring[:, :].rearrange("p (s c) -> p s c", s=SLOTS)
        gslot = big[:, :].rearrange("p (s c) -> p s c", s=SLOTS)
        x = xs[:, :].rearrange("p (t c) -> p t c", t=NT)
        h = hs[:, :].rearrange("p (t c) -> p t c", t=NT)
        hT = ht[:, :].rearrange("p (k n) -> p k n", k=KD)
        uT = hs[:, 0:2048].rearrange("p (k n) -> p k n", k=SSM_K)
        yT = hs[:, 2048:4096].rearrange("p (k n) -> p k n", k=SSM_K)
        proj = big[:, 0:14336].rearrange("p (t c) -> p t c", t=NT)
        C_K, C_V, C_GA, C_GB = 2048, 2560, 3072, 5120

        ident = cn[:, 0:128]
        iota_t = cn[:, 128:384]
        mask_b = cn[:, 384:416].rearrange("p (q b) -> p q b", q=PAIRS)
        mask_c = cn[:, 416:544]
        quarter = cn[:, 544:546]
        nslope = cn[:, 546:562]
        sink = cn[:, 562:578]
        nsink = cn[:, 578:594]
        ssm_d = cn[:, 594:602]
        stat = cn[:, 602:634]
        iota16 = cn[:, 128:144]
        ones_c = cn[:, 636:637]
        par = cn[:, 640:752]

        psum = [ctx.enter_context(nc.psum_tensor(f"bank{i}", [P, 512], F32)) for i in range(8)]
        dense_bank = psum[0:4]
        tb = psum[4:6]
        mb = psum[6:8]

        x_loaded = sem("x_loaded")
        small_loaded = sem("small_loaded")
        wfull = [sem(f"wfull{b}") for b in range(SLOTS)]
        wused = [sem(f"wused{b}") for b in range(SLOTS)]
        pair_evac = [sem(f"pair_evac{g}") for g in range(2)]
        consts_ready = sem("consts_ready")
        gain_loaded = sem("gain_loaded")
        msq_ready = sem("msq_ready")
        rms_ready = sem("rms_ready")
        h_ready = sem("h_ready")
        tb_filled = sem("tb_filled")
        tb_evac = sem("tb_evac")
        dve = sem("dve_steps")
        acs = sem("act_steps")
        pls = sem("pool_steps")
        ssm_loaded = sem("ssm_loaded")
        sp_in = sem("ssm_param_dve")
        sp_act = sem("ssm_param_act")
        sp_t = sem("ssm_param_transposed")
        sp_done = sem("ssm_param_done")
        bc_loaded = sem("bc_loaded")
        ct_done = sem("ct_transposed")
        ct_evac = sem("ct_evacuated")
        bpad_ready = sem("bpad_ready")
        bt_done = sem("bt_transposed")
        bt_evac = sem("bt_evacuated")
        bu_done = sem("bu_done")
        bu_used = sem("bu_used")
        f_ready = sem("phase_ready")
        e_ready = sem("rotation_ready")
        de_ready = sem("states_ready")
        y_done = sem("y_done")
        y_evac = sem("y_evacuated")
        y_act = sem("y_activated")
        dist_ready = sem("dist_ready")
        qk_copied = sem("qk_copied")
        qk_msq = sem("qk_msq")
        qk_rms = sem("qk_rms")
        qk_ready = sem("qk_ready")
        qk_t = sem("qk_transposed")
        qk_tevac = sem("qk_t_evacuated")
        s_done = sem("scores_done")
        nmax_ready = sem("nmax_ready")
        p_exp = sem("p_exp")
        p_ready = sem("p_ready")
        pt_done = sem("p_transposed")
        pt_evac = sem("pt_evacuated")
        o_done = sem("o_done")
        o_evac = sem("o_evacuated")
        gate_sig = sem("gates_sigmoid")
        merged_ready = sem("merged_ready")
        glu_used = sem("glu_used")
        x_ready = sem("x_ready")
        keys_loaded = sem("keys_loaded")
        keys_t = sem("keys_transposed")
        keys_evac = sem("keys_evacuated")
        sk_done = sem("key_scores_done")
        sk_evac = sem("key_scores_evacuated")
        topk_v = sem("topk_values")
        topk_e = sem("topk_exp")
        stage_ready = sem("indices_ready")
        gfull = [sem(f"gfull{b}") for b in range(SLOTS)]
        gused = [sem(f"gused{b}") for b in range(SLOTS)]
        gathers_issued = sem("gathers_issued")
        gelu_ready = sem("gelu_ready")
        out_done = sem("out_done")
        par_loaded = sem("par_loaded")
        par_t = sem("par_transposed")
        par_ready = sem("par_ready")
        rope_loaded = sem("rope_loaded")
        inv_ready = sem("inv_freq_ready")
        ang_ready = sem("angles_ready")
        trig_ready = sem("trig_ready")
        c_msq = sem("latent_msq")
        c_rms = sem("latent_rms")
        c_ready = sem("latents_normed")
        gates_loaded = sem("gates_loaded")
        xc_ready = sem("conv_ready")
        gate_mm = sem("gate_products")
        gate_act = sem("gates_activated")
        lru_act = sem("lru_activated")
        lru_dve = sem("lru_elementwise")
        lam_act = sem("lambda_exp")
        lam_dve = sem("lambda_decay")
        qk2_msq = sem("qk2_msq")
        qk2_rms = sem("qk2_rms")
        qk2_ready = sem("qk2_ready")
        causal_ready = sem("causal_ready")
        hd_copied = sem("head_copied")
        hd_t = sem("head_transposed")
        hd_tevac = sem("head_t_evacuated")
        s2_done = sem("scores2_done")
        nm2_ready = sem("nmax2_ready")
        p2_exp = sem("p2_exp")
        p2_ready = sem("p2_ready")
        pt2_done = sem("p2_transposed")
        pt2_evac = sem("p2t_evacuated")
        o2_done = sem("o2_done")
        o2_evac = sem("o2_evacuated")
        sq_ready = sem("branch_squared")
        sums_done = sem("branch_sums")
        branch_rms = sem("branch_rms")
        mixed_ready = sem("branch_gained")
        turn_over = sem("turn_over")

        gain = sc[:, 0:D]

        def cut(base, sizes):
            at, res = base, []
            for n in sizes:
                res.append((at, at + n))
                at += n
            return res

        (rA, rB, rZI, rZ, rD, rE, rF, rR, rBP, rBT, rCT, rCP, rPR) = cut(
            0, [512] * 8 + [512, 512, 512, 512, 256])
        two = lambda r: sc[:, r[0]:r[1]].rearrange("p (c n) -> p c n", c=2)
        bre_e, bim_e, z_in, z_out, zr_e, zi_e, phase, whole = map(two, (rA, rB, rZI, rZ, rD, rE, rF, rR))
        b_pad = sc[:, rBP[0]:rBP[1]].rearrange("p (i a b c) -> p i a b c", i=2, a=2, b=8)
        b_t = sc[:, rBT[0]:rBT[1]].rearrange("p (i a n) -> p i a n", i=2, a=2)
        c_t = sc[:, rCT[0]:rCT[1]].rearrange("p (d a n) -> p d a n", d=2, a=2)
        c_p = sc[:, rCP[0]:rCP[1]].rearrange("p (j d q c) -> p j d q c", j=2, d=2, q=PAIRS)
        prm = sc[:, rPR[0]:rPR[1]].rearrange("p (j n) -> p j n", j=4)
        b_st = big[:, 14336:14592].rearrange("p (a d q c) -> p a d q c", a=2, d=2, q=PAIRS)
        c_st = big[:, 14592:15104].rearrange("p (d a u n) -> p d a u n", d=2, a=2, u=2)
        rot = big[:, 15104:16128].rearrange("p (i c n) -> p i c n", i=2, c=2)
        pw = [sc[0:64, i * 128:(i + 1) * 128] for i in range(14)]
        step2 = sc[0:64, 1800:1802]

        (rQK, rSQ, rGQ, rQT, rVN, rDI, rS, rPT, rSM) = cut(0, [1280, 1280, 640, 1280, 256, 512, 768, 512, 64])
        qk = sc[:, rQK[0]:rQK[1]].rearrange("p (t j c) -> p t j c", t=NT, j=GQ + 1)
        qk_sq = sc[:, rSQ[0]:rSQ[1]]
        g_qk = sc[:, rGQ[0]:rGQ[1]].rearrange("p (j c) -> p j c", j=GQ + 1)
        qkT = sc[:, rQT[0]:rQT[1]].rearrange("p (j n) -> p j n", j=GQ + 1)
        v_sb = sc[:, rVN[0]:rVN[1]].rearrange("p (t c) -> p t c", t=NT)
        dist = sc[:, rDI[0]:rDI[1]].rearrange("p (t n) -> p t n", t=NT)
        NB = 3
        prob = sc[:, rS[0]:rS[1]].rearrange("p (i n) -> p i n", i=NB)
        probT = sc[:, rPT[0]:rPT[1]].rearrange("p (i k n) -> p i k n", i=2, k=NT)
        sm = sc[:, rSM[0]:rSM[1]]
        nmax_u, sum_u, sink_u = ([sm[:, 20 + NB * n + i:21 + NB * n + i] for i in range(NB)] for n in range(3))
        glu_sg = big[:, 14336:15360].rearrange("p (t c) -> p t c", t=NT)
        q_bank, k_bank, pt_bank, o_bank = tb, mb[0], tb[0], tb[1]
        UA = NT * GQ

        pqT = big[:, 0:4096].rearrange("p (k n) -> p k n", k=KD)
        key_n = big[:, 4096:6144].rearrange("p (h s c) -> p h s c", h=PH, s=2)
        keyT = big[:, 6144:8192].rearrange("p (j c) -> p j c", j=KD)
        kscore = ht[:, :]
        (rW1, rW2, rCA, rCB, rO1, rO2, rV, rIF, rTP, rPF, rIS, rAC, rGE, rWT, rGT, rSS) = cut(
            0, [256, 256, 256, 256, 256, 256, 32, 32, 32, 32, 32, 32, 32, 32, 32, 8])
        sub = lambda r: sc[:, r[0]:r[1]]
        usub = lambda r: sc[:, r[0]:r[1]].bitcast(U32)
        rIU, rPU, rP2, rST = cut(3000, [32, 16, 32, 32])

        c2 = big[:, 0:2 * W_C].rearrange("p (t c) -> p t c", t=NT)
        xrT = big[:, 1664:3712].rearrange("p (k n) -> p k n", k=8)
        ygT = big[:, 3712:5760].rearrange("p (k n) -> p k n", k=8)
        q2 = big[:, 5760:8832].rearrange("p (t h c) -> p t h c", t=NT, h=NH2)
        kv2 = big[:, 8832:12928].rearrange("p (t h c) -> p t h c", t=NT, h=NH2)
        cT = big[:, 12928:14464].rearrange("p (k n) -> p k n", k=6)
        g_cq, g_ckv = big[:, 14464:14976], big[:, 14976:15232]
        g_qh, g_kh = big[:, 15232:15424], big[:, 15424:15616]
        pos_f, inv_freq = big[:, 15616:15618], big[:, 15618:15650]
        ang = big[:, 15650:15778].rearrange("p (j t c) -> p j t c", j=2, t=NT)
        rnd = big[:, 15778:15906].rearrange("p (j t c) -> p j t c", j=2, t=NT)
        trig = big[:, 15906:16034].rearrange("p (j t c) -> p j t c", j=2, t=NT)
        krr = big[:, 16034:16162].rearrange("p (t c) -> p t c", t=NT)
        krg = big[:, 16162:16290].rearrange("p (t c) -> p t c", t=NT)
        pos_i = big[:, 16290:16292].bitcast(I32)
        w_gates = hs[:, 0:2048].rearrange("p (g h j) -> p g h j", g=2, h=NH2)
        xcT = hs[:, 2048:4096].rearrange("p (k n) -> p k n", k=8)
        th_g, rr_g, ii_g = (sc[:, 2048 * i:2048 * (i + 1)] for i in range(3))
        k3 = lambda t: t.rearrange("p (k n) -> p k n", k=8)
        sq_g = big[:, 8832:10880]
        par_rows = sc[0:80, 6144:6272]
        conv_w, conv_b, b_rg, b_ig, lam, g_mix = (par[:, lo:hi] for lo, hi in (
            (0, 32), (32, 40), (40, 48), (48, 56), (56, 64), (64, 80)))
        neg_c, lp = par[:, 80:88], par[:, 88:112]
        kn2 = sc[:, 0:2048].rearrange("p (t h c) -> p t h c", t=NT, h=NH2)
        krh = sc[:, 2048:3072].rearrange("p (t h c) -> p t h c", t=NT, h=NH2)
        qr2 = sc[:, 3072:4096].rearrange("p (t h c) -> p t h c", t=NT, h=NH2)
        qk2_sq = big[:, 1664:1664 + 3072]
        rope_t = big[:, 1664:1664 + 1024].rearrange("p (i t h c) -> p i t h c", i=2, t=NT, h=NH2)
        heads = (sc[:, 4096:6144], big[:, 1664:3712])
        head_n = [w[:, 0:512].rearrange("p (j t c) -> p j t c", j=2, t=NT) for w in heads]
        head_r = [w[:, 512:768].rearrange("p (j t c) -> p j t c", j=2, t=NT) for w in heads]
        head_v = [w[:, 768:1024].rearrange("p (t c) -> p t c", t=NT) for w in heads]
        headT_n = [w[:, 1024:1536].rearrange("p (j n) -> p j n", j=2) for w in heads]
        headT_r = [w[0:64, 1536:2048].rearrange("p (j n) -> p j n", j=2) for w in heads]
        W_S = 3 * P
        tile_keys = ((0, P), (P, W_S))
        prob2 = (sc[:, 6144:6144 + W_S], sc[:, 6656:6656 + W_S])
        prob2T = (big[:, 3712:3712 + W_S], big[:, 4224:4224 + W_S])
        causal = big[:, 0:W_S]
        sm2 = big[:, W_S:512]
        msq2, rms2, rs2 = sm2[:, 0:34], sm2[:, 34:66], sm2[:, 66:98]
        att = [[sm2[:, 98 + 6 * e + 2 * n:100 + 6 * e + 2 * n] for n in range(3)] for e in range(2)]
        rec_sq, att_sq = hs[:, 0:2048], big[:, 5760:5760 + 2048]
        recT, attT = ht[:, 2048:4096], ht[:, 0:2048]

        w_in2 = a["w_in_2"][0].rearrange("(k p) n -> p k n", p=P)
        w_uq = a["w_uq_2"][0].rearrange("(k p) n -> p k n", p=P)
        w_ukv = a["w_ukv_2"][0].rearrange("(k p) n -> p k n", p=P)
        w_out2 = a["w_out_2"][0].rearrange("(k p) n -> p k n", p=P)
        w_pq2 = a["peer_w_q_2"][0].rearrange("(k p) n -> p k n", p=P)
        w_in = a["w_in"][0].rearrange("(k p) n -> p k n", p=P)
        w_ao = a["w_attn_o"][0].rearrange("(k p) n -> p k n", p=P)
        w_ga = a["glu_w_a"][0].rearrange("(k p) n -> p k n", p=P)
        w_gb = a["glu_w_b"][0].rearrange("(k p) n -> p k n", p=P)
        w_out = a["w_out"][0].rearrange("(k p) n -> p k n", p=P)
        w_pq = a["peer_w_query"][0].rearrange("(k p) n -> p k n", p=P)

        block = ctx.enter_context(nc.Block())

        @block.sync
        def _(sp):
            def fill(b, src, r):
                if not (isinstance(r, int) and r == 0):
                    sp.wait_ge(wused[b], r)
                n = src.shape[1] * src.shape[2]
                dst = wslot[:, b, 0:n].rearrange("p (k n) -> p k n", k=src.shape[1])
                sp.dma_start(dst, src).then_inc(wfull[b], 16)

            def fill_round(w, r, col):
                for b in range(SLOTS):
                    k = (b % 4) * KS
                    fill(b, w[:, k:k + KS, ds(col + (b // 4) * 512, 512)], r)

            for t in range(NT):
                sp.dma_start(x[:, t, :], a["x"][0, t * P:(t + 1) * P, :]).then_inc(x_loaded, 16)
            fill_round(w_in, R_U, 3072)
            with sp.Fori(0, 3) as i:
                fill_round(w_in, i + R_QKV, i * 1024)
            with sp.Fori(0, 4) as i:
                fill_round(w_in, i + R_GATE, i * 1024 + 4096)
            with sp.Fori(0, 2) as i:
                for b in range(SLOTS):
                    w = w_ga if b % 4 < 2 else w_gb
                    k = (b % 2) * KS
                    fill(b, w[:, k:k + KS, ds(i * 1024 + (b // 4) * 512, 512)], i + R_GLU)
            with sp.Fori(0, 2) as i:
                fill_round(w_ao, i + R_AO, i * 1024)
            with sp.Fori(0, 2) as i:
                fill_round(w_out, i + R_WO, i * 1024)
            with sp.Fori(0, 2) as i:
                fill_round(w_pq, i + R_PQ, i * 1024)

            for r in range(3):
                for b in range(SLOTS):
                    k, g = (b % 4) * KS, b // 4
                    lo, hi = ((0, 512), (512, W_C))[g] if r == 0 else (W_C + (2 * r - 2 + g) * 512,
                                                                     W_C + (2 * r - 1 + g) * 512)
                    fill(b, w_in2[:, k:k + KS, lo:hi], R_IN2 + r)
            for b in range(3):
                fill(b, w_uq[:, :, b * 512:(b + 1) * 512], R_MID)
            for b in range(4):
                fill(3 + b, w_ukv[:, :, b * 512:(b + 1) * 512], R_MID)
            sp.wait_ge(wused[7], R_MID)
            sp.sem_inc(wfull[7], 16)
            for r, k0 in ((0, 8), (1, 0)):
                for b in range(SLOTS):
                    k = k0 + (b % 2) * KS
                    fill(b, w_out2[:, k:k + KS, (b // 2) * 512:(b // 2 + 1) * 512], R_WO2 + r)
            with sp.Fori(0, 2) as i:
                fill_round(w_pq2, i + R_PQ2, i * 1024)
            for t in range(NT):
                sp.wait_ge(gused[7], (UNITS + (t + 1) * PH) * GROUNDS + 1)
                sp.dma_start(out[0, t * P:(t + 1) * P, :], x[:, t, :]).then_inc(out_done, 16)
            sp.wait_ge(out_done, 16 * NT)

        @block.gpsimd
        def _(pool):
            st = Steps(pool, pls)
            st.add(pool.memset(ident, 0.0))
            st.add(pool.memset(cn[:, 384:546], 0.0))
            st.add(pool.memset(ones_c, 1.0))
            st.wait()
            st.add(pool.affine_select(out=ident, in_=ident, compare_op=ALU.not_equal, fill=1.0, base=0,
                                      pattern=[[-1, P]], channel_multiplier=1))
            st.link(pool.iota(iota_t, pattern=[[1, T]], base=0, channel_multiplier=0,
                             allow_small_or_imprecise_dtypes=True))
            for half in range(2):
                rows = slice(64 * half, 64 * half + 64)
                for q in range(PAIRS):
                    st.link(pool.memset(mask_b[rows, q, 2 * q + half:2 * q + half + 1], 1.0))
                of_half = mask_c[rows, :].rearrange("p (q f c) -> p q f c", q=PAIRS, f=2)[:, :, half, :]
                st.link(pool.memset(of_half, 1.0))
            st.add(pool.memset(quarter[:, 1:2], 0.25))
            for i in range(NQ):
                st.add(pool.memset(nslope[:, i:i + 1], -float(2.0 ** (-8.0 * (i + 1) / NQ))))
            st.wait()
            pool.sem_inc(consts_ready, 1)

            with pool.Fori(0, SSM_K) as k:
                pool.wait_ge(bc_loaded, k * BC + BC)
                for s in range(8):
                    q, d = s // 2, s % 2
                    pool.wait_ge(bt_done, k * 8 + s + 1)
                    pool.tensor_tensor(
                        b_pad[:, s % 2], b_st[:, :, d, q, :].unsqueeze(2).broadcast_to([P, 2, 8, 16]),
                        mask_b[:, q, :].unsqueeze(1).unsqueeze(3).broadcast_to([P, 2, 8, 16]),
                        ALU.mult).then_inc(bpad_ready, 1)

            pool.wait_ge(y_evac, SSM_K + 1)
            st.link(pool.iota(dist, pattern=[[P, NT], [-1, T]], base=0, channel_multiplier=1,
                              allow_small_or_imprecise_dtypes=True))
            pool.sem_inc(dist_ready, 1)
            pool.wait_ge(dist_ready, 2)
            for sign in (1, -1):
                st.link(pool.affine_select(out=dist, in_=dist, compare_op=ALU.is_ge, fill=HUGE, base=WINDOW,
                                           pattern=[[-sign * P, NT], [sign, T]], channel_multiplier=-sign))
            pool.sem_inc(dist_ready, 1)

            def gathers(unit0, down, up):
                for b in range(2):
                    pool.wait_ge(stage_ready, unit0 + b + 1)
                    for kk in range(2 * TOPK):
                        slot, j = kk % SLOTS, kk % TOPK
                        pool.wait_ge(gused[slot], (unit0 + b) * GROUNDS + kk // SLOTS + 1)
                        pool.sem_inc(gathers_issued, 1)
                        table = down if kk < TOPK else up
                        pool.indirect_dma_start(
                            out=gslot[:, slot, :], out_offset=None, in_=table[0],
                            in_offset=bass.IndirectOffsetOnAxis(
                                ap=usub(rST)[:, b * TOPK + j:b * TOPK + j + 1], axis=0),
                        ).then_inc(gfull[slot], 16)

            pool.wait_ge(sk_evac, 8)
            with pool.Fori(0, UNITS // 2) as i:
                gathers(i * 2, a["peer_down"], a["peer_up"])
            pool.wait_ge(x_ready, 16)
            for i in range(ROPE // 2):
                st.add(pool.memset(inv_freq[:, i:i + 1], float(
                    np.float32(ROPE_THETA) ** np.float32(-i / np.float32(ROPE // 2)))))
            st.wait()
            pool.sem_inc(inv_ready, 1)
            pool.wait_ge(qk2_msq, 1)
            st.link(pool.memset(causal, 0.0))
            for lo in (0, 2 * P):
                st.link(pool.affine_select(out=causal[:, lo:lo + P], in_=causal[:, lo:lo + P], compare_op=ALU.is_ge,
                                           fill=-HUGE, base=0, pattern=[[-1, P]], channel_multiplier=1))
            pool.sem_inc(causal_ready, 1)
            pool.wait_ge(sk_evac, 16)
            with pool.Fori(0, UNITS // 2) as i:
                gathers(i * 2 + UNITS, a["peer_u_2"], a["peer_v_2"])

        @block.tensor
        def _(pe):
            def dense_slot(b, r, lhs, used, kt=KD, w_cols=512):
                g, per = b // 4, kt // KS
                if b % per == 0 and used is not None:
                    pe.wait_ge(pair_evac[g if per == 4 else (b // 2) % 2], used)
                pair = g if per == 4 else (b // 2) % 2
                pe.wait_ge(wfull[b], r * 16 + 16)
                for kk in range(KS):
                    k = (b % per) * KS + kk
                    for t in range(NT):
                        mm = pe.matmul(dense_bank[2 * pair + t][:, 0:w_cols], lhs[:, k, t * P:(t + 1) * P],
                                       wslot[:, b, kk * w_cols:(kk + 1) * w_cols], start=(k == 0),
                                       stop=(k == kt - 1))
                mm.then_inc(wused[b], 1)

            def dense_slot_T(b, r, rhs, used):
                g = b // 4
                if b % 4 == 0 and used is not None:
                    pe.wait_ge(pair_evac[g], used)
                pe.wait_ge(wfull[b], r * 16 + 16)
                for kk in range(KS):
                    k = (b % 4) * KS + kk
                    for c in range(4):
                        mm = pe.matmul(dense_bank[2 * g + c // 2][:, (c % 2) * T:(c % 2 + 1) * T],
                                       wslot[:, b, kk * 512 + c * P:kk * 512 + (c + 1) * P], rhs[:, k, :],
                                       start=(k == 0 and c % 2 == 0), stop=(k == KD - 1), skip_group_check=True)
                mm.then_inc(wused[b], 1)

            batches = [0]

            def transpose_tiles(src, ready, level):
                for t in range(NT):
                    pe.wait_ge(ready, level + t + 1)
                    for kk in range(4):
                        n = batches[0]
                        if n >= 2:
                            pe.wait_ge(tb_evac, n - 1)
                        for j in range(4):
                            c = (kk * 4 + j) * P
                            tr = pe.transpose(tb[n % 2][:, j * P:(j + 1) * P], src[:, t, c:c + P], ident)
                        tr.then_inc(tb_filled, 1)
                        batches[0] += 1

            pe.wait_ge(consts_ready, 1)
            pe.sem_inc(bt_done, 2)
            pe.sem_inc(bu_done, 2)
            pe.sem_inc(y_done, 1)
            pe.sem_inc(o_done, 2)
            transpose_tiles(h, h_ready, 0)
            pe.wait_ge(tb_evac, 8)
            for b in range(SLOTS):
                dense_slot_T(b, R_U, hT, None)
            pe.wait_ge(sp_done, 1)
            for j, w in enumerate((6, 7, 8, 9)):
                tr = pe.transpose(tb[0][:, j * 64:(j + 1) * 64], pw[w], ident[0:64, 0:64])
            tr.then_inc(sp_t, 1)

            def b_transposes(k, s):
                pe.wait_ge(bpad_ready, k * 8 + s + 1)
                pe.wait_ge(bt_evac, k * 8 + s + 2)
                for part in range(2):
                    tr = pe.transpose(tb[0][:, part * P:(part + 1) * P],
                                      b_pad[:, s % 2, part].rearrange("p b c -> p (b c)"), ident)
                tr.then_inc(bt_done, 1)

            def b_times_u(k, s):
                pe.wait_ge(bt_evac, k * 8 + s + 3)
                if s == 0:
                    pe.wait_ge(ct_evac, k + 1)
                pe.wait_ge(bu_used, k * 8 + s + 1)
                for part in range(2):
                    mm = pe.matmul(mb[s % 2][:, part * T:(part + 1) * T], b_t[:, s % 2, part, :],
                                   uT[:, ds(k, 1), :].rearrange("p a n -> p (a n)"), start=(part == 0), stop=True,
                                   skip_group_check=True)
                mm.then_inc(bu_done, 1)

            def c_times_states(k, s):
                q, d = s // 2, s % 2
                if s == 0:
                    pe.wait_ge(y_evac, k + 1)
                pe.wait_ge(de_ready, k * 8 + s + 3)
                for n, (j, rhs) in enumerate(((0, zr_e[:, 1, :]), (1, zr_e[:, 0, :]))):
                    mm = pe.matmul(tb[1][32 * q:32 * q + 32, 0:T], c_p[:, j, d, q, :], rhs,
                                   start=(d == 0 and n == 0), stop=(d == 1 and n == 1), skip_group_check=True)
                mm.then_inc(y_done, 1)

            def ssm_tile(k, r, slots):
                every = SLOTS // len(slots)
                dense = {n * every: b for n, b in enumerate(slots)}
                dense_slot(dense[0], r, hT, r * 2)
                pe.wait_ge(bc_loaded, k * BC + BC)
                pe.wait_ge(bu_used, k * 8 + 1)
                for j in range(4):
                    tr = pe.transpose(mb[0][:, j * P:(j + 1) * P],
                                      c_st[:, j // 2, j % 2].rearrange("p u n -> p (u n)"), ident)
                tr.then_inc(ct_done, 1)
                b_transposes(k, 0)
                b_times_u(k, 0)
                b_transposes(k, 1)
                for s in range(8):
                    if s < 7:
                        b_times_u(k, s + 1)
                    if s < 6:
                        b_transposes(k, s + 2)
                    if s + 1 in dense:
                        dense_slot(dense[s + 1], r, hT, r * 2)
                    c_times_states(k, s)

            pe.wait_ge(sp_done, 2)
            with pe.Fori(0, SSM_K - 2) as k:
                ssm_tile(k, k + R_QKV, range(SLOTS))
            ssm_tile(SSM_K - 2, R_GLU - 1, range(4))
            ssm_tile(SSM_K - 1, R_GLU - 1, range(4, SLOTS))

            def glu_part(b, r, used, kk):
                pair = (b // 2) % 2
                if kk == 0:
                    if b % 2 == 0:
                        pe.wait_ge(pair_evac[pair], used)
                    pe.wait_ge(wfull[b], r * 16 + 16)
                k = (b % 2) * KS + kk
                for t in range(NT):
                    mm = pe.matmul(dense_bank[2 * pair + t][:, :], yT[:, k, t * P:(t + 1) * P],
                                   wslot[:, b, kk * 512:(kk + 1) * 512], start=(k == 0), stop=(k == SSM_K - 1))
                if kk == KS - 1:
                    mm.then_inc(wused[b], 1)

            def attention_head(j, b0, r, used):
                for b in (b0, b0 + 1):
                    for kk in range(KS):
                        glu_part(b, r, used, kk)
                for t in range(NT):
                    pe.wait_ge(qk_ready, j + 1)
                    for i in range(GQ):
                        tr = pe.transpose(q_bank[t][:, i * P:(i + 1) * P], qk[:, t, i, :], ident)
                    tr.then_inc(qk_t, 1)
                for t in range(NT):
                    tr = pe.transpose(k_bank[:, t * P:(t + 1) * P], qk[:, t, GQ, :], ident)
                tr.then_inc(qk_t, 1)

                def scores(u):
                    t, i = u // GQ, u % GQ
                    pe.wait_ge(nmax_ready, j * UA + u + 1)
                    pe.matmul(mb[u % 2][:, 0:T], qkT[:, i, t * P:(t + 1) * P], qkT[:, GQ, :],
                              start=True, stop=True).then_inc(s_done, 1)

                def p_times_v(u):
                    pe.wait_ge(pt_evac, j * UA + u + 1)
                    pe.wait_ge(o_evac, j * UA + u + 2)
                    for n in range(NT):
                        mm = pe.matmul(o_bank[:, 0:P], v_sb[:, n, :],
                                       probT[:, u % 2, n, :], start=(n == 0), stop=(n == NT - 1))
                    mm.then_inc(o_done, 1)

                pe.wait_ge(qk_tevac, j * 3 + 3)
                scores(0)
                scores(1)
                for u in range(UA):
                    glu_part(b0 + 2 + u // KS, r, used, u % KS)
                    pe.wait_ge(p_ready, j * UA + u + 1)
                    if u:
                        pe.wait_ge(pt_evac, j * UA + u)
                    for n in range(NT):
                        tr = pe.transpose(pt_bank[:, n * P:(n + 1) * P],
                                          prob[:, u % NB, n * P:(n + 1) * P], ident)
                    tr.then_inc(pt_done, 1)
                    if u + 2 < UA:
                        scores(u + 2)
                    if u >= 1:
                        p_times_v(u - 1)
                p_times_v(UA - 1)

            pe.wait_ge(y_act, 1)
            with pe.Fori(0, NKV // 2) as i:
                for g in range(2):
                    attention_head(i * 2 + g, 4 * g, i + R_GLU, i * 4 + g * 2 + 2 * B_GLU)

            pe.wait_ge(o_evac, NKV * UA + 2)
            with pe.Fori(0, 2) as i:
                for b in range(SLOTS):
                    dense_slot(b, i + R_AO, hT, i * 2 + 2 * B_AO)
            transpose_tiles(proj[:, :, C_GA:C_GA + D], merged_ready, 0)
            pe.wait_ge(tb_evac, 16)
            with pe.Fori(0, 2) as i:
                for b in range(SLOTS):
                    dense_slot(b, i + R_WO, hT, i * 2 + 2 * B_WO)

            def peer_scores(layer, r_pq, b_pq):
                transpose_tiles(h, h_ready, 2 + 4 * layer)
                pe.wait_ge(tb_evac, batches[0])
                with pe.Fori(0, 2) as i:
                    for b in range(SLOTS):
                        dense_slot_T(b, i + r_pq, hT, i * 2 + 2 * b_pq)
                pe.wait_ge(keys_loaded, 32 * (layer + 1))
                for n in range(4):
                    if n >= 2:
                        pe.wait_ge(keys_evac, 4 * layer + n - 1)
                    for j in range(4):
                        i = n * 4 + j
                        tr = pe.transpose(tb[n % 2][:, j * P:(j + 1) * P], key_n[:, i // 2, i % 2, :], ident)
                    tr.then_inc(keys_t, 1)
                pe.wait_ge(keys_evac, 4 * layer + 4)
                for g in range(2):
                    pe.wait_ge(pair_evac[g], 2 * b_pq + 4)
                for n in range(8):
                    if n >= 2:
                        pe.wait_ge(sk_evac, 8 * layer + n - 1)
                    for j in range(4):
                        t, i = n // 4, (n % 4) * 4 + j
                        mm = pe.matmul(mb[n % 2][:, j * P:(j + 1) * P], pqT[:, i, t * P:(t + 1) * P],
                                       keyT[:, i, :], start=True, stop=True)
                    mm.then_inc(sk_done, 1)

            peer_scores(0, R_PQ, B_PQ)

            def lru_gates():
                pe.wait_ge(gates_loaded, 32)
                pe.wait_ge(xc_ready, 1)
                for hh in range(NH2):
                    if hh >= 2:
                        pe.wait_ge(gate_act, 2 * (hh - 1))
                    for g in range(2):
                        mm = pe.matmul(mb[hh % 2][:, g * T:(g + 1) * T], w_gates[:, g, hh, :], xcT[:, hh, :],
                                       start=(g == 0), stop=True, skip_group_check=True)
                    mm.then_inc(gate_mm, 1)

            pe.wait_ge(par_loaded, 16 * 7)
            pe.transpose(mb[0][:, 0:80], par_rows, ident[0:80, 0:80]).then_inc(par_t, 1)
            transpose_tiles(h, h_ready, 4)
            pe.wait_ge(tb_evac, batches[0])
            for b in range(SLOTS):
                dense_slot(b, R_IN2, hT, 2 * B_IN2, w_cols=512 if b < 4 else W_C - 512)
            for b in range(SLOTS):
                dense_slot_T(b, R_IN2 + 1, hT, 2 * (B_IN2 + 1))
            for b in range(SLOTS):
                if b == 4:
                    lru_gates()
                dense_slot_T(b, R_IN2 + 2, hT, 2 * (B_IN2 + 2))
            pe.wait_ge(c_ready, 1)
            for t in range(NT):
                for n_tr, lo in ((4, 0), (2, 4)):
                    n = batches[0]
                    pe.wait_ge(tb_evac, n - 1)
                    for j in range(n_tr):
                        tr = pe.transpose(tb[n % 2][:, j * P:(j + 1) * P],
                                          c2[:, t, (lo + j) * P:(lo + j + 1) * P], ident)
                    tr.then_inc(tb_filled, 1)
                    batches[0] += 1
            pe.wait_ge(tb_evac, batches[0])
            for b in range(7):
                pair = b % 2
                pe.wait_ge(pair_evac[pair], 2 * (B_UQ + b // 2))
                pe.wait_ge(wfull[b], 16 * (R_MID + 1))
                lo, kt = (0, 4) if b < 3 else (4, 2)
                for k in range(kt):
                    for t in range(NT):
                        mm = pe.matmul(dense_bank[2 * pair + t][:, :], cT[:, lo + k, t * P:(t + 1) * P],
                                       wslot[:, b, k * 512:(k + 1) * 512], start=(k == 0), stop=(k == kt - 1))
                mm.then_inc(wused[b], 1)
            pe.sem_inc(wused[7], 1)
            def branch_sums(sq, n):
                pe.wait_ge(sq_ready, n)
                for t in range(NT):
                    for k in range(8):
                        mm = pe.matmul(mb[0][:, t:t + 1], k3(sq)[:, k, t * P:(t + 1) * P], ones_c,
                                       start=(k == 0), stop=(k == 7), skip_group_check=True)
                mm.then_inc(sums_done, 1)

            pe.wait_ge(gate_act, 16)
            branch_sums(rec_sq, 1)
            pe.wait_ge(mixed_ready, 1)
            for b in range(6):
                dense_slot(b, R_WO2, hT[:, 8:16, :], 2 * B_WO2 + (b // 4) * 2, kt=8)
            pe.sem_inc(o2_done, 2)
            pe.wait_ge(pair_evac[0], 2 * B_WO2 + 4)
            pe.wait_ge(pair_evac[1], 2 * B_WO2 + 2)
            with pe.Fori(0, NH2 // 2) as i2:
                for e in range(2):
                    j = i2 * 2 + e
                    pe.wait_ge(hd_copied, j * 5 + 5)
                    pe.wait_ge(hd_tevac, j * 2 + 2)
                    for bank, rows, src in ((dense_bank[2], P, head_n[e]), (dense_bank[3], ROPE, head_r[e])):
                        for n in range(4):
                            tr = pe.transpose(bank[0:rows, n * P:(n + 1) * P], src[:, n // 2, n % 2, :], ident)
                    tr.then_inc(hd_t, 1)
                for e in range(2):
                    j = i2 * 2 + e
                    pe.wait_ge(hd_tevac, j * 2 + 4)
                    pe.wait_ge(nm2_ready, j + 1)
                    for t, (lo, hi) in enumerate(tile_keys):
                        for part, src in enumerate((headT_n[e], headT_r[e])):
                            mm = pe.matmul(mb[e][:, lo:hi], src[:, 0, t * P:(t + 1) * P], src[:, 1, 0:hi - lo],
                                           start=(t == 0 and part == 0), stop=(part == 1), skip_group_check=True)
                    mm.then_inc(s2_done, 1)
                for e in range(2):
                    j = i2 * 2 + e
                    pe.wait_ge(p2_ready, j + 1)
                    for n in range(3):
                        tr = pe.transpose(tb[e][:, n * P:(n + 1) * P], prob2[e][:, n * P:(n + 1) * P], ident)
                    tr.then_inc(pt2_done, 1)
                for e in range(2):
                    j = i2 * 2 + e
                    pe.wait_ge(pt2_evac, j + 1)
                    pe.wait_ge(o2_evac, j + 1)
                    for n, (t, key) in enumerate(((0, 0), (1, 0), (1, 1))):
                        mm = pe.matmul(dense_bank[e][:, t * P:(t + 1) * P], head_v[e][:, key, :],
                                       prob2T[e][:, n * P:(n + 1) * P], start=(n == 0), stop=(n != 1),
                                       skip_group_check=True)
                    mm.then_inc(o2_done, 1)
            for b in (6, 7):
                dense_slot(b, R_WO2, hT[:, 8:16, :], 2 * B_WO2 + 2, kt=8)
            branch_sums(att_sq, 2)
            pe.wait_ge(mixed_ready, 2)
            for b in range(SLOTS):
                dense_slot(b, R_WO2 + 1, hT, 2 * B_WO2 + 4 + (b // 4) * 2, kt=8)
            peer_scores(1, R_PQ2, B_PQ2)

        @block.scalar
        def _(act):
            st = Steps(act, acs)

            def norm_rms(m):
                for t in range(NT):
                    act.wait_ge(msq_ready, 2 * m + t + 1)
                    act.activation(stat[:, 4 + t:5 + t], stat[:, 2 + t:3 + t], ACT.Sqrt).then_inc(rms_ready, 1)

            batches = [0]

            def evac_tiles():
                for t in range(NT):
                    for kk in range(4):
                        n = batches[0]
                        act.wait_ge(tb_filled, n + 1)
                        act.activation(hT[:, kk * 4:(kk + 1) * 4, t * P:(t + 1) * P],
                                       tb[n % 2][:, :].rearrange("p (k n) -> p k n", k=4),
                                       ACT.Copy).then_inc(tb_evac, 1)
                        batches[0] += 1

            act.dma_start(gain, a["mix_norm_g"][0].partition_broadcast(P)).then_inc(gain_loaded, 16)
            act.dma_start(ssm_d, a["ssm_d"][0].rearrange("(k p) -> p k", p=P),
                          allow_slow_non_contiguous=True).then_inc(small_loaded, 16)
            act.dma_start(sink, a["attn_sink"][0].partition_broadcast(P)).then_inc(small_loaded, 16)
            act.sem_inc(bt_evac, 2)
            norm_rms(0)
            evac_tiles()

            for dst, name in ((pw[0], "ssm_a_re"), (pw[1], "ssm_a_im")):
                act.dma_start(dst, a[name].rearrange("l d (g two) n -> (l d g) (two n)",
                                                     two=2)).then_inc(ssm_loaded, 16)
            act.dma_start(step2, a["ssm_log_step"].rearrange("l d (g two) -> (l d g) two",
                                                             two=2)).then_inc(ssm_loaded, 16)

            b_dram = [a[n].rearrange("l d (k q two) n c -> k (two n) (l d) q c", q=PAIRS, two=2)
                      for n in ("ssm_b_re", "ssm_b_im")]
            c_dram = [a[n].rearrange("l d (k g) c n -> k (g c) (l d) n", g=8) for n in ("ssm_c_re", "ssm_c_im")]

            def load_bc(k):
                for part in range(2):
                    for d in range(2):
                        src = b_dram[part][ds(k, 1), :, d].rearrange("k p q c -> (k p) q c")
                        act.dma_start(b_st[:, part, d], src).then_inc(bc_loaded, 16)
                    src = c_dram[part][ds(k, 1)].rearrange("k p d n -> (k p) d n")
                    for u in range(2):
                        act.dma_start(c_st[:, :, part, u, :], src).then_inc(bc_loaded, 16)

            load_bc(0)
            act.wait_ge(ssm_loaded, 48)
            act.activation(step2, step2, ACT.Exp).then_inc(sp_act, 1)
            act.wait_ge(sp_in, 1)
            act.activation(pw[6], pw[2], ACT.Exp).then_inc(sp_act, 1)
            act.wait_ge(sp_in, 2)
            act.activation(pw[4], pw[10], ACT.Sin, scale=TWO_PI_BELOW).then_inc(sp_act, 1)
            act.activation(pw[5], pw[11], ACT.Sin, scale=TWO_PI_BELOW).then_inc(sp_act, 1)

            for g in range(2):
                act.wait_ge(wused[4 * g + 3], R_U + 1)
                for c in range(2):
                    act.activation(uT[:, 4 * g + 2 * c:4 * g + 2 * c + 2, :],
                                   dense_bank[2 * g + c][:, :].rearrange("p (k n) -> p k n", k=2),
                                   ACT.Copy).then_inc(pair_evac[g], 1)

            def dense_evac(r, g, dest, col, n=512):
                act.wait_ge(wused[4 * g + 3], r + 1)
                for t in range(NT):
                    act.activation(dest[:, t, ds(col, n)], dense_bank[2 * g + t][:, 0:n],
                                   ACT.Copy).then_inc(pair_evac[g], 1)

            def ssm_tile(k, i, groups):
                for s in range(8):
                    act.wait_ge(bt_done, k * 8 + s + 3)
                    act.wait_ge(bu_done, k * 8 + s + 1)
                    act.activation(b_t[:, s % 2].rearrange("p a n -> p (a n)"),
                                   tb[0][:, 0:2 * P], ACT.Copy).then_inc(bt_evac, 1)
                    act.wait_ge(f_ready, k * 8 + s + 1)
                    act.wait_ge(de_ready, k * 8 + s + 1)
                    act.activation(rot[:, s % 2], phase, ACT.Sin, scale=TWO_PI_BELOW).then_inc(e_ready, 1)
                    if s in groups:
                        dense_evac(i + R_QKV, groups[s], proj, (i * 2 + groups[s]) * 512)

            def reload_bc(k):
                act.wait_ge(bpad_ready, k * 8 + 8)
                act.wait_ge(ct_done, k + 1)
                load_bc(k + 1)

            with act.Fori(0, SSM_K - 2) as k:
                ssm_tile(k, k, {3: 0, 7: 1})
                reload_bc(k)
            last = R_GLU - 1 - R_QKV
            ssm_tile(SSM_K - 2, last, {7: 0})
            reload_bc(SSM_K - 2)
            ssm_tile(SSM_K - 1, last, {7: 1})

            act.wait_ge(y_evac, SSM_K + 1)
            act.dma_start(g_qk[:, 0, :], a["q_norm_g"][0].partition_broadcast(P)).then_inc(small_loaded, 16)
            act.dma_start(g_qk[:, GQ, :], a["k_norm_g"][0].partition_broadcast(P)).then_inc(small_loaded, 16)
            act.activation(hs[:, 2048:4096], hs[:, 2048:4096], ACT.Gelu).then_inc(y_act, 1)
            def gate_sigmoid(col):
                for t in range(NT):
                    act.activation(proj[:, t, col:col + D], proj[:, t, col:col + D], ACT.Sigmoid).then_inc(gate_sig, 1)

            act.wait_ge(pair_evac[1], 2 * B_GLU)
            gate_sigmoid(C_GB)

            def attention_head(j, g, r, used):
                act.wait_ge(o_evac, j * UA + 2)
                act.activation(qk[:, :, 0:GQ, :].rearrange("p t j c -> p t (j c)"), proj[:, :, ds(j * 512, 512)],
                               ACT.Copy).then_inc(qk_copied, 1)
                act.activation(qk[:, :, GQ, :], proj[:, :, ds(j * HD + C_K, HD)], ACT.Copy).then_inc(qk_copied, 1)
                act.activation(v_sb, proj[:, :, ds(j * HD + C_V, HD)], ACT.Copy).then_inc(qk_copied, 1)
                act.wait_ge(qk_msq, j + 1)
                act.activation(sm[:, 10:20], sm[:, 0:10], ACT.Sqrt).then_inc(qk_rms, 1)
                for t in range(NT):
                    act.wait_ge(qk_t, j * 3 + t + 1)
                    act.activation(qkT[:, 0:GQ, t * P:(t + 1) * P], q_bank[t][:, :].rearrange("p (j n) -> p j n", j=GQ),
                                   ACT.Copy).then_inc(qk_tevac, 1)
                act.wait_ge(qk_t, j * 3 + 3)
                act.activation(qkT[:, GQ, :], k_bank[:, 0:T], ACT.Copy).then_inc(qk_tevac, 1)

                def exps(u):
                    nmax = nmax_u[u % NB]
                    act.wait_ge(nmax_ready, j * UA + u + 3)
                    act.activation(prob[:, u % NB, :], prob[:, u % NB, :], ACT.Exp, bias=nmax,
                                   accum_out=sum_u[u % NB]).then_inc(p_exp, 1)
                    act.activation(sink_u[u % NB], sink[:, ds(j * GQ + u % GQ, 1)], ACT.Exp,
                                   bias=nmax).then_inc(p_exp, 1)

                exps(0)
                for u in range(UA):
                    if u + 1 < UA:
                        exps(u + 1)
                    act.wait_ge(pt_done, j * UA + u + 1)
                    act.wait_ge(o_done, j * UA + u + 1)
                    act.activation(probT[:, u % 2].rearrange("p k n -> p (k n)"),
                                   pt_bank[:, 0:T], ACT.Copy).then_inc(pt_evac, 1)
                act.wait_ge(wused[4 * g + 3], r + 1)
                act.wait_ge(glu_used, used)
                for t in range(NT):
                    act.activation(glu_sg[:, t, :], dense_bank[2 + t][:, :], ACT.Sigmoid).then_inc(pair_evac[1], 1)

            with act.Fori(0, NKV // 2) as i:
                for g in range(2):
                    attention_head(i * 2 + g, g, i + R_GLU, i * 4 + g * 2 + 2)
            gate_sigmoid(C_GA)
            evac_tiles()

            def peer_head(layer, g, keys, r_pq, gain_after):
                act.wait_ge(x_ready, gain_after)
                act.dma_start(gain, g.partition_broadcast(P)).then_inc(gain_loaded, 16)
                for s in range(2):
                    act.dma_start(key_n[:, :, s, :], keys[s].rearrange("h k d -> k h d")).then_inc(keys_loaded, 16)
                norm_rms(1 + 2 * layer)
                evac_tiles()
                with act.Fori(0, 2) as i:
                    for g in range(2):
                        act.wait_ge(wused[4 * g + 3], i + r_pq + 1)
                        for c in range(2):
                            act.activation(pqT[:, ds(i * 8 + 4 * g + 2 * c, 2), :],
                                           dense_bank[2 * g + c][:, :].rearrange("p (k n) -> p k n", k=2),
                                           ACT.Copy).then_inc(pair_evac[g], 1)
                for n in range(4):
                    act.wait_ge(keys_t, 4 * layer + n + 1)
                    act.activation(keyT[:, n * 4:(n + 1) * 4, :].rearrange("p j c -> p (j c)"), tb[n % 2][:, :],
                                   ACT.Copy).then_inc(keys_evac, 1)
                for n in range(8):
                    act.wait_ge(sk_done, 8 * layer + n + 1)
                    act.activation(kscore[:, n * 512:(n + 1) * 512], mb[n % 2][:, :], ACT.Copy).then_inc(sk_evac, 1)

            def peer_soft(u, b):
                act.wait_ge(topk_v, u + 1)
                act.activation(sub(rGT)[:, b * TOPK:(b + 1) * TOPK], sub(rTP)[:, b * TOPK:(b + 1) * TOPK], ACT.Exp,
                               bias=sub(rSS)[:, b:b + 1], accum_out=sub(rSS)[:, 2 + b:3 + b]).then_inc(topk_e, 1)

            def peer_gelu(u, b):
                act.wait_ge(gused[7], u * GROUNDS + 3)
                act.activation(sub(rGE)[:, b * TOPK:(b + 1) * TOPK], sub(rAC)[:, b * TOPK:(b + 1) * TOPK],
                               ACT.Gelu).then_inc(gelu_ready, 1)

            def peer_units(layer):
                base = layer * UNITS
                peer_soft(base, 0)
                with act.Fori(0, UNITS // 2 - 1) as i:
                    peer_gelu(i * 2 + base, 0)
                    peer_soft(i * 2 + base + 1, 1)
                    peer_gelu(i * 2 + base + 1, 1)
                    peer_soft(i * 2 + base + 2, 0)
                last = base + UNITS - 2
                peer_gelu(last, 0)
                peer_soft(last + 1, 1)
                peer_gelu(last + 1, 1)

            peer_head(0, a["ffn_norm_g"][0], (a["peer_sub_keys_1"][0], a["peer_sub_keys_2"][0]), R_PQ, 8)
            peer_units(0)

            act.wait_ge(x_ready, 16)
            act.dma_start(gain, a["mix_norm_g_2"][0].partition_broadcast(P)).then_inc(gain_loaded, 16)
            rows = 0
            for name in ("conv_w_2", "conv_b_2", "b_rgate_2", "b_igate_2", "lru_lambda_2", "attn_out_norm_g_2",
                         "rec_out_norm_g_2"):
                src = (a[name][0].rearrange("j (k p) -> (j k) p", p=P) if name == "conv_w_2"
                       else a[name][0].rearrange("(k p) -> k p", p=P))
                n = src.shape[0]
                act.dma_start(par_rows[rows:rows + n, :], src).then_inc(par_loaded, 16)
                rows += n
            for dst, name in ((g_cq, "q_norm_g_2"), (g_ckv, "kv_norm_g_2"), (g_qh, "q_head_norm_g_2"),
                              (g_kh, "k_head_norm_g_2")):
                act.dma_start(dst, a[name][0].partition_broadcast(P)).then_inc(rope_loaded, 16)
            act.dma_start(pos_i, a["positions_2"][0].rearrange("(t p) -> p t", p=P),
                          allow_slow_non_contiguous=True).then_inc(rope_loaded, 16)
            norm_rms(2)
            evac_tiles()
            for g, name in enumerate(("w_rgate_2", "w_igate_2")):
                act.dma_start(w_gates[:, g], a[name][0].rearrange("h i j -> i h j")).then_inc(gates_loaded, 16)
            act.wait_ge(ang_ready, 1)
            act.activation(trig, ang, ACT.Sin, scale=TWO_PI_BELOW).then_inc(trig_ready, 1)
            act.wait_ge(par_ready, 1)
            act.activation(lp[:, 0:8], lam, ACT.Abs).then_inc(lam_act, 1)
            act.wait_ge(lam_act, 1)
            act.activation(lp[:, 8:16], lp[:, 0:8], ACT.Exp, scale=-1.0).then_inc(lam_act, 1)
            for g in range(2):
                n = 512 if g == 0 else W_C - 512
                dense_evac(R_IN2, g, c2, g * 512, n)
            act.wait_ge(c_msq, 1)
            act.activation(stat[:, 20:24], stat[:, 16:20], ACT.Sqrt).then_inc(c_rms, 1)
            def evac_T(r, g, dst):
                act.wait_ge(wused[4 * g + 3], r + 1)
                for c in range(2):
                    act.activation(dst[:, 4 * g + 2 * c:4 * g + 2 * c + 2, :],
                                   dense_bank[2 * g + c][:, :].rearrange("p (k n) -> p k n", k=2),
                                   ACT.Copy).then_inc(pair_evac[g], 1)

            evac_T(R_IN2 + 1, 0, xrT)
            evac_T(R_IN2 + 1, 1, xrT)
            evac_T(R_IN2 + 2, 0, ygT)
            for hh in range(NH2):
                act.wait_ge(gate_mm, hh + 1)
                for g, (dst, bias) in enumerate(((rr_g, b_rg), (ii_g, b_ig))):
                    act.activation(k3(dst)[:, hh, :], mb[hh % 2][:, g * T:(g + 1) * T], ACT.Sigmoid,
                                   bias=bias[:, hh:hh + 1]).then_inc(gate_act, 1)
            act.wait_ge(lam_dve, 1)
            act.wait_ge(gate_act, 16)
            for hh in range(NH2):
                act.activation(k3(th_g)[:, hh, :], k3(rr_g)[:, hh, :], ACT.Tanh,
                               scale=neg_c[:, hh:hh + 1]).then_inc(lru_act, 1)
            act.wait_ge(lru_act, 8)
            for hh in range(NH2):
                act.activation(k3(rr_g)[:, hh, :], k3(rr_g)[:, hh, :], ACT.Exp,
                               scale=neg_c[:, hh:hh + 1]).then_inc(lru_act, 1)
            evac_T(R_IN2 + 2, 1, ygT)
            for t in range(NT):
                for n_tr, lo in ((4, 0), (2, 4)):
                    n = batches[0]
                    act.wait_ge(tb_filled, n + 1)
                    act.activation(cT[:, lo:lo + n_tr, t * P:(t + 1) * P],
                                   tb[n % 2][:, 0:n_tr * P].rearrange("p (k n) -> p k n", k=n_tr),
                                   ACT.Copy).then_inc(tb_evac, 1)
                    batches[0] += 1
            act.wait_ge(lru_dve, 1)
            act.activation(th_g, th_g, ACT.Sqrt, scale=-1.0).then_inc(lru_act, 1)
            act.wait_ge(pair_evac[1], 2 * B_UQ)
            act.activation(ygT, ygT, ACT.Gelu).then_inc(lru_act, 1)
            q2f = q2.rearrange("p t h c -> p t (h c)")
            kv2f = kv2.rearrange("p t h c -> p t (h c)")

            def up_evac(b):
                act.wait_ge(wused[b], R_MID + 1)
                dst, col = (q2f, b * 512) if b < 3 else (kv2f, (b - 3) * 512)
                for t in range(NT):
                    act.activation(dst[:, t, col:col + 512], dense_bank[2 * (b % 2) + t][:, :],
                                   ACT.Copy).then_inc(pair_evac[b % 2], 1)

            up_evac(0)
            up_evac(1)
            up_evac(2)
            up_evac(3)
            up_evac(4)
            up_evac(5)
            up_evac(6)
            act.wait_ge(pair_evac[1], 2 * B_WO2 - 2)
            act.sem_inc(pair_evac[1], 2)
            act.wait_ge(sums_done, 2)
            act.activation(stat[:, 28:30], stat[:, 24:26], ACT.Sqrt).then_inc(branch_rms, 1)
            act.wait_ge(qk2_msq, 1)
            act.activation(rms2, msq2[:, 0:32], ACT.Sqrt).then_inc(qk2_rms, 1)
            act.wait_ge(qk2_ready, 1)
            act.sem_inc(hd_tevac, 2)
            with act.Fori(0, NH2 // 2) as i2:
                for e in range(2):
                    j = i2 * 2 + e
                    act.wait_ge(o2_done, j + 1)
                    hj = ds(j, 1)
                    for dst, src in ((head_n[e][:, 0], q2[:, :, hj, 0:NOPE]), (head_n[e][:, 1], kn2[:, :, hj, :]),
                                     (head_r[e][:, 0], qr2[:, :, hj, :]), (head_r[e][:, 1], krh[:, :, hj, :]),
                                     (head_v[e], kv2[:, :, hj, NOPE:2 * NOPE])):
                        act.activation(dst, src.rearrange("p t h c -> p t (h c)"), ACT.Copy).then_inc(hd_copied, 1)
                for e in range(2):
                    j = i2 * 2 + e
                    act.wait_ge(hd_t, j + 1)
                    act.activation(headT_n[e].rearrange("p j n -> p (j n)"), dense_bank[2][:, :],
                                   ACT.Copy).then_inc(hd_tevac, 1)
                    act.activation(headT_r[e].rearrange("p j n -> p (j n)"), dense_bank[3][0:ROPE, :],
                                   ACT.Copy).then_inc(hd_tevac, 1)
                for e in range(2):
                    j = i2 * 2 + e
                    act.wait_ge(nm2_ready, j + 3)
                    for t, (lo, hi) in enumerate(tile_keys):
                        act.activation(prob2[e][:, lo:hi], prob2[e][:, lo:hi], ACT.Exp, bias=att[e][0][:, t:t + 1],
                                       accum_out=att[e][1][:, t:t + 1]).then_inc(p2_exp, 1)
                for e in range(2):
                    j = i2 * 2 + e
                    act.wait_ge(pt2_done, j + 1)
                    act.activation(prob2T[e], tb[e][:, 0:W_S], ACT.Copy).then_inc(pt2_evac, 1)
            act.wait_ge(sums_done, 4)
            act.activation(stat[:, 30:32], stat[:, 26:28], ACT.Sqrt).then_inc(branch_rms, 1)
            peer_head(1, a["ffn_norm_g_2"][0], (a["peer_keys_1_2"][0], a["peer_keys_2_2"][0]), R_PQ2, 24)
            peer_units(1)

        @block.vector
        def _(v):
            st = Steps(v, dve)
            v.sem_inc(bu_used, 2)
            v.sem_inc(de_ready, 2)
            v.sem_inc(y_evac, 1)
            v.sem_inc(nmax_ready, 2)
            v.sem_inc(o_evac, 2)
            v.sem_inc(glu_used, 2)
            for b in range(SLOTS):
                v.sem_inc(gused[b], 1)

            def norm(m):
                for t in range(NT):
                    st.link(v.tensor_tensor_reduce(h[:, t, :], x[:, t, :], x[:, t, :], 1.0, 0.0, ALU.mult, ALU.add,
                                                   stat[:, t:t + 1]))
                    v.tensor_scalar(stat[:, 2 + t:3 + t], stat[:, t:t + 1], 1.0 / D, EPS, ALU.mult,
                                    ALU.add).then_inc(msq_ready, 1)
                v.wait_ge(gain_loaded, 16 * (m + 1))
                for t in range(NT):
                    v.wait_ge(rms_ready, 2 * m + t + 1)
                    st.link(v.reciprocal(stat[:, 6 + t:7 + t], stat[:, 4 + t:5 + t]))
                    v.scalar_tensor_tensor(h[:, t, :], x[:, t, :], stat[:, 6 + t:7 + t], gain, ALU.mult,
                                           ALU.mult).then_inc(h_ready, 1)

            v.wait_ge(x_loaded, 32)
            norm(0)

            a_re, a_im = pw[0], pw[1]
            bcast = lambda i: step2.unsqueeze(2).broadcast_to([64, 2, 64])
            v.wait_ge(sp_act, 1)
            v.wait_ge(ssm_loaded, 48)
            halves = lambda w: w.rearrange("p (f n) -> p f n", f=2)
            v.tensor_tensor(halves(pw[2]), halves(a_re), bcast(0), ALU.mult).then_inc(sp_in, 1)
            st.link(v.tensor_tensor(halves(pw[3]), halves(a_im), bcast(0), ALU.mult))
            st.link(v.tensor_scalar(pw[3], pw[3], float(1 / (2 * np.pi)), None, ALU.mult))
            st.link(v.tensor_scalar(pw[12], pw[3], ROUND, -ROUND, ALU.add, ALU.add))
            st.link(v.tensor_tensor(pw[7], pw[3], pw[12], ALU.subtract))
            st.link(v.tensor_scalar(pw[3], pw[7], 0.25, None, ALU.add))
            st.link(v.tensor_scalar(pw[12], pw[3], ROUND, -ROUND, ALU.add, ALU.add))
            st.link(v.tensor_copy(pw[10], pw[7]))
            v.tensor_tensor(pw[11], pw[3], pw[12], ALU.subtract).then_inc(sp_in, 1)
            v.wait_ge(sp_act, 4)
            st.link(v.tensor_tensor(pw[5], pw[5], pw[6], ALU.mult))
            st.link(v.tensor_scalar(pw[5], pw[5], -1.0, None, ALU.add))
            st.link(v.tensor_tensor(pw[4], pw[4], pw[6], ALU.mult))
            st.add(v.tensor_tensor(pw[12], a_re, a_re, ALU.mult))
            st.link(v.tensor_tensor(pw[13], a_im, a_im, ALU.mult))
            st.link(v.tensor_tensor(pw[12], pw[12], pw[13], ALU.add))
            st.link(v.reciprocal(pw[12], pw[12]))
            st.add(v.tensor_tensor(pw[8], pw[5], a_re, ALU.mult))
            st.add(v.tensor_tensor(pw[13], pw[4], a_im, ALU.mult))
            st.add(v.tensor_tensor(pw[9], pw[4], a_re, ALU.mult))
            st.link(v.tensor_tensor(pw[3], pw[5], a_im, ALU.mult))
            st.add(v.tensor_tensor(pw[8], pw[8], pw[13], ALU.add))
            st.link(v.tensor_tensor(pw[9], pw[9], pw[3], ALU.subtract))
            st.link(v.tensor_tensor(pw[8], pw[8], pw[12], ALU.mult))
            v.tensor_tensor(pw[9], pw[9], pw[12], ALU.mult).then_inc(sp_done, 1)
            v.wait_ge(sp_t, 1)
            v.tensor_copy(prm.rearrange("p j n -> p (j n)"), tb[0][:, 0:256]).then_inc(sp_done, 1)
            v.wait_ge(sp_done, 2)
            for g in range(2):
                v.wait_ge(pair_evac[g], 2)
            v.wait_ge(small_loaded, 32)

            def direction(t, d):
                return t if d == 0 else t[:, :, ::-1]

            def phase_1(k, s):
                q, d = s // 2, s % 2
                return v.scalar_tensor_tensor(
                    phase, iota_t.unsqueeze(1).broadcast_to([P, 2, T]), prm[:, 1, ds(k * 4 + (d * 32 + q), 1)],
                    quarter.unsqueeze(2).broadcast_to([P, 2, T]), ALU.mult, ALU.add)

            def phase_2():
                return v.tensor_scalar(whole, phase, ROUND, -ROUND, ALU.add, ALU.add)

            def phase_3():
                return v.tensor_tensor(phase, phase, whole, ALU.subtract)

            def ssm_tile(k):
                st.link(phase_1(k, 0))
                st.link(phase_2())
                phase_3().then_inc(f_ready, 1)
                v.wait_ge(ct_done, k + 1)
                v.tensor_tensor(c_t.rearrange("p d a n -> p (d a) n"),
                                mb[0][:, :].rearrange("p (j n) -> p j n", j=4),
                                mask_c.unsqueeze(1).broadcast_to([P, 4, P]), ALU.mult).then_inc(ct_evac, 1)
                v.wait_ge(ct_evac, k + 1)
                f = [prm[:, 2 + j, :].rearrange("p (d n) -> p d n", d=2)[:, :, ds(k * 4, 4)]
                     .unsqueeze(3).broadcast_to([P, 2, PAIRS, 32]) for j in range(2)]
                c = [c_t[:, :, j, :].rearrange("p d (q c) -> p d q c", q=PAIRS) for j in range(2)]
                t4 = [sc[:, r[0] + 256 * j:r[0] + 256 * (j + 1)] for r in (rA, rB) for j in range(2)]
                w4 = [w.rearrange("p (d q c) -> p d q c", d=2, q=PAIRS) for w in t4]
                st.add(v.tensor_tensor(w4[0], c[0], f[0], ALU.mult))
                st.add(v.tensor_tensor(w4[1], c[1], f[1], ALU.mult))
                st.add(v.tensor_tensor(w4[2], c[0], f[1], ALU.mult))
                st.add(v.tensor_tensor(w4[3], c[1], f[0], ALU.mult))
                v.wait_ge(y_done, k * 8 + 1)
                st.wait()
                flat = [c_p[:, j].rearrange("p d q c -> p (d q c)") for j in range(2)]
                st.add(v.tensor_tensor(flat[0], t4[0], t4[1], ALU.subtract))
                st.link(v.scalar_tensor_tensor(flat[1], t4[2], -1.0, t4[3], ALU.mult, ALU.subtract))
                for s in range(8):
                    q, d = s // 2, s % 2
                    both = lambda t: t.unsqueeze(1).broadcast_to([P, 2, T])
                    e = direction(rot[:, s % 2], d)
                    radius = prm[:, 0, ds(k * 4 + (d * 32 + q), 1)].broadcast_to([P, T])
                    v.wait_ge(bu_done, k * 8 + s + 3)
                    v.wait_ge(e_ready, k * 8 + s + 1)
                    st.add(v.tensor_tensor(bre_e, both(mb[s % 2][:, 0:T]), e, ALU.mult))
                    v.tensor_tensor(bim_e, both(mb[s % 2][:, T:2 * T]), e, ALU.mult).then_inc(bu_used, 1)
                    p1 = st.add(phase_1(k, s + 1)) if s < 7 else None
                    v.wait_ge(bu_used, k * 8 + s + 3)
                    st.add(v.tensor_tensor(z_in[:, 0, :], bre_e[:, 1, :], bim_e[:, 0, :], ALU.add))
                    z2 = st.add(v.tensor_tensor(z_in[:, 1, :], bim_e[:, 1, :], bre_e[:, 0, :], ALU.subtract))
                    if s < 7:
                        st.wait(p1)
                        p2 = st.add(phase_2())
                    st.wait(z2)
                    for c_ in range(2):
                        zi, zo = z_in[:, c_, :], z_out[:, c_, :]
                        if d:
                            zi, zo = zi[:, ::-1], zo[:, ::-1]
                        z3 = st.add(v.tensor_tensor_scan(zo, radius, zi, 0.0, ALU.mult, ALU.add))
                    if s < 7:
                        st.wait(p2)
                        phase_3().then_inc(f_ready, 1)
                    v.wait_ge(y_done, k * 8 + s + 1)
                    st.wait(z3)
                    st.add(v.tensor_tensor(zr_e, both(z_out[:, 0, :]), e, ALU.mult))
                    st.link(v.tensor_tensor(zi_e, both(z_out[:, 1, :]), e, ALU.mult))
                    st.add(v.tensor_tensor(zr_e[:, 1, :], zr_e[:, 1, :], zi_e[:, 0, :], ALU.subtract))
                    v.tensor_tensor(zr_e[:, 0, :], zr_e[:, 0, :], zi_e[:, 1, :], ALU.add).then_inc(de_ready, 1)
                v.wait_ge(y_done, k * 8 + 9)
                kk = ds(k, 1)
                v.scalar_tensor_tensor(yT[:, kk, :].rearrange("p a n -> p (a n)"),
                                       uT[:, kk, :].rearrange("p a n -> p (a n)"), ssm_d[:, kk],
                                       tb[1][:, 0:T], ALU.mult, ALU.add).then_inc(y_evac, 1)
                v.wait_ge(y_evac, k + 2)
                v.sem_inc(turn_over, 1)
                st.clear()

            st.clear()
            v.wait_ge(consts_ready, 1)
            with v.Fori(0, SSM_K) as k:
                ssm_tile(k)

            v.wait_ge(dist_ready, 1)
            v.scalar_tensor_tensor(dist, dist, -1.0, dist, ALU.mult, ALU.max).then_inc(dist_ready, 1)
            st.add(v.tensor_scalar(nsink, sink, -1.0, None, ALU.mult))
            v.wait_ge(small_loaded, 64)
            for i in range(1, GQ):
                st.add(v.tensor_scalar(g_qk[:, i, :], g_qk[:, 0, :], float(HD ** -0.5), None, ALU.mult))
            st.wait()
            st.link(v.tensor_scalar(g_qk[:, 0, :], g_qk[:, 0, :], float(HD ** -0.5), None, ALU.mult))
            v.wait_ge(dist_ready, 3)
            st.clear()
            v.wait_ge(gate_sig, 2)

            def attention_head(j, g, r, used):
                gb = lambda t: proj[:, t, ds(j * 512 + C_GB, 512)]
                v.wait_ge(qk_copied, j * 3 + 3)
                rows = qk.rearrange("p t j c -> p (t j) c")
                flat = qk.rearrange("p t j c -> p (t j c)")
                st.link(v.tensor_tensor(qk_sq, flat, flat, ALU.mult))
                st.link(v.tensor_reduce(sm[:, 0:10], qk_sq.rearrange("p (r c) -> p r c", c=HD), AX, ALU.add))
                v.tensor_scalar(sm[:, 0:10], sm[:, 0:10], 1.0 / HD, EPS, ALU.mult, ALU.add).then_inc(qk_msq, 1)
                v.wait_ge(qk_rms, j + 1)
                st.link(v.reciprocal(sm[:, 30:40], sm[:, 10:20]))
                st.link(v.tensor_tensor(rows, rows, sm[:, 30:40].unsqueeze(2).broadcast_to([P, 10, HD]), ALU.mult))
                v.tensor_tensor(qk, qk, g_qk.unsqueeze(1).broadcast_to([P, NT, GQ + 1, HD]),
                                ALU.mult).then_inc(qk_ready, 1)

                def logits(u):
                    t, i = u // GQ, u % GQ
                    v.wait_ge(s_done, j * UA + u + 1)
                    if u >= NB:
                        v.wait_ge(pt_done, j * UA + u - NB + 1)
                    st.link(v.scalar_tensor_tensor(prob[:, u % NB, :], dist[:, t, :], nslope[:, ds(j * GQ + i, 1)],
                                                   mb[u % 2][:, 0:T], ALU.mult, ALU.add))
                    st.link(v.tensor_reduce(sm[:, 40:41], prob[:, u % NB, :], AX, ALU.max, negate=True))
                    v.tensor_tensor(nmax_u[u % NB], sm[:, 40:41], nsink[:, ds(j * GQ + i, 1)],
                                    ALU.min).then_inc(nmax_ready, 1)

                def take_o(u):
                    t, i = u // GQ, u % GQ
                    v.wait_ge(o_done, j * UA + u + 3)
                    v.tensor_copy(hT[:, ds(j * GQ + i, 1), t * P:(t + 1) * P].rearrange("p a n -> p (a n)"),
                                  o_bank[:, 0:P]).then_inc(o_evac, 1)

                logits(0)
                logits(1)
                for u in range(UA):
                    if u >= 2:
                        take_o(u - 2)
                    if u == 4:
                        v.wait_ge(wused[4 * g + 1], r + 1)
                        for t_ in range(NT):
                            v.tensor_tensor(gb(t_), dense_bank[t_][:, :], gb(t_), ALU.mult).then_inc(pair_evac[0], 1)
                    v.wait_ge(p_exp, (j * UA + u) * 2 + 2)
                    st.link(v.tensor_tensor(sm[:, 41:42], sum_u[u % NB], sink_u[u % NB], ALU.add))
                    st.link(v.reciprocal(sm[:, 42:43], sm[:, 41:42]))
                    v.tensor_scalar(prob[:, u % NB, :], prob[:, u % NB, :], sm[:, 42:43], None,
                                    ALU.mult).then_inc(p_ready, 1)
                    if u + 2 < UA:
                        logits(u + 2)
                take_o(UA - 2)
                take_o(UA - 1)
                v.wait_ge(pair_evac[0], used + 2)
                for t_ in range(NT):
                    v.wait_ge(pair_evac[1], used + t_ + 1)
                    v.tensor_tensor(gb(t_), gb(t_), glu_sg[:, t_, :], ALU.mult).then_inc(glu_used, 1)
                st.clear()

            with v.Fori(0, NKV // 2) as i:
                for g in range(2):
                    attention_head(i * 2 + g, g, i + R_GLU, i * 4 + g * 2 + 2 * B_GLU)

            v.wait_ge(gate_sig, 2 * NT)
            v.wait_ge(glu_used, 2 * NKV + 2)
            with v.Fori(0, 2) as i:
                for g in range(2):
                    v.wait_ge(wused[4 * g + 3], i + R_AO + 1)
                    for t in range(NT):
                        m = proj[:, t, ds(i * 1024 + (C_GA + g * 512), 512)]
                        v.tensor_tensor(m, dense_bank[2 * g + t][:, :], m, ALU.mult).then_inc(pair_evac[g], 1)
                    v.wait_ge(pair_evac[g], i * 2 + (2 * B_AO + 2))
                    for t in range(NT):
                        m = proj[:, t, ds(i * 1024 + (C_GA + g * 512), 512)]
                        gb = proj[:, t, ds(i * 1024 + (C_GB + g * 512), 512)]
                        st.add(v.tensor_tensor(m, m, gb, ALU.add))
                    st.wait()
                v.sem_inc(turn_over, 1)
                st.clear()
            v.sem_inc(merged_ready, 2)

            def add_to_x(r):
                with v.Fori(0, 2) as i:
                    for g in range(2):
                        v.wait_ge(wused[4 * g + 3], i + r + 1)
                        for t in range(NT):
                            xc = x[:, t, ds(i * 1024 + g * 512, 512)]
                            v.tensor_tensor(xc, dense_bank[2 * g + t][:, :], xc, ALU.add).then_inc(pair_evac[g], 1)

            add_to_x(R_WO)
            for g in range(2):
                v.wait_ge(pair_evac[g], 2 * B_PQ)
            v.sem_inc(x_ready, 8)

            def choose(unit, b, base):
                w1, w2 = sub(rW1), sub(rW2)
                val, cand = sub(rV), sub(rCA)
                iu = usub(rIU)
                st.link(v.tensor_copy(w1, kscore[:, ds((unit - base) * 256, 256)]))
                for s in range(2):
                    src, alt = w1[:, s * P:(s + 1) * P], w2[:, s * P:(s + 1) * P]
                    c = 16 * s
                    st.link(v.max(val[:, c:c + 8], src))
                    st.add(v.max_index(iu[:, c:c + 8], val[:, c:c + 8], src))
                    st.link(v.match_replace(alt, val[:, c:c + 8], src, -HUGE))
                    st.link(v.max(val[:, c + 8:c + 16], alt))
                    st.add(v.max_index(iu[:, c + 8:c + 16], val[:, c + 8:c + 16], alt))
                c3 = cand.rearrange("p (a b) -> p a b", a=TOPK)
                st.wait()
                st.link(v.tensor_tensor(c3, val[:, 0:16].unsqueeze(2).broadcast_to([P, 16, 16]),
                                        val[:, 16:32].unsqueeze(1).broadcast_to([P, 16, 16]), ALU.add))
                top = sub(rTP)[:, b * TOPK:(b + 1) * TOPK]
                pos = usub(rPU)
                st.link(v.max(top[:, 0:8], cand))
                st.add(v.max_index(pos[:, 0:8], top[:, 0:8], cand))
                st.link(v.match_replace(sub(rCB), top[:, 0:8], cand, -HUGE))
                st.link(v.max(top[:, 8:16], sub(rCB)))
                v.tensor_scalar(sub(rSS)[:, b:b + 1], top[:, 0:1], -1.0, None, ALU.mult).then_inc(topk_v, 1)
                st.link(v.max_index(pos[:, 8:16], top[:, 8:16], sub(rCB)))
                p2 = usub(rP2)
                st.add(v.tensor_scalar(p2[:, 0:16], pos, 4, None, ALU.logical_shift_right))
                st.add(v.tensor_scalar(p2[:, 16:32], pos, 15, None, ALU.bitwise_and))
                st.link(v.tensor_copy(sub(rIF), iu))
                st.link(v.tensor_copy(sub(rPF), p2))
                for s in range(2):
                    hot = sub((rO1, rO2)[s]).rearrange("p (a b) -> p a b", a=TOPK)
                    st.link(v.tensor_tensor(
                        hot, sub(rPF)[:, 16 * s:16 * s + 16].unsqueeze(2).broadcast_to([P, 16, 16]),
                        iota16.unsqueeze(1).broadcast_to([P, 16, 16]), ALU.is_equal))
                    st.link(v.tensor_tensor(
                        hot, hot, sub(rIF)[:, 16 * s:16 * s + 16].unsqueeze(1).broadcast_to([P, 16, 16]), ALU.mult))
                    st.link(v.tensor_reduce(sub(rIS)[:, 16 * s:16 * s + 16], hot, AX, ALU.add))
                v.scalar_tensor_tensor(usub(rST)[:, b * TOPK:(b + 1) * TOPK], sub(rIS)[:, 0:16], float(NKEY),
                                       sub(rIS)[:, 16:32], ALU.mult, ALU.add).then_inc(stage_ready, 1)
                v.wait_ge(topk_e, unit + 1)
                st.link(v.reciprocal(sub(rSS)[:, 4 + b:5 + b], sub(rSS)[:, 2 + b:3 + b]))
                gt = sub(rGT)[:, b * TOPK:(b + 1) * TOPK]
                st.link(v.tensor_scalar(gt, gt, sub(rSS)[:, 4 + b:5 + b], None, ALU.mult))

            def unit_down(unit, b, t):
                for kk in range(TOPK):
                    slot = kk % SLOTS
                    v.wait_ge(gfull[slot], (unit * GROUNDS + kk // SLOTS) * 16 + 16)
                    v.tensor_tensor_reduce(gslot[:, slot, :], gslot[:, slot, :], h[:, t, :], 1.0, 0.0, ALU.mult,
                                           ALU.add, sub(rAC)[:, b * TOPK + kk:b * TOPK + kk + 1]
                                           ).then_inc(gused[slot], 1)

            def unit_up(unit, b, t):
                v.wait_ge(gelu_ready, unit + 1)
                wt = sub(rWT)[:, b * TOPK:(b + 1) * TOPK]
                st.link(v.tensor_tensor(wt, sub(rGT)[:, b * TOPK:(b + 1) * TOPK],
                                        sub(rGE)[:, b * TOPK:(b + 1) * TOPK], ALU.mult))
                for kk in range(TOPK):
                    slot = kk % SLOTS
                    rnd = unit * GROUNDS + 2 + kk // SLOTS
                    v.wait_ge(gfull[slot], rnd * 16 + 16)
                    if kk:
                        prev = (kk - 1) % SLOTS
                        v.wait_ge(gused[prev], unit * GROUNDS + 2 + (kk - 1) // SLOTS + 2)
                    v.scalar_tensor_tensor(x[:, t, :], gslot[:, slot, :], wt[:, kk:kk + 1], x[:, t, :], ALU.mult,
                                           ALU.add).then_inc(gused[slot], 1)
                v.wait_ge(gused[SLOTS - 1], unit * GROUNDS + 5)
                v.sem_inc(turn_over, 1)

            def peer_units(layer):
                base = layer * UNITS
                v.wait_ge(sk_evac, 8 * layer + 1)
                choose(base, 0, base)
                v.wait_ge(sk_evac, 8 * (layer + 1))
                st.clear()
                for t in range(NT):
                    pairs = PH // 2 - (t == NT - 1)
                    first = base + t * PH
                    with v.Fori(0, pairs) as i:
                        for b in range(2):
                            unit = i * 2 + (first + b)
                            unit_down(unit, b, t)
                            choose(unit + 1, 1 - b, base)
                            unit_up(unit, b, t)
                        st.clear()
                last = base + UNITS - 2
                unit_down(last, 0, NT - 1)
                choose(last + 1, 1, base)
                unit_up(last, 0, NT - 1)
                unit_down(last + 1, 1, NT - 1)
                unit_up(last + 1, 1, NT - 1)

            norm(1)
            peer_units(0)
            v.sem_inc(x_ready, 8)

            norm(2)
            v.wait_ge(rope_loaded, 16 * 5)
            v.wait_ge(inv_ready, 1)
            st.link(v.tensor_copy(pos_f, pos_i))
            a0, a1, n0 = ang[:, 0], ang[:, 1], rnd[:, 0]
            for t in range(NT):
                st.add(v.tensor_scalar(a0[:, t, :], inv_freq, pos_f[:, t:t + 1], None, ALU.mult))
            st.wait()
            st.link(v.tensor_scalar(n0, a0, float(1 / (2 * np.pi)), None, ALU.mult))
            st.link(v.tensor_scalar(n0, n0, ROUND, -ROUND, ALU.add, ALU.add))
            for part in (PI_A, PI_B, PI_C):
                st.link(v.scalar_tensor_tensor(a0, n0, -part, a0, ALU.mult, ALU.add))
            st.link(v.tensor_scalar(a0, a0, float(1 / (2 * np.pi)), None, ALU.mult))
            st.link(v.tensor_scalar(a1, a0, 0.25, None, ALU.add))
            st.link(v.tensor_scalar(rnd, ang, ROUND, -ROUND, ALU.add, ALU.add))
            v.tensor_tensor(ang, ang, rnd, ALU.subtract).then_inc(ang_ready, 1)
            v.wait_ge(par_t, 1)
            v.tensor_copy(par[:, 0:80], mb[0][:, 0:80]).then_inc(par_ready, 1)
            v.wait_ge(lam_act, 2)
            e_, z_ = lp[:, 8:16], lp[:, 16:24]
            st.link(v.tensor_scalar(z_, e_, 2.0, None, ALU.add))
            st.link(v.reciprocal(z_, z_))
            st.link(v.tensor_tensor(z_, z_, e_, ALU.mult))
            st.link(v.tensor_tensor(lp[:, 0:8], z_, z_, ALU.mult))
            st.link(v.tensor_scalar(neg_c, lp[:, 0:8], 1 / 17, 1 / 15, ALU.mult, ALU.add))
            for odd in (13, 11, 9, 7, 5, 3, 1):
                st.link(v.tensor_tensor(neg_c, neg_c, lp[:, 0:8], ALU.mult))
                st.link(v.tensor_scalar(neg_c, neg_c, 1 / odd, None, ALU.add))
            st.link(v.scalar_tensor_tensor(neg_c, neg_c, 2.0, z_, ALU.mult, ALU.mult))
            st.link(v.tensor_scalar(e_, lam, -1.0, 0.0, ALU.mult, ALU.max))
            st.link(v.tensor_tensor(neg_c, neg_c, e_, ALU.add))
            v.tensor_scalar(neg_c, neg_c, -LRU_C, None, ALU.mult).then_inc(lam_dve, 1)
            for g in range(2):
                v.wait_ge(pair_evac[g], 2 * B_IN2 + 2)
            junk = big[:, 12928:13440]
            for t in range(NT):
                for g, (lo, hi) in enumerate(((0, Q_LORA), (Q_LORA, Q_LORA + KV_LORA))):
                    n = hi - lo
                    st.link(v.tensor_tensor_reduce(junk[:, 0:n], c2[:, t, lo:hi], c2[:, t, lo:hi], 1.0, 0.0,
                                                   ALU.mult, ALU.add, stat[:, 12 + 2 * t + g:13 + 2 * t + g]))
                    ins = v.tensor_scalar(stat[:, 16 + 2 * t + g:17 + 2 * t + g],
                                          stat[:, 12 + 2 * t + g:13 + 2 * t + g], 1.0 / n, EPS, ALU.mult, ALU.add)
                    if t == 1 and g == 1:
                        ins.then_inc(c_msq, 1)
                    else:
                        st.link(ins)
            v.wait_ge(c_rms, 1)
            st.link(v.reciprocal(stat[:, 12:16], stat[:, 20:24]))
            for t in range(NT):
                for g, (lo, hi) in enumerate(((0, Q_LORA), (Q_LORA, Q_LORA + KV_LORA))):
                    st.add(v.scalar_tensor_tensor(c2[:, t, lo:hi], c2[:, t, lo:hi],
                                                  stat[:, 12 + 2 * t + g:13 + 2 * t + g], (g_cq, g_ckv)[g],
                                                  ALU.mult, ALU.mult))
            st.wait()
            v.sem_inc(c_ready, 1)
            for g in range(2):
                v.wait_ge(pair_evac[g], 2 * B_IN2 + 4)
            for k in range(8):
                st.add(v.tensor_scalar(xcT[:, k, :], xrT[:, k, :], conv_w[:, 24 + k:25 + k], conv_b[:, k:k + 1],
                                       ALU.mult, ALU.add))
            for j in (2, 1, 0):
                back = CONV - 1 - j
                for k in range(8):
                    st.wait(st.n - 7)
                    st.add(v.scalar_tensor_tensor(xcT[:, k, back:T], xrT[:, k, 0:T - back],
                                                  conv_w[:, 8 * j + k:8 * j + k + 1], xcT[:, k, back:T],
                                                  ALU.mult, ALU.add))
            st.wait()
            v.sem_inc(xc_ready, 1)
            v.wait_ge(lru_act, 16)
            st.link(v.tensor_tensor(sq_g, rr_g, rr_g, ALU.mult))
            v.scalar_tensor_tensor(th_g, sq_g, 1.0, th_g, ALU.add, ALU.mult).then_inc(lru_dve, 1)
            st.link(v.tensor_tensor(ii_g, ii_g, hs[:, 2048:4096], ALU.mult))
            v.wait_ge(lru_act, 17)
            st.link(v.tensor_tensor(ii_g, ii_g, th_g, ALU.mult))
            for k in range(8):
                st.add(v.tensor_tensor_scan(k3(th_g)[:, k, :], k3(rr_g)[:, k, :], k3(ii_g)[:, k, :], 0.0,
                                            ALU.mult, ALU.add))
            st.wait()
            v.wait_ge(lru_act, 18)
            v.wait_ge(wused[7], R_IN2 + 3)
            st.link(v.tensor_tensor(recT, th_g, big[:, 3712:5760], ALU.mult))

            def gain_branch(xT, sq, n):
                v.tensor_tensor(sq, xT, xT, ALU.mult).then_inc(sq_ready, 1)
                v.wait_ge(sq_ready, n + 1)
                v.tensor_tensor(k3(xT), k3(xT), g_mix[:, 8 - 8 * n:16 - 8 * n].unsqueeze(2).broadcast_to([P, 8, T]),
                                ALU.mult).then_inc(mixed_ready, 1)

            def branch_mean(n):
                v.wait_ge(sums_done, 2 * n + 1)
                v.tensor_scalar(stat[:, 24 + 2 * n:26 + 2 * n], mb[0][:, 0:2], 1.0 / REC, EPS, ALU.mult,
                                ALU.add).then_inc(sums_done, 1)

            def branch_rs(n):
                v.wait_ge(branch_rms, n + 1)
                st.link(v.reciprocal(stat[:, 24 + 2 * n:26 + 2 * n], stat[:, 28 + 2 * n:30 + 2 * n]))

            def branch_to_x(n, c):
                v.wait_ge(wused[2 * c + 1], R_WO2 + n + 1)
                for t in range(NT):
                    xc = x[:, t, c * 512:(c + 1) * 512]
                    v.scalar_tensor_tensor(xc, dense_bank[2 * (c % 2) + t][:, :],
                                           stat[:, 24 + 2 * n + t:25 + 2 * n + t], xc, ALU.mult,
                                           ALU.add).then_inc(pair_evac[c % 2], 1)

            gain_branch(recT, rec_sq, 0)

            v.wait_ge(pair_evac[0], 2 * B_WO2)
            v.wait_ge(pair_evac[1], 2 * B_WO2)
            branch_mean(0)
            q2f = big[:, 5760:8832]
            rope_k = c2[:, :, Q_LORA + KV_LORA:W_C]
            st.add(v.tensor_tensor(krr, rope_k, rope_k, ALU.mult))
            st.link(v.tensor_tensor(krg, rope_k, g_kh[:, NOPE:QKD].unsqueeze(1).broadcast_to([P, NT, ROPE]), ALU.mult))
            st.link(v.tensor_tensor(qk2_sq, q2f, q2f, ALU.mult))
            st.link(v.tensor_reduce(msq2[:, 0:16], qk2_sq.rearrange("p (r c) -> p r c", c=QKD), AX, ALU.add))
            kn_raw = kv2[:, :, :, 0:NOPE]
            sq4 = qk2_sq[:, 0:2048].rearrange("p (t h c) -> p t h c", t=NT, h=NH2)
            st.link(v.tensor_tensor(sq4, kn_raw, kn_raw, ALU.mult))
            st.add(v.tensor_reduce(msq2[:, 16:32], qk2_sq[:, 0:2048].rearrange("p (r c) -> p r c", c=NOPE), AX,
                                   ALU.add))
            st.link(v.tensor_reduce(msq2[:, 32:34], krr, AX, ALU.add))
            mk = msq2[:, 16:32].rearrange("p (t h) -> p t h", t=NT)
            st.link(v.tensor_tensor(mk, mk, msq2[:, 32:34].unsqueeze(2).broadcast_to([P, NT, NH2]), ALU.add))
            v.tensor_scalar(msq2[:, 0:32], msq2[:, 0:32], 1.0 / QKD, EPS, ALU.mult, ALU.add).then_inc(qk2_msq, 1)
            v.wait_ge(qk2_rms, 1)
            st.add(v.tensor_scalar(g_qh, g_qh, float(QKD ** -0.5), None, ALU.mult))
            st.link(v.reciprocal(rs2, rms2))
            q_rows = q2.rearrange("p t h c -> p (t h) c")
            st.link(v.tensor_tensor(q_rows, q_rows, rs2[:, 0:16].unsqueeze(2).broadcast_to([P, 16, QKD]), ALU.mult))
            kn_rows = kn2.rearrange("p t h c -> p (t h) c")
            kn_src = kn_raw.rearrange("p t h c -> p (t h) c")
            st.link(v.tensor_tensor(kn_rows, kn_src, rs2[:, 16:32].unsqueeze(2).broadcast_to([P, 16, NOPE]), ALU.mult))
            st.add(v.tensor_tensor(q_rows, q_rows, g_qh.unsqueeze(1).broadcast_to([P, 16, QKD]), ALU.mult))
            st.link(v.tensor_tensor(kn_rows, kn_rows, g_kh[:, 0:NOPE].unsqueeze(1).broadcast_to([P, 16, NOPE]),
                                    ALU.mult))
            branch_rs(0)
            branch_to_x(0, 0)
            v.wait_ge(trig_ready, 1)
            half = ROPE // 2
            sin4, cos4 = (trig[:, i].unsqueeze(2).broadcast_to([P, NT, NH2, half]) for i in range(2))
            t1, t2 = q2[:, :, :, NOPE:NOPE + half], q2[:, :, :, NOPE + half:QKD]
            for (p, q_, op, lo) in ((t1, t2, ALU.subtract, 0), (t2, t1, ALU.add, half)):
                st.add(v.tensor_tensor(rope_t[:, 0], p, cos4, ALU.mult))
                st.link(v.tensor_tensor(rope_t[:, 1], q_, sin4, ALU.mult))
                st.link(v.tensor_tensor(qr2[:, :, :, lo:lo + half], rope_t[:, 0], rope_t[:, 1], op))
            k1, k2 = krg[:, :, 0:half], krg[:, :, half:ROPE]
            u0, u1 = (big[:, 4736 + 64 * i:4736 + 64 * (i + 1)].rearrange("p (t c) -> p t c", t=NT) for i in range(2))
            for (p, q_, op, lo) in ((k1, k2, ALU.subtract, 0), (k2, k1, ALU.add, half)):
                st.add(v.tensor_tensor(u0, p, trig[:, 1], ALU.mult))
                st.link(v.tensor_tensor(u1, q_, trig[:, 0], ALU.mult))
                st.link(v.tensor_tensor(krr[:, :, lo:lo + half], u0, u1, op))
            v.tensor_tensor(krh, krr.unsqueeze(2).broadcast_to([P, NT, NH2, ROPE]),
                            rs2[:, 16:32].rearrange("p (t h) -> p t h", t=NT).unsqueeze(3)
                            .broadcast_to([P, NT, NH2, ROPE]), ALU.mult).then_inc(qk2_ready, 1)
            branch_to_x(0, 1)
            branch_to_x(0, 2)
            v.wait_ge(causal_ready, 1)
            v.sem_inc(nm2_ready, 2)
            v.sem_inc(o2_evac, 2)
            st.clear()
            with v.Fori(0, NH2 // 2) as i2:
                for e in range(2):
                    j = i2 * 2 + e
                    v.wait_ge(s2_done, j + 1)
                    st.link(v.tensor_tensor(prob2[e], mb[e][:, 0:W_S], causal, ALU.add))
                    for t, (lo, hi) in enumerate(tile_keys):
                        ins = v.tensor_reduce(att[e][0][:, t:t + 1], prob2[e][:, lo:hi], AX, ALU.max, negate=True)
                    ins.then_inc(nm2_ready, 1)
                for e in range(2):
                    j = i2 * 2 + e
                    v.wait_ge(p2_exp, j * 2 + 2)
                    st.link(v.reciprocal(att[e][2], att[e][1]))
                    for t, (lo, hi) in enumerate(tile_keys):
                        ins = v.tensor_scalar(prob2[e][:, lo:hi], prob2[e][:, lo:hi], att[e][2][:, t:t + 1], None,
                                              ALU.mult)
                    ins.then_inc(p2_ready, 1)
                for e in range(2):
                    j = i2 * 2 + e
                    v.wait_ge(o2_done, j + 3)
                    v.tensor_copy(hT[:, ds(j, 1), :].rearrange("p a n -> p (a n)"),
                                  dense_bank[e][:, 0:T]).then_inc(o2_evac, 1)
                st.clear()
            v.wait_ge(o2_evac, NH2 + 2)
            gain_branch(attT, att_sq, 1)
            branch_to_x(0, 3)
            branch_mean(1)
            branch_rs(1)
            v.wait_ge(pair_evac[0], 2 * B_WO2 + 4)
            v.wait_ge(pair_evac[1], 2 * B_WO2 + 4)
            for c in range(4):
                branch_to_x(1, c)
            for g in range(2):
                v.wait_ge(pair_evac[g], 2 * B_PQ2)
            v.sem_inc(x_ready, 8)
            norm(3)
            peer_units(1)


def kernel(**inputs):
    import concourse.bacc as _bacc
    from concourse.bass_utils import run_bass_kernel_spmd

    nc = _bacc.Bacc("TRN2", target_bir_lowering=False, num_devices=1)
    arrays = {"in_" + name: np.asarray(value) for name, value in inputs.items()}
    ins = {name: nc.dram_tensor("in_" + name, arrays["in_" + name].shape,
                                mybir.dt.from_np(arrays["in_" + name].dtype), kind="ExternalInput").ap()
           for name in inputs}
    y = nc.dram_tensor("out0", (1, T, D), F32, kind="ExternalOutput").ap()
    two_blocks(nc, ins, y)
    nc.compile()
    got = run_bass_kernel_spmd(nc, [arrays], core_ids=[0]).results
    return np.asarray(got[0]["out0"])
```
